# Optimizing a Trainium2 kernel written in Bass

```python
import jax, jax.numpy as jnp
from jax import lax
import numpy as np

D_MODEL = 1024
BATCH = 1
SEQ = 256
DEPTH = 2
DEC_BATCH = 8
DEC_SEQ = 1
PAST_LEN = 256
PAGE_SIZE = 128

N_A_LAYERS = DEPTH // 2
N_B_LAYERS = DEPTH - N_A_LAYERS
N_DENSE = (DEPTH + 1) // 2
N_MOE = DEPTH // 2
GLA_HEADS = 4
GLA_KEY_DIM = D_MODEL // 2
GLA_VAL_DIM = D_MODEL
GLA_DK = GLA_KEY_DIM // GLA_HEADS
GLA_DV = GLA_VAL_DIM // GLA_HEADS
GLA_GATE_RANK = 16
GLA_GATE_NORM = 16.0
GLA_CHUNK = 64
GLA_IN_DIM = 2 * GLA_KEY_DIM + 2 * GLA_VAL_DIM + GLA_GATE_RANK
SB_HEADS = 16
SB_HEAD_DIM = D_MODEL // SB_HEADS
SB_QBLOCK = 128
SB_BIAS_INIT = -7.0
D_FF = 2816
N_EXPERTS = 8
TOP_K = 2
D_FF_EXPERT = 3584
EPS = 1e-6

kernel_name = "yoco_gla_stickbreaking_adaln_decoder_step"

def rmsnorm(x, g):
    xf = x.astype(jnp.float32)
    y = xf * lax.rsqrt(jnp.mean(xf * xf, axis=-1, keepdims=True) + EPS)
    return (y * g.astype(jnp.float32)).astype(x.dtype)

def modulate(h, shift, scale):
    return h * (1 + scale[:, None, :]) + shift[:, None, :]

def gla_scan(q, k, v, log_a, s0):
    B, L = q.shape[:2]
    C = min(GLA_CHUNK, L)
    n = -(-L // C)
    pad = n * C - L

    def prep(t):
        t = jnp.pad(t.astype(jnp.float32), ((0, 0), (0, pad), (0, 0), (0, 0)))
        return t.reshape(B, n, C, t.shape[2], t.shape[3]).swapaxes(0, 1)

    qc, kc, vc, ac = prep(q), prep(k), prep(v), prep(log_a)
    causal = jnp.tril(jnp.ones((C, C), dtype=bool))[None, :, :, None, None]

    def step(S, inp):
        qi, ki, vi, ai = inp
        b = jnp.cumsum(ai, axis=1)
        o_inter = jnp.einsum('bthk,bhkv->bthv', qi * jnp.exp(b), S)
        diff = b[:, :, None] - b[:, None, :]
        decay = jnp.exp(jnp.where(causal, diff, -jnp.inf))
        scores = jnp.einsum('bthk,bshk,btshk->bhts', qi, ki, decay)
        o_intra = jnp.einsum('bhts,bshv->bthv', scores, vi)
        b_last = b[:, -1]
        S = jnp.exp(b_last)[..., None] * S + jnp.einsum('bshk,bshv->bhkv', ki * jnp.exp(b_last[:, None] - b), vi)
        return S, o_inter + o_intra

    S, o = lax.scan(step, s0.astype(jnp.float32), (qc, kc, vc, ac))
    o = o.swapaxes(0, 1).reshape(B, n * C, o.shape[3], o.shape[4])[:, :L]
    return o, S

def gla_mixer(h, s0, w_in, w_gate2, b_gate, g_norm, w_out):
    B, L, _ = h.shape
    proj = h @ w_in
    q, k, v, g, r = jnp.split(proj, [GLA_KEY_DIM, 2 * GLA_KEY_DIM, 2 * GLA_KEY_DIM + GLA_VAL_DIM,
                                     2 * GLA_KEY_DIM + 2 * GLA_VAL_DIM], axis=-1)
    log_a = jax.nn.log_sigmoid((r @ w_gate2 + b_gate).astype(jnp.float32)) / GLA_GATE_NORM
    q = q.reshape(B, L, GLA_HEADS, GLA_DK) * (GLA_DK ** -0.5)
    k = k.reshape(B, L, GLA_HEADS, GLA_DK)
    v = v.reshape(B, L, GLA_HEADS, GLA_DV)
    o, S = gla_scan(q, k, v, log_a.reshape(B, L, GLA_HEADS, GLA_DK), s0)
    o = rmsnorm(o, g_norm).reshape(B, L, GLA_VAL_DIM).astype(h.dtype) * jax.nn.silu(g)
    return o @ w_out, S

def stick_breaking_attention(q, k, v, bias, q_offset):
    Lq = q.shape[1]
    bias_f = bias.astype(jnp.float32)[None, :, None, None]
    outs = []
    for start in range(0, Lq, SB_QBLOCK):
        stop = min(start + SB_QBLOCK, Lq)
        n_keys = q_offset + stop - 1
        qb = q[:, start:stop].astype(jnp.float32)
        kb = k[:, :n_keys].astype(jnp.float32)
        vb = v[:, :n_keys].astype(jnp.float32)
        z = jnp.einsum('bqhd,bkhd->bhqk', qb, kb) * (SB_HEAD_DIM ** -0.5) + bias_f
        t_pos = q_offset + jnp.arange(start, stop)
        s_pos = jnp.arange(n_keys)
        mask = s_pos[None, :] < t_pos[:, None]
        log1m = jnp.where(mask, jax.nn.log_sigmoid(-z), 0.0)
        later = lax.cumsum(log1m, axis=3, reverse=True) - log1m
        log_att = jnp.where(mask, log1m + z + later, -jnp.inf)
        outs.append(jnp.einsum('bhqk,bkhd->bqhd', jnp.exp(log_att), vb))
    return jnp.concatenate(outs, axis=1).astype(q.dtype)

def sb_mixer(h, k_all, v_all, q_offset, w_q, b_sb, w_out):
    B, L, _ = h.shape
    q = (h @ w_q).reshape(B, L, SB_HEADS, SB_HEAD_DIM)
    o = stick_breaking_attention(q, k_all, v_all, b_sb, q_offset)
    return o.reshape(B, L, D_MODEL) @ w_out

def shared_kv(x, c, kv_norm, kv_ada_w, kv_ada_b, kv_w):
    B, L, _ = x.shape
    shift, scale = jnp.split(jax.nn.silu(c) @ kv_ada_w + kv_ada_b, 2, axis=-1)
    h = modulate(rmsnorm(x, kv_norm), shift, scale)
    k, v = jnp.split(h @ kv_w, 2, axis=-1)
    return k.reshape(B, L, SB_HEADS, SB_HEAD_DIM), v.reshape(B, L, SB_HEADS, SB_HEAD_DIM)

def swiglu(h, w_gate_up, w_down):
    a, b = jnp.split(h @ w_gate_up, 2, axis=-1)
    return (jax.nn.silu(a) * b) @ w_down

def moe_swiglu(h, w_router, b_router, w_gate_up, w_down):
    logits = (h @ w_router).astype(jnp.float32) + b_router.astype(jnp.float32)
    top_val, top_idx = lax.top_k(logits, TOP_K)
    top_w = jax.nn.softmax(top_val, axis=-1)
    gates = jnp.sum(jax.nn.one_hot(top_idx, N_EXPERTS, dtype=jnp.float32) * top_w[..., None], axis=-2)
    gates = gates.astype(h.dtype)
    y = jnp.zeros_like(h)
    for e in range(N_EXPERTS):
        y = y + gates[..., e:e + 1] * swiglu(h, w_gate_up[e], w_down[e])
    return y

def trunk(x, c, gla_s0, past_k, past_v, p):
    q_offset = past_k.shape[1]
    new_states = []
    k_all = v_all = new_k = new_v = None
    for layer in range(DEPTH):
        sh1, sc1, g1, sh2, sc2, g2 = jnp.split(jax.nn.silu(c) @ p['ada_w'][layer] + p['ada_b'][layer], 6, axis=-1)
        h = modulate(rmsnorm(x, p['norm_mix'][layer]), sh1, sc1)
        if layer < N_A_LAYERS:
            out, S = gla_mixer(h, gla_s0[layer], p['gla_w_in'][layer], p['gla_w_gate2'][layer],
                               p['gla_b_gate'][layer], p['gla_norm'][layer], p['gla_w_out'][layer])
            new_states.append(S)
        else:
            bi = layer - N_A_LAYERS
            out = sb_mixer(h, k_all, v_all, q_offset, p['sb_w_q'][bi], p['sb_b'][bi], p['sb_w_out'][bi])
        x = x + g1[:, None, :] * out
        h = modulate(rmsnorm(x, p['norm_ffn'][layer]), sh2, sc2)
        if layer % 2 == 0:
            f = swiglu(h, p['ffn_w_gate_up'][layer // 2], p['ffn_w_down'][layer // 2])
        else:
            f = moe_swiglu(h, p['moe_w_router'][layer // 2], p['moe_b_router'][layer // 2],
                           p['moe_w_gate_up'][layer // 2], p['moe_w_down'][layer // 2])
        x = x + g2[:, None, :] * f
        if layer == N_A_LAYERS - 1:
            new_k, new_v = shared_kv(x, c, p['kv_norm'], p['kv_ada_w'], p['kv_ada_b'], p['kv_w'])
            k_all = jnp.concatenate([past_k.astype(new_k.dtype), new_k], axis=1)
            v_all = jnp.concatenate([past_v.astype(new_v.dtype), new_v], axis=1)
    shf, scf = jnp.split(jax.nn.silu(c) @ p['final_ada_w'] + p['final_ada_b'], 2, axis=-1)
    y = modulate(rmsnorm(x, p['final_norm']), shf, scf)
    return y, new_k, new_v, jnp.stack(new_states)

def setup_inputs(seed: int = 0) -> dict:
    key = jax.random.key(seed)
    ks = iter(jax.random.split(key, 40))

    def nrm(shape, scale):
        return jax.random.normal(next(ks), shape, jnp.float32) * scale

    def gain(shape):
        return 1.0 + nrm(shape, 0.02)

    n_pages = PAST_LEN // PAGE_SIZE
    n_pool = (DEC_BATCH * n_pages * 5) // 4
    d = D_MODEL
    out = {}
    out['x_prompt'] = nrm((BATCH, SEQ, d), 1.0)
    out['x_sample'] = nrm((DEC_BATCH, DEC_SEQ, d), 1.0)
    out['cache_k'] = nrm((n_pool, PAGE_SIZE, SB_HEADS, SB_HEAD_DIM), 1.0)
    out['cache_v'] = nrm((n_pool, PAGE_SIZE, SB_HEADS, SB_HEAD_DIM), 1.0)
    out['state_gla'] = nrm((N_A_LAYERS, DEC_BATCH, GLA_HEADS, GLA_DK, GLA_DV), 0.5)
    out['page_table'] = jax.random.permutation(next(ks), n_pool)[:DEC_BATCH * n_pages].reshape(
        DEC_BATCH, n_pages).astype(jnp.int32)
    out['c_prompt'] = nrm((BATCH, d), 1.0)
    out['c_sample'] = nrm((DEC_BATCH, d), 1.0)
    out['ada_w'] = nrm((DEPTH, d, 6 * d), 0.5 * d ** -0.5)
    out['ada_b'] = nrm((DEPTH, 6 * d), 0.02)
    out['norm_mix'] = gain((DEPTH, d))
    out['norm_ffn'] = gain((DEPTH, d))
    out['gla_w_in'] = nrm((N_A_LAYERS, d, GLA_IN_DIM), d ** -0.5)
    out['gla_w_gate2'] = nrm((N_A_LAYERS, GLA_GATE_RANK, GLA_KEY_DIM), GLA_GATE_RANK ** -0.5)
    out['gla_b_gate'] = nrm((N_A_LAYERS, GLA_KEY_DIM), 0.02)
    out['gla_norm'] = gain((N_A_LAYERS, GLA_DV))
    out['gla_w_out'] = nrm((N_A_LAYERS, GLA_VAL_DIM, d), GLA_VAL_DIM ** -0.5)
    out['kv_norm'] = gain((d,))
    out['kv_ada_w'] = nrm((d, 2 * d), 0.5 * d ** -0.5)
    out['kv_ada_b'] = nrm((2 * d,), 0.02)
    out['kv_w'] = nrm((d, 2 * d), d ** -0.5)
    out['sb_w_q'] = nrm((N_B_LAYERS, d, d), d ** -0.5)
    out['sb_b'] = SB_BIAS_INIT + nrm((N_B_LAYERS, SB_HEADS), 0.1)
    out['sb_w_out'] = nrm((N_B_LAYERS, d, d), d ** -0.5)
    out['ffn_w_gate_up'] = nrm((N_DENSE, d, 2 * D_FF), d ** -0.5)
    out['ffn_w_down'] = nrm((N_DENSE, D_FF, d), D_FF ** -0.5)
    out['moe_w_router'] = nrm((N_MOE, d, N_EXPERTS), d ** -0.5)
    out['moe_b_router'] = nrm((N_MOE, N_EXPERTS), 0.01)
    out['moe_w_gate_up'] = nrm((N_MOE, N_EXPERTS, d, 2 * D_FF_EXPERT), d ** -0.5)
    out['moe_w_down'] = nrm((N_MOE, N_EXPERTS, D_FF_EXPERT, d), D_FF_EXPERT ** -0.5)
    out['final_norm'] = gain((d,))
    out['final_ada_w'] = nrm((d, 2 * d), 0.5 * d ** -0.5)
    out['final_ada_b'] = nrm((2 * d,), 0.02)
    return out

def reference(x_prompt, x_sample, cache_k, cache_v, state_gla, page_table, c_prompt, c_sample,
              ada_w, ada_b, norm_mix, norm_ffn, gla_w_in, gla_w_gate2, gla_b_gate, gla_norm, gla_w_out,
              kv_norm, kv_ada_w, kv_ada_b, kv_w, sb_w_q, sb_b, sb_w_out, ffn_w_gate_up, ffn_w_down,
              moe_w_router, moe_b_router, moe_w_gate_up, moe_w_down, final_norm, final_ada_w, final_ada_b):
    p = dict(ada_w=ada_w, ada_b=ada_b, norm_mix=norm_mix, norm_ffn=norm_ffn, gla_w_in=gla_w_in,
             gla_w_gate2=gla_w_gate2, gla_b_gate=gla_b_gate, gla_norm=gla_norm, gla_w_out=gla_w_out,
             kv_norm=kv_norm, kv_ada_w=kv_ada_w, kv_ada_b=kv_ada_b, kv_w=kv_w, sb_w_q=sb_w_q, sb_b=sb_b,
             sb_w_out=sb_w_out, ffn_w_gate_up=ffn_w_gate_up, ffn_w_down=ffn_w_down,
             moe_w_router=moe_w_router, moe_b_router=moe_b_router, moe_w_gate_up=moe_w_gate_up,
             moe_w_down=moe_w_down, final_norm=final_norm, final_ada_w=final_ada_w, final_ada_b=final_ada_b)
    b_p = x_prompt.shape[0]
    gla0 = jnp.zeros((N_A_LAYERS, b_p, GLA_HEADS, GLA_DK, GLA_DV), jnp.float32)
    empty = jnp.zeros((b_p, 0, SB_HEADS, SB_HEAD_DIM), x_prompt.dtype)
    y_prompt, k_prompt, v_prompt, gla_prompt = trunk(x_prompt, c_prompt, gla0, empty, empty, p)
    b_s = x_sample.shape[0]
    past_k = cache_k[page_table].reshape(b_s, -1, SB_HEADS, SB_HEAD_DIM)
    past_v = cache_v[page_table].reshape(b_s, -1, SB_HEADS, SB_HEAD_DIM)
    y_sample, k_sample, v_sample, gla_sample = trunk(x_sample, c_sample, state_gla, past_k, past_v, p)
    return (y_prompt, y_sample, k_prompt, v_prompt, gla_prompt, k_sample, v_sample, gla_sample)


_drawn_inputs = setup_inputs


def setup_inputs(seed=0):
    import zlib

    import numpy as np

    out = dict(_drawn_inputs(seed))
    spreads = {}
    factors = {'cache_k': 6.302,
     'cache_v': 5.417,
     'gla_b_gate': 6.442,
     'gla_norm': 8.0,
     'kv_norm': 8.224,
     'sb_w_q': 4.09,
     'sb_b': 8.0,
     'moe_b_router': 23.035,
     'final_norm': 7.846,
     'norm_ffn': 4.913,
     'kv_ada_b': 2.898,
     'final_ada_b': 2.672}
    for name, (base, spread) in spreads.items():
        noise = np.random.default_rng([zlib.crc32(name.encode()), seed]).standard_normal(out[name].shape)
        drawn = base * np.exp(spread * noise) if base else spread * noise
        out[name] = __import__('jax').numpy.asarray(drawn.astype(out[name].dtype))
    for name, factor in factors.items():
        out[name] = (out[name] * factor).astype(out[name].dtype)
    return out
```

```python
from contextlib import ExitStack

import concourse.bass as bass
from concourse import mybir

ALU = mybir.AluOpType
ACT = mybir.ActivationFunctionType
AX = mybir.AxisListType
F32 = mybir.dt.float32
U32 = mybir.dt.uint32

P = 128
D = 1024
KC = D // P
TP = 256
NB = 8
T = TP + NB
TT = 3
TOK = [P, P, NB]
NC9 = 1 + NB
GH, DK, DV, C = 4, 128, 256, 64
NCH = TP // C
HALF = C // 2
GR = 16
SH, SD = 16, 64
PAGES = 2
FF, FE, NE = 2816, 3584, 8
FFC, FEC = FF // P, FE // P
EPS = 1e-6
EXP_CAP = 43.0
RING = 6
TILE = 4096
MIX0, FFN0, KV, MIX1, FFN1, FINAL = range(6)
SHIFT = {MIX0: 0, FFN0: 24, KV: 96, MIX1: 48, FFN1: 72, FINAL: 112}
SCALE = {MIX0: 8, FFN0: 32, KV: 104, MIX1: 56, FFN1: 80, FINAL: 120}
GAIN = {MIX0: 0, FFN0: 16, KV: 32, MIX1: 8, FFN1: 24, FINAL: 40}
GATE = {MIX0: 16, FFN0: 40, MIX1: 64, FFN1: 88}
GLA_GAIN, GLA_BIAS, VEC_B = 48, 50, 54
N_ADA = 32
STREAM = ([("ada", i) for i in range(N_ADA)] + [("gla_in", i) for i in range(6)] + [("gla_out", i) for i in range(2)]
          + [("ffn_up", i) for i in range(11)] + [("ffn_down", i) for i in range(6)] + [("kv", i) for i in range(4)]
          + [("sb_q", i) for i in range(2)] + [("k_cache", i) for i in range(4)] + [("v_cache", i) for i in range(4)]
          + [("sb_out", i) for i in range(2)])
TILE_AT = {k: n for n, k in enumerate(STREAM)}
BASE = len(STREAM)
PER_E = 21
PER_IT = 2 * PER_E
WORK = 13 * 1024 + 96
BLOCKS = ([("gla_in", i) for i in range(25)] + [("gla_out", i) for i in range(8)] + [("ffn_up", i) for i in range(44)]
          + [("ffn_down", i) for i in range(48)] + [("kv", i) for i in range(16)] + [("sb_q", i) for i in range(8)]
          + [("sb_out", i) for i in range(8)])
BLOCK_AT = {k: n for n, k in enumerate(BLOCKS)}
BY_ACT = ("gla_in", "kv", "sb_q")


def build(nc, A, O):
    y_prompt, y_sample, k_prompt, v_prompt, gla_prompt, k_sample, v_sample, gla_sample = O
    ctx = ExitStack()
    with ctx:
        def sb(name, shape, dt=F32):
            return ctx.enter_context(nc.sbuf_tensor(name, shape, dt))

        def sem(name):
            return ctx.enter_context(nc.semaphore(name))

        ring = [sb(f"ring{i}", [P, TILE]) for i in range(RING)]
        x = sb("x", [P, KC, T])
        h = sb("h", [P, KC, T])
        big = sb("big", [P, 28, T])
        work = sb("work", [P, WORK])
        mod = sb("mod", [P, P, NC9])
        gain = sb("gain", [P, 6, KC, NC9])
        vec_a = sb("vec_a", [P, P])
        vec_b = sb("vec_b", [P, VEC_B])
        cT = sb("cT", [P, KC, NC9])
        rstd = sb("rstd", [P, T])
        wr = sb("wr", [P, KC, GR])
        w_router = sb("w_router", [P, KC, NE])
        sb_bias = sb("sb_bias", [P, SH])
        router_bias = sb("router_bias", [P, NE])
        ident = sb("ident", [P, P])
        ones = sb("ones", [P, P])
        after = sb("after", [P, P])
        before = sb("before", [P, P])
        not_before = sb("not_before", [P, P])
        upto = sb("upto", [C, C])
        sel_to = sb("sel_to", [SH, NB, NB])
        iota8 = sb("iota8", [P, NE])
        tmp8 = sb("tmp8", [P, KC, NB])
        psum = ctx.enter_context(nc.psum_tensor("psum", [P, 8 * 512], F32))
        pb = [psum[:, i * 512:(i + 1) * 512] for i in range(8)]

        def piece(at, shape):
            n = 1
            for s in shape[1:]:
                n *= s
            v = work[0:shape[0], at:at + n]
            if len(shape) == 3:
                v = v.rearrange("p (a b) -> p a b", a=shape[1])
            if len(shape) == 4:
                v = v.rearrange("p (a b c) -> p a b c", a=shape[1], b=shape[2])
            return v, at + n

        crow, at = piece(0, [NC9, D])
        csilu, at = piece(at, [NC9, D])
        ada_row, at = piece(at, [NC9, 2, 512])
        at = 0
        la, at = piece(at, [P, GH, T])
        orstd = la
        silu_a = la[:, 0:2, :]
        t_abs, at = piece(at, [P, GH, T])
        cum_a, _ = piece(GH * T, [P, 32, HALF])
        ke, _ = piece(GH * T, [P, GH, TP])
        cum, at = piece(at, [P, 32, HALF])
        s0 = [piece(at, [P, GH, DV])[0], piece(at + 1024, [P, GH, DV])[0]]
        qd, at = piece(at, [P, 32, HALF])
        kd, at = piece(at, [P, 32, HALF])
        qo, at = piece(at, [P, 16, HALF])
        ko, at = piece(at, [P, 16, HALF])
        qe, at = piece(at, [P, GH, TP])
        dec, at = piece(at, [P, 16])
        w_gate2, _ = piece(at, [GR, GH * DK])
        vs_tok, _ = piece(at, [NB, D])
        st, at = piece(at, [C, 16, C])
        rT, _ = piece(at, [GR, T])
        vtok = []
        for i in range(2):
            v, at = piece(at, [C, D])
            vtok.append(v)
        ktok, at = piece(at, [C, 2 * GH * DK])
        state = []
        for i in range(2):
            v, at = piece(at, [P, GH, DV])
            state.append(v)
        assert at <= WORK, at
        ea = sb("ea", [P, GH, NB])
        at = 0
        kvtok, at = piece(at, [P, TT, 2 * D])
        z_buf, at = piece(at, [P, 2, 768])
        l_buf, at = piece(at, [P, 2, 768])
        zs, at = piece(at, [P, PAGES, NB * SH])
        ls, at = piece(at, [P, PAGES, NB * SH])
        prod, _ = piece(at, [P, D])
        os_row, at = piece(at, [SH, D])
        qs_tok, at = piece(at, [NB, D])
        os_tok = qs_tok
        assert at <= WORK, at
        at = 0
        gate_bc, at = piece(at, [P, NE, T])
        logit, at = piece(at, [P, TT, NE])
        top, at = piece(at, [P, TT, 8])
        gate_tok, at = piece(at, [P, TT, NE])
        hit, at = piece(at, [P, TT, NE])
        top_f, at = piece(at, [P, TT, 8])
        e2, at = piece(at, [P, 8])
        w1, at = piece(at, [P, 8])
        w2, at = piece(at, [P, 8])
        gateT, at = piece(at, [NE, T])
        silu_m, at = piece(at, [P, 2, T])
        gated, at = piece(at, [P, 2, T])
        assert at <= WORK, at
        top_i = sb("top_i", [P, TT, 8], U32)
        xtok = big[:, :, :].rearrange("p a b -> p (a b)")[:, 0:TT * D].rearrange("p (t d) -> p t d", t=TT)

        def sel(b):
            return ident[0:NB, b:b + 1].to_broadcast([NB, P])

        S = {}

        def named(*names):
            for n in names:
                S[n] = sem(n)

        named("consts", "small_loaded", "x_loaded", "weight_used", "vec_turned", "vec_kept", "c_silu", "c_turned",
              "c_kept", "x_turned", "x_kept", "ada_row_done", "ada_copied", "ada_turned", "ada_kept", "gains_ready",
              "squared", "ss_done", "ms_ready", "root_ready", "scaled", "h_ready", "hs_ready",
              "block_done", "kept_act", "kept_dve", "silu_done", "act_step", "dve_step",
              "gate_done", "gate_z", "log_sig", "cum_ready", "args_ready", "exps_ready", "decayed", "scores_done",
              "scores_kept", "v_turned", "v_kept", "o_done", "o_kept", "u_done", "state_ready", "vs_turned", "vs_kept",
              "vbc_done", "s_updated", "s0_loaded0", "s0_loaded1", "s0_stored0", "s0_stored1", "os_done", "os_kept",
              "osq_ready", "oss_done", "oms_ready", "oroot_ready", "o_ready", "state_stored",
              "kv_turned", "kv_kept", "kv_stored", "qs_turned", "qs_kept", "qbc_done", "kcache_used", "z_s_ready",
              "z_done", "z_ready", "soft_ready", "l_ready", "rc_done", "arg_ready", "p_exp", "p_ready", "pv_done",
              "pv_kept", "rcs_done", "args_s", "exps_s", "opv_done", "own_ready", "ot_done", "ot_kept", "otT_done",
              "otT_kept", "logits_done", "logits_ready", "gates_exp", "gates_exp_done", "down_part", "gates_ready", "gateT_done", "gateT_kept",
              "gbc_done", "gbc_kept", "pair_done", "pair_silu", "pair_kept", "down_done", "down_kept", "y_turned",
              "y_kept", "y_stored", "gate_half_done", "gated_ready", "part_added", "masked")
        loaded = [sem(f"ring_loaded{i}") for i in range(RING)]

        lands, count = [], [0] * RING
        for n, (kind, i) in enumerate(STREAM):
            count[n % RING] += 64 if kind in ("k_cache", "v_cache") else 32 if kind == "ffn_up" else 16
            lands.append(count[n % RING])
        LAND0 = list(count)

        def read_out(kind, i):
            if kind == "ada":
                return S["ada_row_done"], i + 1
            if kind == "k_cache":
                return S["z_s_ready"], 2 * i + 2
            if kind == "v_cache":
                return S["opv_done"], 2 * i + 2
            per = 8 if kind == "ffn_down" else 4
            return S["block_done"], BLOCK_AT[kind, per * i + per - 1] + 1

        empt, a_n, d_n = [], 0, 0
        for kind, i in BLOCKS:
            if kind in BY_ACT:
                a_n += 1
                empt.append(("kept_act", a_n))
            elif kind == "ffn_up":
                d_n += i % 2
                empt.append(("kept_dve", d_n + 1 - i % 2))
            else:
                d_n += 1
                empt.append(("kept_dve", d_n))

        block = ctx.enter_context(nc.Block())

        def slot(kind, i):
            return ring[TILE_AT[kind, i] % RING]

        def landed(eng, kind, i):
            n = TILE_AT[kind, i]
            eng.wait_ge(loaded[n % RING], lands[n])

        def cols8(tile, n=512):
            return tile[:, 0:KC * n].rearrange("p (k c) -> p k c", k=KC)

        def rows(w, lo, n, c0=0, c1=D):
            return w[lo:lo + n * P, c0:c1].rearrange("(k p) c -> p k c", p=P)

        @block.sync
        def _(eng):
            for w, lo in ((A["ada_b"].rearrange("l (c p) -> (l c) p", p=P), 0),
                          (A["kv_ada_b"].rearrange("(c p) -> c p", p=P), 96),
                          (A["final_ada_b"].rearrange("(c p) -> c p", p=P), 112)):
                eng.dma_start(h[lo:lo + w.shape[0], 0, 0:P], w).then_inc(S["small_loaded"], 16)
            for w, lo in ((A["norm_mix"].rearrange("l (c p) -> (l c) p", p=P), 0),
                          (A["norm_ffn"].rearrange("l (c p) -> (l c) p", p=P), 16),
                          (A["kv_norm"].rearrange("(c p) -> c p", p=P), 32),
                          (A["final_norm"].rearrange("(c p) -> c p", p=P), 40),
                          (A["gla_norm"].rearrange("l (c p) -> (l c) p", p=P), GLA_GAIN),
                          (A["gla_b_gate"].rearrange("l (c p) -> (l c) p", p=P), GLA_BIAS)):
                eng.dma_start(h[lo:lo + w.shape[0], 1, 0:P], w).then_inc(S["small_loaded"], 16)
            eng.dma_start(crow[0:1, :], A["c_prompt"]).then_inc(S["small_loaded"], 16)
            eng.dma_start(crow[1:NC9, :], A["c_sample"]).then_inc(S["small_loaded"], 16)
            eng.dma_start(wr[:], rows(A["gla_w_in"][0], 0, KC, 3072, 3088)).then_inc(S["small_loaded"], 16)
            eng.dma_start(w_router[:], rows(A["moe_w_router"][0], 0, KC, 0, NE)).then_inc(S["small_loaded"], 16)
            eng.dma_start(w_gate2, A["gla_w_gate2"][0]).then_inc(S["small_loaded"], 16)
            eng.dma_start(sb_bias[:], A["sb_b"][0].partition_broadcast(P)).then_inc(S["small_loaded"], 16)
            eng.dma_start(router_bias[:], A["moe_b_router"][0].partition_broadcast(P)).then_inc(S["small_loaded"], 16)
            for t in range(2):
                eng.dma_start(xtok[:, t, :], A["x_prompt"][0, t * P:(t + 1) * P, :]).then_inc(S["x_loaded"], 16)
            eng.dma_start(xtok[0:NB, 2, :], A["x_sample"].rearrange("b s d -> (b s) d")).then_inc(S["x_loaded"], 16)

            for n, (kind, i) in enumerate(STREAM):
                dst = ring[n % RING]
                if n >= RING:
                    eng.wait_ge(*read_out(*STREAM[n - RING]))
                if kind in ("k_cache", "v_cache"):
                    cache = A["cache_k" if kind == "k_cache" else "cache_v"].rearrange("n s h d -> n s (h d)")
                    for j in range(4):
                        b, page = 2 * i + j // 2, j % 2
                        at_page = eng.value_load(A["page_table"][b:b + 1, page:page + 1], min_val=0,
                                                 max_val=A["cache_k"].shape[0] - 1)
                        eng.dma_start(dst[:, j * D:(j + 1) * D], cache[at_page]).then_inc(loaded[n % RING], 16)
                    continue
                c = i * 512
                if kind == "ada":
                    w, c = ((A["ada_w"][i // 12], (i % 12) * 512) if i < 24 else
                            (A["kv_ada_w"], (i - 24) * 512) if i < 28 else (A["final_ada_w"], (i - 28) * 512))
                    eng.dma_start(cols8(dst), rows(w, 0, KC, c, c + 512)).then_inc(loaded[n % RING], 16)
                elif kind == "ffn_up":
                    w = A["ffn_w_gate_up"][0].rearrange("(k p) (s c) -> p k s c", p=P, s=2)[:, :, :, i * 256:(i + 1) * 256]
                    d4 = dst[:].rearrange("p (k s c) -> p k s c", k=KC, s=2)
                    for s in range(2):
                        eng.dma_start(d4[:, :, s, :], w[:, :, s, :]).then_inc(loaded[n % RING], 16)
                elif kind == "ffn_down":
                    k = min(4, FFC - 4 * i)
                    eng.dma_start(dst[:, 0:k * D].rearrange("p (k c) -> p k c", k=k),
                                  rows(A["ffn_w_down"][0], i * 512, k)).then_inc(loaded[n % RING], 16)
                else:
                    w = {"gla_in": A["gla_w_in"][0], "gla_out": A["gla_w_out"][0], "kv": A["kv_w"],
                         "sb_q": A["sb_w_q"][0], "sb_out": A["sb_w_out"][0]}[kind]
                    eng.dma_start(cols8(dst), rows(w, 0, KC, c, c + 512)).then_inc(loaded[n % RING], 16)

            up, down = A["moe_w_gate_up"][0], A["moe_w_down"][0]

            def load(j, it):
                e, i = j // PER_E, j % PER_E
                dst = ring[(BASE + j) % RING]
                expert = it * 2 + e
                if i < 14:
                    c = (i % 2) * FE + (i // 2) * 512
                    src, to = up[expert, :, c:c + 512].rearrange("(k p) c -> p k c", p=P), cols8(dst)
                else:
                    lo = (i - 14) * 512
                    src = down[expert, lo:lo + 512, :].rearrange("(k p) c -> p k c", p=P)
                    to = dst[:].rearrange("p (k c) -> p k c", k=4)
                return to, src

            def read_by(j, it):
                e, i = j // PER_E, j % PER_E
                if i < 14:
                    return S["pair_done"], it * 56 + (28 * e + 4 * (i // 2) + 4)
                return S["down_done"], it * 112 + (56 * e + 8 * (i - 14) + 8)

            for j in range(RING):
                eng.wait_ge(*read_out(*STREAM[BASE - RING + j]))
                to, src = load(j, 0)
                eng.dma_start(to, src).then_inc(loaded[(BASE + j) % RING], 16)
            with eng.Fori(0, NE // 2 - 1) as it:
                for j in range(RING, PER_IT + RING):
                    to, src = load(j, it)
                    who, value = read_by(j - RING, it)
                    value = eng.snap(value)
                    eng.wait_ge(who, value)
                    eng.dma_start(to, src).then_inc(loaded[(BASE + j) % RING], 16)
            it = NE // 2 - 1
            for j in range(RING, PER_IT):
                to, src = load(j, it)
                eng.wait_ge(*read_by(j - RING, it))
                eng.dma_start(to, src).then_inc(loaded[(BASE + j) % RING], 16)

        @block.gpsimd
        def _(eng):
            eng.memset(ones[:], 1.0).then_inc(S["consts"], 1)
            eng.memset(ident[:], 0.0).then_inc(S["consts"], 1)
            eng.memset(sel_to[:], 0.0).then_inc(S["consts"], 1)
            eng.memset(not_before[:], -1.0).then_inc(S["consts"], 1)
            eng.wait_ge(S["consts"], 4)
            eng.affine_select(out=ident[:], in_=ident[:], compare_op=ALU.not_equal, fill=1.0, base=0,
                              pattern=[[-1, P]], channel_multiplier=1).then_inc(S["consts"], 1)
            eng.affine_select(out=after[:], in_=ones[:], compare_op=ALU.is_ge, fill=0.0, base=0,
                              pattern=[[-1, P]], channel_multiplier=1).then_inc(S["consts"], 1)
            eng.affine_select(out=before[:], in_=ones[:], compare_op=ALU.is_gt, fill=0.0, base=0,
                              pattern=[[1, P]], channel_multiplier=-1).then_inc(S["consts"], 1)
            eng.affine_select(out=not_before[:], in_=not_before[:], compare_op=ALU.is_gt, fill=0.0, base=0,
                              pattern=[[1, P]], channel_multiplier=-1).then_inc(S["consts"], 1)
            eng.affine_select(out=upto[:], in_=ones[0:C, 0:C], compare_op=ALU.is_ge, fill=0.0, base=0,
                              pattern=[[1, C]], channel_multiplier=-1).then_inc(S["consts"], 1)
            eng.affine_select(out=sel_to[:], in_=sel_to[:], compare_op=ALU.not_equal, fill=1.0, base=0,
                              pattern=[[-1, NB], [1, NB]], channel_multiplier=0).then_inc(S["consts"], 1)
            eng.iota(iota8[:], pattern=[[1, NE]], base=0, channel_multiplier=0,
                     allow_small_or_imprecise_dtypes=True).then_inc(S["consts"], 1)
            src = A["state_gla"][0].rearrange("b h k v -> b k h v")
            dst = gla_sample[0].rearrange("b h k v -> b k h v")
            eng.wait_ge(S["scores_done"], 1)
            for b in range(NB + 1):
                if b < NB:
                    if b >= 2:
                        eng.wait_ge(S[f"s0_stored{b % 2}"], 16 * (b // 2))
                        eng.wait_ge(S["os_done"], b - 1)
                    eng.dma_start(s0[b % 2], src[b]).then_inc(S[f"s0_loaded{b % 2}"], 16)
                if b >= 1:
                    eng.wait_ge(S["s_updated"], b)
                    eng.dma_start(dst[b - 1], s0[(b - 1) % 2]).then_inc(S[f"s0_stored{(b - 1) % 2}"], 16)
            eng.wait_ge(S["state_ready"], NCH)
            eng.dma_start(gla_prompt[0, 0].rearrange("h k v -> k h v"), state[(NCH - 1) % 2]).then_inc(S["state_stored"], 16)
            eng.wait_ge(S["kv_kept"], 12)
            for t, outs in ((0, (k_prompt, v_prompt)), (1, (k_prompt, v_prompt)), (2, (k_sample, v_sample))):
                for s, o in enumerate(outs):
                    flat = o.rearrange("b s h d -> (b s) (h d)")
                    lo = t * P if t < 2 else 0
                    eng.dma_start(flat[lo:lo + TOK[t], :],
                                  kvtok[0:TOK[t], t, s * D:(s + 1) * D]).then_inc(S["kv_stored"], 16)
            for t in range(TT):
                eng.wait_ge(S["y_kept"], 2 * t + 2)
                dst_y = (y_prompt[0, t * P:(t + 1) * P, :] if t < 2 else y_sample.rearrange("b s d -> (b s) d"))
                eng.dma_start(dst_y, xtok[0:TOK[t], t, :]).then_inc(S["y_stored"], 16)
            eng.wait_ge(S["s0_stored0"], 16 * NB // 2)
            eng.wait_ge(S["s0_stored1"], 16 * NB // 2)
            eng.wait_ge(S["state_stored"], 16)
            eng.wait_ge(S["kv_stored"], 16 * 6)
            eng.wait_ge(S["y_stored"], 16 * TT)

        @block.tensor
        def _(eng):
            eng.wait_ge(S["consts"], 11)
            eng.wait_ge(S["small_loaded"], 16 * 16)
            eng.transpose(pb[4][:, 0:P], h[:, 0, 0:P], ident[:])
            eng.transpose(pb[4][:, P:P + VEC_B], h[0:VEC_B, 1, 0:P], ident[0:VEC_B, 0:VEC_B]).then_inc(S["vec_turned"], 1)
            eng.wait_ge(S["c_silu"], 1)
            for k in range(KC):
                last = eng.transpose(pb[5][:, k * 16:k * 16 + NC9], csilu[:, k * P:(k + 1) * P], ident[0:NC9, 0:NC9])
            last.then_inc(S["c_turned"], 1)
            eng.wait_ge(S["x_loaded"], 16 * TT)
            for k in range(KC):
                if k >= 2:
                    eng.wait_ge(S["x_kept"], k - 1)
                for t in range(TT):
                    n = TOK[t]
                    last = eng.transpose(pb[6 + k % 2][:, t * P:t * P + n], xtok[0:n, t, k * P:(k + 1) * P], ident[0:n, 0:n])
                last.then_inc(S["x_turned"], 1)

            def ada_turn(i):
                eng.wait_ge(S["ada_copied"], i + 1)
                if i >= 2:
                    eng.wait_ge(S["ada_kept"], i - 1)
                for j in range(4):
                    last = eng.transpose(pb[2 + i % 2][:, j * 16:j * 16 + NC9], ada_row[:, i % 2, j * P:(j + 1) * P],
                                         ident[0:NC9, 0:NC9])
                last.then_inc(S["ada_turned"], 1)

            eng.wait_ge(S["c_kept"], 1)
            for i in range(N_ADA):
                w = cols8(slot("ada", i))
                landed(eng, "ada", i)
                if i >= 2:
                    eng.wait_ge(S["ada_copied"], i - 1)
                for k in range(KC):
                    last = eng.matmul(pb[i % 2][0:NC9, :], cT[:, k, :], w[:, k, :], start=k == 0, stop=k == KC - 1)
                last.then_inc(S["ada_row_done"], 1)
                if i >= 1:
                    ada_turn(i - 1)
            ada_turn(N_ADA - 1)

            def sum_squares(m):
                for k in range(KC):
                    eng.wait_ge(S["squared"], m * KC + k + 1)
                    last = eng.matmul(pb[7][:, 0:T], ones[:], h[:, k, :], start=k == 0, stop=k == KC - 1)
                last.then_inc(S["ss_done"], 1)

            def free_bank(n):
                if n >= 4:
                    who, value = empt[n - 4]
                    eng.wait_ge(S[who], value)

            def project(kind, n_tiles, src, ready):
                for i in range(n_tiles):
                    w = cols8(slot(kind, i))
                    landed(eng, kind, i)
                    for j in range(4):
                        n = BLOCK_AT[kind, 4 * i + j]
                        free_bank(n)
                        for k in range(KC):
                            if i == 0 and j == 0:
                                ready(k)
                            last = eng.matmul(pb[n % 4][:, 0:T], w[:, k, j * P:(j + 1) * P], src[:, k, :],
                                              start=k == 0, stop=k == KC - 1)
                        last.then_inc(S["block_done"], 1)

            def h_is_ready(m):
                def ready(k):
                    eng.wait_ge(S["h_ready"], m * KC + k + 1)
                    if k == 0:
                        eng.wait_ge(S["hs_ready"], m + 1)
                return ready

            sum_squares(MIX0)
            project("gla_in", 6, h, h_is_ready(MIX0))
            n = BLOCK_AT["gla_in", 24]
            free_bank(n)
            for k in range(KC):
                last = eng.matmul(pb[n % 4][0:GR, 0:T], wr[:, k, :], h[:, k, :], start=k == 0, stop=k == KC - 1)
            last.then_inc(S["block_done"], 1)
            eng.wait_ge(S["kept_act"], 25)
            for g in range(GH):
                last = eng.matmul(pb[4 + g][:, 0:T], w_gate2[:, g * DK:(g + 1) * DK], rT[:], start=True, stop=True)
            last.then_inc(S["gate_done"], 1)
            eng.wait_ge(S["decayed"], 4)
            for c in range(NCH):
                for g in range(GH):
                    u, v = g * NCH + c, c * GH + g
                    to = pb[4 + v // 8][:, (v % 8) * C:(v % 8 + 1) * C]
                    for a in range(2):
                        eng.matmul(to[a * HALF:(a + 1) * HALF, a * HALF:(a + 1) * HALF], kd[:, 2 * u + a, :],
                                   qd[:, 2 * u + a, :], start=True, stop=True)
                    last = eng.matmul(to[0:HALF, HALF:C], ko[:, u, :], qo[:, u, :], start=True, stop=True)
            last.then_inc(S["scores_done"], 1)
            eng.wait_ge(S["decayed"], 6)
            for c in range(NCH):
                if c >= 1:
                    eng.wait_ge(S["v_kept"], 2 * c)
                for j in range(8):
                    eng.transpose(pb[j // 4][0:C, (j % 4) * P:(j % 4 + 1) * P], big[:, 8 + j, c * C:(c + 1) * C], ident[:])
                for g in range(GH):
                    last = eng.transpose(pb[2][0:C, g * DK:(g + 1) * DK], ke[:, g, c * C:(c + 1) * C], ident[:])
                last.then_inc(S["v_turned"], 1)
                eng.wait_ge(S["v_kept"], 2 * c + 2)
                if c == 0:
                    eng.wait_ge(S["scores_kept"], 1)
                if c >= 1:
                    eng.wait_ge(S["o_kept"], c)
                    eng.wait_ge(S["state_ready"], c)
                for g in range(GH):
                    for a in range(2):
                        to = pb[3][:, (2 * g + a) * C:(2 * g + a + 1) * C]
                        last = eng.matmul(to, vtok[c % 2][:, g * DV + a * P:g * DV + (a + 1) * P], st[:, c * GH + g, :],
                                          start=True, stop=c == 0)
                        if c > 0:
                            last = eng.matmul(to, state[(c - 1) % 2][:, g, a * P:(a + 1) * P], qe[:, g, c * C:(c + 1) * C],
                                              start=False, stop=True)
                last.then_inc(S["o_done"], 1)
                for g in range(GH):
                    last = eng.matmul(pb[6 + g // 2][:, (g % 2) * DV:(g % 2 + 1) * DV],
                                      ktok[:, (c % 2) * 512 + g * DK:(c % 2) * 512 + (g + 1) * DK],
                                      vtok[c % 2][:, g * DV:(g + 1) * DV], start=True, stop=True)
                last.then_inc(S["u_done"], 1)
            eng.wait_ge(S["v_kept"], 2 * NCH)
            for j in range(8):
                last = eng.transpose(pb[j // 4][0:NB, (j % 4) * P:(j % 4 + 1) * P], big[:, 8 + j, TP:T], ident[:])
            last.then_inc(S["vs_turned"], 1)
            eng.wait_ge(S["vs_kept"], 1)
            eng.wait_ge(S["state_ready"], NCH)
            eng.wait_ge(S["o_kept"], NCH)
            for b in range(NB + 1):
                if b < NB:
                    if b >= 2:
                        eng.wait_ge(S["s_updated"], b - 1)
                    for a in range(2):
                        last = eng.matmul(pb[4 + 2 * (b % 2) + a], sel(b), vs_tok[:, a * 512:(a + 1) * 512],
                                          start=True, stop=True)
                    last.then_inc(S["vbc_done"], 1)
                if b >= 1:
                    eng.wait_ge(S["s_updated"], b)
                    for g in range(GH):
                        for a in range(2):
                            at8 = (2 * g + a) * NB + b - 1
                            last = eng.matmul(pb[3][:, at8:at8 + 1], s0[(b - 1) % 2][:, g, a * P:(a + 1) * P],
                                              big[:, g, TP + b - 1:TP + b], start=True, stop=True)
                    last.then_inc(S["os_done"], 1)
            for g in range(GH):
                eng.wait_ge(S["osq_ready"], g + 1)
                for a in range(2):
                    last = eng.matmul(pb[4 + g][:, 0:T], ones[:], big[:, 2 * g + a, :], start=a == 0, stop=a == 1)
            last.then_inc(S["oss_done"], 1)
            project("gla_out", 2, h, lambda k: eng.wait_ge(S["o_ready"], k + 1))

            sum_squares(FFN0)
            for i in range(11):
                w = slot("ffn_up", i)[:].rearrange("p (k s c) -> p k s c", k=KC, s=2)
                landed(eng, "ffn_up", i)
                for j in range(2):
                    for s in range(2):
                        n = BLOCK_AT["ffn_up", 4 * i + 2 * j + s]
                        free_bank(n)
                        for k in range(KC):
                            if i == 0 and j == 0 and s == 0:
                                h_is_ready(FFN0)(k)
                            last = eng.matmul(pb[n % 4][:, 0:T], w[:, k, s, j * P:(j + 1) * P], h[:, k, :],
                                              start=k == 0, stop=k == KC - 1)
                        last.then_inc(S["block_done"], 1)
            for i in range(6):
                ks = min(4, FFC - 4 * i)
                w = slot("ffn_down", i)[:].rearrange("p (k c) -> p k c", k=4)
                landed(eng, "ffn_down", i)
                if i == 0:
                    eng.wait_ge(S["kept_dve"], empt[BLOCK_AT["ffn_up", 43]][1])
                for j in range(8):
                    n = BLOCK_AT["ffn_down", 8 * i + j]
                    free_bank(n)
                    for k in range(ks):
                        last = eng.matmul(pb[n % 4][:, 0:T], w[:, k, j * P:(j + 1) * P], big[:, 4 * i + k, :],
                                          start=k == 0, stop=k == ks - 1)
                    last.then_inc(S["block_done"], 1)

            sum_squares(KV)
            project("kv", 4, h, h_is_ready(KV))
            for t in range(TT):
                n = TOK[t]
                for q in range(4):
                    i = 4 * t + q
                    if i == 0:
                        eng.wait_ge(S["kept_act"], empt[BLOCK_AT["kv", 15]][1])
                    if i >= 2:
                        eng.wait_ge(S["kv_kept"], i - 1)
                    for j in range(4):
                        last = eng.transpose(pb[4 + i % 2][0:n, j * P:(j + 1) * P], big[:, 4 * q + j, t * P:t * P + n], ident[:])
                    last.then_inc(S["kv_turned"], 1)
            sum_squares(MIX1)
            project("sb_q", 2, h, h_is_ready(MIX1))
            eng.wait_ge(S["kept_act"], empt[BLOCK_AT["sb_q", 7]][1])
            for j in range(8):
                last = eng.transpose(pb[4 + j // 4][0:NB, (j % 4) * P:(j % 4 + 1) * P], big[:, 16 + j, TP:T], ident[:])
            last.then_inc(S["qs_turned"], 1)
            eng.wait_ge(S["qs_kept"], 1)
            for b in range(NB):
                if b >= 2:
                    eng.wait_ge(S["z_s_ready"], b - 1)
                for a in range(2):
                    last = eng.matmul(pb[4 + 2 * (b % 2) + a], sel(b), qs_tok[:, a * 512:(a + 1) * 512],
                                      start=True, stop=True)
                last.then_inc(S["qbc_done"], 1)

            def z_products(g):
                if g >= 2:
                    eng.wait_ge(S["z_ready"], g - 1)
                for a in range(2):
                    to = pb[2 * (g % 2) + a]
                    k, q = big[a * SD:(a + 1) * SD, g, 0:TP], big[a * SD:(a + 1) * SD, 16 + g, 0:TP]
                    eng.matmul(to[:, 0:P], k[:, 0:P], q[:, 0:P], start=True, stop=True)
                    eng.matmul(to[:, P:2 * P], k[:, P:TP], q[:, P:TP], start=True, stop=True)
                    last = eng.matmul(to[:, 2 * P:3 * P], k[:, 0:P], q[:, P:TP], start=True, stop=True)
                last.then_inc(S["z_done"], 1)

            def later_sums(g):
                eng.wait_ge(S["l_ready"], g + 1)
                if g >= 1:
                    eng.wait_ge(S["arg_ready"], g)
                lg = l_buf[:, g % 2, :]
                eng.matmul(pb[4], after[:], lg[:, 0:512], start=True, stop=True)
                eng.matmul(pb[5][:, 0:256], after[:], lg[:, 512:768], start=True, stop=False)
                eng.matmul(pb[5][:, 0:256], ones[:], lg[:, 256:512], start=False, stop=True).then_inc(S["rc_done"], 1)

            def values(g):
                eng.wait_ge(S["p_ready"], g + 1)
                if g >= 2:
                    eng.wait_ge(S["pv_kept"], g - 1)
                pg = z_buf[:, g % 2, :]
                for a in range(2):
                    lo = D + (2 * g + a) * SD
                    to = pb[6 + g % 2][a * SD:(a + 1) * SD, :]
                    eng.matmul(to[:, 0:P], kvtok[:, 0, lo:lo + SD], pg[:, a * P:(a + 1) * P], start=True, stop=True)
                    eng.matmul(to[:, P:TP], kvtok[:, 0, lo:lo + SD], pg[:, 512 + a * P:512 + (a + 1) * P],
                               start=True, stop=False)
                    last = eng.matmul(to[:, P:TP], kvtok[:, 1, lo:lo + SD], pg[:, 256 + a * P:256 + (a + 1) * P],
                                      start=False, stop=True)
                last.then_inc(S["pv_done"], 1)

            eng.wait_ge(S["kv_kept"], 12)
            eng.wait_ge(S["z_s_ready"], NB)
            G = SH // 2
            for g in range(G + 2):
                if g < G:
                    z_products(g)
                if 1 <= g <= G:
                    later_sums(g - 1)
                if g >= 2:
                    values(g - 2)
            eng.wait_ge(S["l_ready"], G + 1)
            eng.wait_ge(S["arg_ready"], G)
            eng.matmul(pb[4][:, 0:128], after[:], ls[:, 0, :], start=True, stop=False, skip_group_check=True)
            eng.matmul(pb[4][:, 0:128], ones[:], ls[:, 1, :], start=False, stop=True, skip_group_check=True)
            eng.matmul(pb[4][:, 128:256], after[:], ls[:, 1, :], start=True, stop=True).then_inc(S["rcs_done"], 1)
            eng.wait_ge(S["exps_s"], 1)
            eng.wait_ge(S["z_ready"], G)
            for b in range(NB + 1):
                if b < NB:
                    if b % 2 == 0:
                        landed(eng, "v_cache", b // 2)
                    if b >= 1:
                        eng.wait_ge(S["own_ready"], b)
                    vt = slot("v_cache", b // 2)
                    for a in range(2):
                        for page in range(PAGES):
                            lo = ((b % 2) * 2 + page) * D + a * 512
                            last = eng.matmul(pb[a][0:SH, :], zs[:, page, b * SH:(b + 1) * SH], vt[:, lo:lo + 512],
                                              start=page == 0, stop=page == 1)
                    last.then_inc(S["opv_done"], 1)
                if b >= 1:
                    eng.wait_ge(S["own_ready"], b)
                    for a in range(2):
                        last = eng.matmul(pb[2 + a][0:NB, :], sel_to[:, b - 1, :], os_row[:, a * 512:(a + 1) * 512],
                                          start=b == 1, stop=b == NB, skip_group_check=True)
                    last.then_inc(S["ot_done"], 1)
            eng.wait_ge(S["ot_kept"], 1)
            eng.wait_ge(S["pv_kept"], G)
            for j in range(8):
                last = eng.transpose(pb[5][:, j * 8:(j + 1) * 8], os_tok[:, j * P:(j + 1) * P], ident[0:NB, 0:NB])
            last.then_inc(S["otT_done"], 1)
            project("sb_out", 2, h, lambda k: eng.wait_ge(S["otT_kept"], 1) if k == 0 else None)

            sum_squares(FFN1)
            for t in range(TT):
                for k in range(KC):
                    if t == 0:
                        h_is_ready(FFN1)(k)
                    last = eng.matmul(pb[4][0:TOK[t], t * NE:(t + 1) * NE], h[:, k, t * P:t * P + TOK[t]], w_router[:, k, :],
                                      start=k == 0, stop=k == KC - 1)
            last.then_inc(S["logits_done"], 1)
            eng.wait_ge(S["gates_ready"], 1)
            for t in range(TT):
                n = TOK[t]
                last = eng.transpose(pb[5][0:NE, t * P:t * P + n], gate_tok[0:n, t, :], ident[0:n, 0:n])
            last.then_inc(S["gateT_done"], 1)
            eng.wait_ge(S["gateT_kept"], 1)
            for e in range(NE):
                if e >= 2:
                    eng.wait_ge(S["gbc_kept"], e - 1)
                eng.matmul(pb[6 + e % 2][:, 0:T], sel(e), gateT[:], start=True, stop=True).then_inc(S["gbc_done"], 1)
            eng.wait_ge(S["kept_dve"], empt[-1][1])
            with eng.Fori(0, NE // 2) as it:
                for e in range(2):
                    for p in range(7):
                        ws = []
                        for s in range(2):
                            j = PER_E * e + 2 * p + s
                            eng.wait_ge(loaded[(BASE + j) % RING], it * (PER_IT // RING * 16) + LAND0[(BASE + j) % RING] + 16 * (j // RING + 1))
                            ws.append(cols8(ring[(BASE + j) % RING]))
                        for q in range(4):
                            n = 4 * p + q
                            if n >= 2:
                                eng.wait_ge(S["pair_kept"], it * 56 + (28 * e + n - 1))
                            else:
                                eng.wait_ge(S["down_kept"], it * 112 + 56 * e)
                            for s in range(2):
                                for k in range(KC):
                                    last = eng.matmul(pb[2 * (n % 2) + s][:, 0:T], ws[s][:, k, q * P:(q + 1) * P], h[:, k, :],
                                                      start=k == 0, stop=k == KC - 1)
                                last.then_inc(S["gate_half_done" if s == 0 else "pair_done"], 1)
                    eng.wait_ge(S["pair_kept"], it * 56 + 28 * (e + 1))
                    for i in range(7):
                        j = PER_E * e + 14 + i
                        eng.wait_ge(loaded[(BASE + j) % RING], it * (PER_IT // RING * 16) + LAND0[(BASE + j) % RING] + 16 * (j // RING + 1))
                        w = ring[(BASE + j) % RING][:].rearrange("p (k c) -> p k c", k=4)
                        for dc in range(8):
                            n = 8 * i + dc
                            if n >= 4:
                                eng.wait_ge(S["down_kept"], it * 112 + (56 * e + n - 3))
                            for k in range(4):
                                last = eng.matmul(pb[n % 4][:, 0:T], w[:, k, dc * P:(dc + 1) * P], big[:, 4 * i + k, :],
                                                  start=k == 0, stop=k == 3)
                            last.then_inc(S["down_done"], 1)

            sum_squares(FINAL)
            for t in range(TT):
                n = TOK[t]
                for a in range(2):
                    i = 2 * t + a
                    if i == 0:
                        for k in range(KC):
                            h_is_ready(FINAL)(k)
                    if i >= 2:
                        eng.wait_ge(S["y_kept"], i - 1)
                    for j in range(4):
                        last = eng.transpose(pb[4 + i % 2][0:n, j * P:(j + 1) * P], h[:, 4 * a + j, t * P:t * P + n], ident[:])
                    last.then_inc(S["y_turned"], 1)

        @block.scalar
        def _(eng):
            steps = [0]

            def link(ins):
                steps[0] += 1
                ins.then_inc(S["act_step"], 1)
                eng.wait_ge(S["act_step"], steps[0])

            eng.wait_ge(S["small_loaded"], 16 * 16)
            eng.activation(csilu, crow, ACT.Silu).then_inc(S["c_silu"], 1)
            for i in range(N_ADA):
                eng.wait_ge(S["ada_row_done"], i + 1)
                if i >= 2:
                    eng.wait_ge(S["ada_turned"], i - 1)
                eng.copy(ada_row[:, i % 2, :], pb[i % 2][0:NC9, :]).then_inc(S["ada_copied"], 1)

            def norm(m):
                for k in range(KC):
                    eng.activation(h[:, k, :], x[:, k, :], ACT.Square).then_inc(S["squared"], 1)
                eng.wait_ge(S["ms_ready"], m + 1)
                eng.activation(rstd[:], rstd[:], ACT.Sqrt).then_inc(S["root_ready"], 1)
                for k in range(KC):
                    eng.wait_ge(S["scaled"], m * KC + k + 1)
                    eng.activation(h[:, k, 0:TP], h[:, k, 0:TP], ACT.Identity, bias=mod[:, SHIFT[m] + k, 0:1],
                                   scale=gain[:, m, k, 0:1]).then_inc(S["h_ready"], 1)

            def block(kind, i):
                n = BLOCK_AT[kind, i]
                eng.wait_ge(S["block_done"], n + 1)
                return pb[n % 4][:, 0:T]

            eng.wait_ge(S["x_kept"], KC)
            eng.wait_ge(S["vec_kept"], 2)
            eng.wait_ge(S["gains_ready"], 6)
            norm(MIX0)
            for i in range(24):
                got = block("gla_in", i)
                if i < 4:
                    ins = eng.activation(big[:, i, :], got, ACT.Copy, scale=float(DK) ** -0.5)
                else:
                    ins = eng.activation(big[:, i, :], got, ACT.Copy if i < 16 else ACT.Silu)
                ins.then_inc(S["kept_act"], 1)
            eng.copy(rT, block("gla_in", 24)[0:GR, :]).then_inc(S["kept_act"], 1)
            eng.wait_ge(S["gate_done"], 1)
            for g in range(GH):
                eng.activation(la[:, g, :], pb[4 + g][:, 0:T], ACT.Identity, bias=vec_b[:, GLA_BIAS + g:GLA_BIAS + g + 1])
                last = eng.activation(t_abs[:, g, :], pb[4 + g][:, 0:T], ACT.Abs,
                                      bias=vec_b[:, GLA_BIAS + g:GLA_BIAS + g + 1])
            link(last)
            link(eng.activation(t_abs, t_abs, ACT.Exp, scale=-1.0))
            eng.activation(t_abs, t_abs, ACT.Ln, bias=1.0).then_inc(S["log_sig"], 1)
            eng.wait_ge(S["args_ready"], 1)
            ends = cum.rearrange("p (u s) t -> p u s t", s=2)[:, :, 1, HALF - 1]
            for to, arg in ((qd, qd), (kd, kd), (qo, qo), (ko, ko),
                            (qe, cum.rearrange("p u t -> p (u t)").rearrange("p (h t) -> p h t", h=GH)),
                            (ke, ke), (dec, ends), (ea[:], la[:, :, TP:T])):
                eng.activation(to, arg, ACT.Exp).then_inc(S["exps_ready"], 1)
            for c in range(NCH):
                eng.wait_ge(S["v_turned"], c + 1)
                if c >= 2:
                    eng.wait_ge(S["u_done"], c - 1)
                eng.copy(vtok[c % 2][:, 0:512], pb[0][0:C, :])
                eng.copy(vtok[c % 2][:, 512:D], pb[1][0:C, :]).then_inc(S["v_kept"], 1)
                eng.copy(ktok[:, (c % 2) * 512:(c % 2 + 1) * 512], pb[2][0:C, :]).then_inc(S["v_kept"], 1)
            eng.wait_ge(S["vs_turned"], 1)
            eng.wait_ge(S["o_done"], NCH)
            eng.copy(vs_tok[:, 0:512], pb[0][0:NB, :])
            eng.copy(vs_tok[:, 512:D], pb[1][0:NB, :]).then_inc(S["vs_kept"], 1)
            eng.wait_ge(S["os_kept"], 1)
            for g in range(GH):
                eng.activation(big[:, 2 * g:2 * g + 2, :], h[:, 2 * g:2 * g + 2, :], ACT.Square).then_inc(S["osq_ready"], 1)
            eng.wait_ge(S["oms_ready"], 1)
            eng.activation(orstd, orstd, ACT.Sqrt).then_inc(S["oroot_ready"], 1)

            eng.wait_ge(S["kept_dve"], empt[BLOCK_AT["gla_out", 7]][1])
            norm(FFN0)
            for i in range(FFC):
                got = block("ffn_up", 2 * i)
                if i >= 2:
                    eng.wait_ge(S["kept_dve"], empt[BLOCK_AT["ffn_up", 2 * i - 4]][1])
                eng.activation(silu_a[:, i % 2, :], got, ACT.Silu).then_inc(S["silu_done"], 1)
            eng.wait_ge(S["kept_dve"], empt[BLOCK_AT["ffn_down", 47]][1])
            norm(KV)
            for i in range(16):
                eng.copy(big[:, i, :], block("kv", i)).then_inc(S["kept_act"], 1)
            eng.wait_ge(S["s0_stored0"], 16 * NB // 2)
            eng.wait_ge(S["s0_stored1"], 16 * NB // 2)
            eng.wait_ge(S["state_stored"], 16)
            for i in range(12):
                t, q = i // 4, i % 4
                eng.wait_ge(S["kv_turned"], i + 1)
                eng.copy(kvtok[0:TOK[t], t, q * 512:(q + 1) * 512], pb[4 + i % 2][0:TOK[t], :]).then_inc(S["kv_kept"], 1)
            norm(MIX1)
            for i in range(8):
                eng.copy(big[:, 16 + i, :], block("sb_q", i)).then_inc(S["kept_act"], 1)
            eng.wait_ge(S["qs_turned"], 1)
            eng.copy(qs_tok[:, 0:512], pb[4][0:NB, :])
            eng.copy(qs_tok[:, 512:D], pb[5][0:NB, :]).then_inc(S["qs_kept"], 1)

            def soft(g, z, to):
                eng.wait_ge(S["z_ready"], g + 1)
                if 2 <= g < SH // 2:
                    eng.wait_ge(S["rc_done"], g - 1)
                link(eng.activation(to, z, ACT.Abs))
                link(eng.activation(to, to, ACT.Exp, scale=-1.0))
                eng.activation(to, to, ACT.Ln, bias=1.0).then_inc(S["soft_ready"], 1)

            G = SH // 2
            for g in range(G + 2):
                if g < G:
                    soft(g, z_buf[:, g % 2, :], l_buf[:, g % 2, :])
                if 1 <= g <= G:
                    eng.wait_ge(S["arg_ready"], g)
                    zg = z_buf[:, (g - 1) % 2, :]
                    eng.activation(zg, zg, ACT.Exp).then_inc(S["p_exp"], 1)
                if g >= 2:
                    eng.wait_ge(S["pv_done"], g - 1)
                    eng.copy(h[:, g - 2, 0:TP], pb[6 + g % 2][:, 0:TP]).then_inc(S["pv_kept"], 1)
            soft(G, zs, ls)
            eng.wait_ge(S["args_s"], 1)
            eng.activation(zs, zs, ACT.Exp).then_inc(S["exps_s"], 1)
            eng.wait_ge(S["otT_done"], 1)
            eng.copy(h[:, :, TP:T], pb[5][:, 0:64].rearrange("p (k b) -> p k b", b=NB)).then_inc(S["otT_kept"], 1)

            eng.wait_ge(S["kept_dve"], empt[-1][1])
            norm(FFN1)
            eng.wait_ge(S["gates_exp"], 1)
            for t in range(TT):
                last = eng.activation(e2[0:TOK[t], t:t + 1], e2[0:TOK[t], t:t + 1], ACT.Exp)
            last.then_inc(S["gates_exp_done"], 1)
            eng.wait_ge(S["gateT_done"], 1)
            eng.copy(gateT, pb[5][0:NE, 0:T]).then_inc(S["gateT_kept"], 1)
            for e in range(NE):
                eng.wait_ge(S["gbc_done"], e + 1)
                eng.copy(gate_bc[:, e, :], pb[6 + e % 2][:, 0:T]).then_inc(S["gbc_kept"], 1)
            with eng.Fori(0, NE // 2) as it:
                for n in range(2 * FEC):
                    eng.wait_ge(S["gate_half_done"], it * 56 + (n + 1))
                    eng.activation(silu_m[:, n % 2, :], pb[2 * (n % 2)][:, 0:T], ACT.Silu).then_inc(S["pair_silu"], 1)
            eng.wait_ge(S["down_kept"], NE * 56)
            norm(FINAL)
            for i in range(6):
                t, a = i // 2, i % 2
                eng.wait_ge(S["y_turned"], i + 1)
                eng.copy(xtok[0:TOK[t], t, a * 512:(a + 1) * 512], pb[4 + i % 2][0:TOK[t], :]).then_inc(S["y_kept"], 1)

        @block.vector
        def _(eng):
            steps = [0]

            def link(ins):
                steps[0] += 1
                ins.then_inc(S["dve_step"], 1)
                eng.wait_ge(S["dve_step"], steps[0])

            eng.wait_ge(S["vec_turned"], 1)
            eng.tensor_copy(vec_a[:], pb[4][:, 0:P]).then_inc(S["vec_kept"], 1)
            eng.tensor_copy(vec_b[:], pb[4][:, P:P + VEC_B]).then_inc(S["vec_kept"], 1)
            eng.wait_ge(S["c_turned"], 1)
            eng.tensor_copy(cT[:], pb[5][:, 0:P].rearrange("p (k c) -> p k c", c=16)[:, :, 0:NC9]).then_inc(S["c_kept"], 1)
            for k in range(KC):
                eng.wait_ge(S["x_turned"], k + 1)
                eng.tensor_copy(x[:, k, :], pb[6 + k % 2][:, 0:T]).then_inc(S["x_kept"], 1)
            eng.wait_ge(S["vec_kept"], 2)
            for i in range(N_ADA):
                eng.wait_ge(S["ada_turned"], i + 1)
                eng.tensor_tensor(mod[:, 4 * i:4 * i + 4, :],
                                  pb[2 + i % 2][:, 0:64].rearrange("p (k c) -> p k c", c=16)[:, :, 0:NC9],
                                  vec_a[:, 4 * i:4 * i + 4].unsqueeze(2).to_broadcast([P, 4, NC9]),
                                  ALU.add).then_inc(S["ada_kept"], 1)
            eng.wait_ge(S["ada_kept"], N_ADA)
            for m in range(6):
                eng.scalar_tensor_tensor(gain[:, m, :, :], mod[:, SCALE[m]:SCALE[m] + KC, :], 1.0,
                                         vec_b[:, GAIN[m]:GAIN[m] + KC].unsqueeze(2).to_broadcast([P, KC, NC9]),
                                         ALU.add, ALU.mult).then_inc(S["gains_ready"], 1)
            eng.wait_ge(S["gains_ready"], 6)

            def norm(m):
                eng.wait_ge(S["ss_done"], m + 1)
                eng.tensor_scalar(rstd[:], pb[7][:, 0:T], 1.0 / D, EPS, ALU.mult, ALU.add).then_inc(S["ms_ready"], 1)
                eng.wait_ge(S["root_ready"], m + 1)
                link(eng.reciprocal(rstd[:], rstd[:]))
                for k in range(KC):
                    eng.tensor_tensor(h[:, k, :], x[:, k, :], rstd[:], ALU.mult).then_inc(S["scaled"], 1)
                eng.wait_ge(S["scaled"], (m + 1) * KC)
                hs = h[:, :, TP:T]
                link(eng.tensor_tensor(hs, hs, gain[:, m, :, 1:NC9], ALU.mult))
                eng.tensor_tensor(hs, hs, mod[:, SHIFT[m]:SHIFT[m] + KC, 1:NC9], ALU.add).then_inc(S["hs_ready"], 1)

            def add_to_x(got, k, gate, parted, value):
                xs, ts = x[:, k, TP:T], tmp8[:, k, :]
                eng.scalar_tensor_tensor(x[:, k, 0:TP], got[:, 0:TP], mod[:, gate + k, 0:1], x[:, k, 0:TP], ALU.mult, ALU.add)
                eng.tensor_tensor(ts, got[:, TP:T], mod[:, gate + k, 1:NC9], ALU.mult).then_inc(parted, 1)
                eng.wait_ge(parted, value)
                return eng.tensor_tensor(xs, xs, ts, ALU.add)

            parts = [0]

            def add_block(kind, i, gate):
                n = BLOCK_AT[kind, i]
                eng.wait_ge(S["block_done"], n + 1)
                if empt[n][1] > 1:
                    eng.wait_ge(S["kept_dve"], empt[n][1] - 1)
                parts[0] += 1
                add_to_x(pb[n % 4], i % 8, gate, S["part_added"], parts[0]).then_inc(S["kept_dve"], 1)

            norm(MIX0)
            eng.wait_ge(S["log_sig"], 1)
            link(eng.scalar_tensor_tensor(la, la, 0.0, t_abs, ALU.min, ALU.subtract))
            link(eng.tensor_scalar(la, la, 1.0 / 16.0, None, ALU.mult))
            four = lambda v: v.rearrange("p (h c s) t -> p h c (s t)", h=GH, c=NCH)
            src = la[:, :, 0:TP].rearrange("p h (c t) -> p h c t", t=C)
            for n, d in enumerate((1, 2, 4, 8, 16, 32)):
                dst = four(cum_a if n % 2 == 0 else cum)
                eng.tensor_copy(dst[:, :, :, 0:d], src[:, :, :, 0:d])
                link(eng.tensor_tensor(dst[:, :, :, d:C], src[:, :, :, d:C], src[:, :, :, 0:C - d], ALU.add))
                src = dst
            mid = cum[:, :, HALF // 2 - 1:HALF // 2].to_broadcast([P, 32, HALF])
            link(eng.tensor_tensor(qd, cum, mid, ALU.subtract))
            eng.tensor_scalar(kd, qd, -1.0, EXP_CAP, ALU.mult, ALU.min)
            halves = cum.rearrange("p (u s) t -> p u s t", s=2)
            seam = halves[:, :, 0, HALF - 1:HALF].to_broadcast([P, 16, HALF])
            eng.tensor_tensor(qo, halves[:, :, 1, :], seam, ALU.subtract)
            link(eng.tensor_tensor(ko, seam, halves[:, :, 0, :], ALU.subtract))
            chunks = cum.rearrange("p (u s) t -> p u (s t)", s=2)
            eng.tensor_tensor(ke.rearrange("p h t -> p (h t)").rearrange("p (u t) -> p u t", u=16),
                              chunks[:, :, C - 1:C].to_broadcast([P, 16, C]), chunks, ALU.subtract)
            eng.tensor_scalar(qd, qd, EXP_CAP, None, ALU.min).then_inc(S["args_ready"], 1)
            q, k = big[:, 0:GH, 0:TP], big[:, GH:2 * GH, 0:TP]
            by_head = lambda v: v.rearrange("p (h u) t -> p h (u t)", h=GH)
            side = lambda v, s: v.rearrange("p h (c s t) -> p h c s t", c=NCH, s=2)[:, :, :, s, :]
            by_chunk = lambda v: v.rearrange("p (h c) t -> p h c t", h=GH)
            for n, (v, w) in enumerate(((by_head(qd), q), (by_head(kd), k), (by_chunk(qo), side(q, 1)),
                                        (by_chunk(ko), side(k, 0)), (qe, q), (ke, k))):
                eng.wait_ge(S["exps_ready"], n + 1)
                eng.tensor_tensor(v, v, w, ALU.mult).then_inc(S["decayed"], 1)
            link(eng.memset(st[HALF:C, :, 0:HALF], 0.0))
            eng.wait_ge(S["scores_done"], 1)
            for n in range(2):
                got = pb[4 + n].rearrange("p (u t) -> p u t", t=C)
                eng.tensor_tensor(st[:, 8 * n:8 * n + 8, HALF:C], got[0:C, :, HALF:C],
                                  upto[:, HALF:C].unsqueeze(1).to_broadcast([C, 8, HALF]), ALU.mult)
                last = eng.tensor_tensor(st[0:HALF, 8 * n:8 * n + 8, 0:HALF], got[0:HALF, :, 0:HALF],
                                         upto[0:HALF, 0:HALF].unsqueeze(1).to_broadcast([HALF, 8, HALF]), ALU.mult)
            last.then_inc(S["scores_kept"], 1)
            for c in range(NCH):
                eng.wait_ge(S["o_done"], c + 1)
                eng.tensor_copy(h[:, :, c * C:(c + 1) * C], pb[3].rearrange("p (k t) -> p k t", t=C)).then_inc(S["o_kept"], 1)
                eng.wait_ge(S["u_done"], c + 1)
                u = psum[:, 6 * 512:8 * 512].rearrange("p (g v) -> p g v", g=GH)
                if c == 0:
                    eng.tensor_copy(state[0], u).then_inc(S["state_ready"], 1)
                    continue
                eng.wait_ge(S["state_ready"], c)
                eng.wait_ge(S["exps_ready"], 7)
                for g in range(GH):
                    last = eng.scalar_tensor_tensor(state[c % 2][:, g, :], state[(c - 1) % 2][:, g, :],
                                                    dec[:, g * NCH + c:g * NCH + c + 1], u[:, g, :], ALU.mult, ALU.add)
                last.then_inc(S["state_ready"], 1)
            eng.wait_ge(S["exps_ready"], 8)
            for b in range(NB):
                eng.wait_ge(S[f"s0_loaded{b % 2}"], 16 * (b // 2 + 1))
                s = s0[b % 2]
                for g in range(GH):
                    last = eng.tensor_scalar(s[:, g, :], s[:, g, :], ea[:, g, b:b + 1], None, ALU.mult)
                link(last)
                eng.wait_ge(S["vbc_done"], b + 1)
                v = psum[:, (4 + 2 * (b % 2)) * 512:(6 + 2 * (b % 2)) * 512].rearrange("p (g v) -> p g v", g=GH)
                for g in range(GH):
                    last = eng.scalar_tensor_tensor(s[:, g, :], v[:, g, :], big[:, GH + g, TP + b:TP + b + 1], s[:, g, :],
                                                    ALU.mult, ALU.add)
                last.then_inc(S["s_updated"], 1)
            eng.wait_ge(S["os_done"], NB)
            eng.tensor_copy(h[:, :, TP:T], pb[3][:, 0:64].rearrange("p (k b) -> p k b", b=NB)).then_inc(S["os_kept"], 1)
            eng.wait_ge(S["oss_done"], 1)
            for g in range(GH):
                last = eng.tensor_scalar(orstd[:, g, :], pb[4 + g][:, 0:T], 1.0 / DV, EPS, ALU.mult, ALU.add)
            last.then_inc(S["oms_ready"], 1)
            eng.wait_ge(S["oroot_ready"], 1)
            link(eng.reciprocal(orstd, orstd))
            for j in range(KC):
                link(eng.scalar_tensor_tensor(h[:, j, :], h[:, j, :], vec_b[:, GLA_GAIN + j % 2:GLA_GAIN + j % 2 + 1],
                                              orstd[:, j // 2, :], ALU.mult, ALU.mult))
                eng.tensor_tensor(h[:, j, :], h[:, j, :], big[:, 16 + j, :], ALU.mult).then_inc(S["o_ready"], 1)
            for i in range(8):
                add_block("gla_out", i, GATE[MIX0])

            norm(FFN0)
            for i in range(FFC):
                n = BLOCK_AT["ffn_up", 2 * i + 1]
                eng.wait_ge(S["block_done"], n + 1)
                eng.wait_ge(S["silu_done"], i + 1)
                eng.tensor_tensor(big[:, i, :], silu_a[:, i % 2, :], pb[n % 4][:, 0:T], ALU.mult).then_inc(S["kept_dve"], 1)
            for i in range(48):
                add_block("ffn_down", i, GATE[FFN0])
            norm(KV)
            norm(MIX1)

            for b in range(NB):
                if b % 2 == 0:
                    landed(eng, "k_cache", b // 2)
                eng.wait_ge(S["qbc_done"], b + 1)
                qb = psum[:, (4 + 2 * (b % 2)) * 512:(6 + 2 * (b % 2)) * 512]
                for page in range(PAGES):
                    lo = ((b % 2) * 2 + page) * D
                    link(eng.tensor_tensor(prod, slot("k_cache", b // 2)[:, lo:lo + D], qb, ALU.mult))
                    last = eng.tensor_reduce(zs[:, page, b * SH:(b + 1) * SH], prod.rearrange("p (h d) -> p h d", h=SH),
                                             AX.X, ALU.add)
                    if page == 0:
                        link(last)
                last.then_inc(S["z_s_ready"], 1)
                eng.wait_ge(S["z_s_ready"], b + 1)

            G = SH // 2
            scale = float(SD) ** -0.5
            mask4 = lambda v: v[:].unsqueeze(1).to_broadcast([P, 4, P])
            as4 = lambda v: v.rearrange("p (a t) -> p a t", t=P)
            for g in range(G + 1):
                if g < G:
                    eng.wait_ge(S["z_done"], g + 1)
                    if g >= 2:
                        eng.wait_ge(S["pv_done"], g - 1)
                    zg = z_buf[:, g % 2, :]
                    for a in range(2):
                        bias = sb_bias[:, 2 * g + a:2 * g + a + 1]
                        pick = lambda v: v.rearrange("p (s a t) -> p s a t", s=2, a=2)[:, :, a, :]
                        got = pb[2 * (g % 2) + a]
                        eng.tensor_scalar(pick(zg[:, 0:512]), got[:, 0:2 * P].rearrange("p (s t) -> p s t", s=2), scale, bias,
                                          ALU.mult, ALU.add)
                        last = eng.tensor_scalar(zg[:, 512 + a * P:512 + (a + 1) * P],
                                                 got[:, 2 * P:3 * P], scale, bias, ALU.mult, ALU.add)
                    last.then_inc(S["z_ready"], 1)
                if g >= 1:
                    zg = z_buf[:, (g - 1) % 2, :]
                    eng.wait_ge(S["rc_done"], g)
                    eng.tensor_tensor(zg[:, 0:512], zg[:, 0:512], pb[4], ALU.add)
                    eng.tensor_tensor(zg[:, 512:768], zg[:, 512:768], pb[5][:, 0:256], ALU.add).then_inc(S["arg_ready"], 1)
                if g < G:
                    zg, lg = z_buf[:, g % 2, :], l_buf[:, g % 2, :]
                    eng.wait_ge(S["soft_ready"], g + 1)
                    link(eng.scalar_tensor_tensor(lg, zg, 0.0, lg, ALU.max, ALU.add))
                    eng.tensor_tensor(as4(lg[:, 0:512]), as4(lg[:, 0:512]), mask4(not_before), ALU.mult)
                    eng.tensor_scalar(lg[:, 512:768], lg[:, 512:768], -1.0, None, ALU.mult).then_inc(S["l_ready"], 1)
                    link(eng.tensor_tensor(as4(zg[:, 0:512]), as4(zg[:, 0:512]), mask4(before), ALU.mult))
                if g >= 1:
                    zg = z_buf[:, (g - 1) % 2, :]
                    eng.wait_ge(S["p_exp"], g)
                    eng.tensor_tensor(as4(zg[:, 0:512]), as4(zg[:, 0:512]), mask4(before), ALU.mult).then_inc(S["p_ready"], 1)
            rows16 = lambda v: v.rearrange("p a b -> p (a b)").rearrange("p (a b) -> p a b", b=SH)
            eng.scalar_tensor_tensor(rows16(zs), rows16(zs), scale,
                                     sb_bias[:].unsqueeze(1).to_broadcast([P, PAGES * NB, SH]),
                                     ALU.mult, ALU.add).then_inc(S["z_ready"], 1)
            eng.wait_ge(S["soft_ready"], G + 1)
            link(eng.scalar_tensor_tensor(ls, zs, 0.0, ls, ALU.max, ALU.add))
            eng.tensor_scalar(ls, ls, -1.0, None, ALU.mult).then_inc(S["l_ready"], 1)
            eng.wait_ge(S["rcs_done"], 1)
            eng.tensor_tensor(zs, zs, pb[4][:, 0:256].rearrange("p (a b) -> p a b", a=PAGES), ALU.add).then_inc(S["args_s"], 1)
            own = ident[0:SH, 0:SH].unsqueeze(2).to_broadcast([SH, SH, SD])
            for b in range(NB):
                eng.wait_ge(S["opv_done"], b + 1)
                if b >= 1:
                    eng.wait_ge(S["ot_done"], b)
                eng.tensor_tensor(os_row.rearrange("p (h d) -> p h d", h=SH),
                                  psum[0:SH, 0:D].rearrange("p (h d) -> p h d", h=SH), own, ALU.mult).then_inc(S["own_ready"], 1)
            eng.wait_ge(S["ot_done"], NB)
            eng.tensor_copy(os_tok, psum[0:NB, D:2 * D]).then_inc(S["ot_kept"], 1)
            for i in range(8):
                add_block("sb_out", i, GATE[MIX1])

            norm(FFN1)
            eng.wait_ge(S["kv_stored"], 16 * 6)
            eng.wait_ge(S["logits_done"], 1)
            for t in range(TT):
                n = TOK[t]
                lg, tp = logit[0:n, t, :], top[0:n, t, :]
                link(eng.tensor_tensor(lg, pb[4][0:n, t * NE:(t + 1) * NE], router_bias[0:n, :], ALU.add))
                link(eng.max(tp, lg))
                link(eng.max_index(top_i[0:n, t, :], tp, lg))
                eng.tensor_copy(top_f[0:n, t, :], top_i[0:n, t, :])
                link(eng.tensor_tensor(e2[0:n, t:t + 1], tp[:, 1:2], tp[:, 0:1], ALU.subtract))
            eng.nop().then_inc(S["gates_exp"], 1)
            eng.wait_ge(S["gates_exp_done"], 1)
            for t in range(TT):
                n = TOK[t]
                link(eng.tensor_scalar(w1[0:n, t:t + 1], e2[0:n, t:t + 1], 1.0, None, ALU.add))
                link(eng.reciprocal(w1[0:n, t:t + 1], w1[0:n, t:t + 1]))
                link(eng.tensor_tensor(w2[0:n, t:t + 1], e2[0:n, t:t + 1], w1[0:n, t:t + 1], ALU.mult))
                eng.tensor_scalar(hit[0:n, t, :], iota8[0:n, :], top_f[0:n, t, 0:1], w1[0:n, t:t + 1], ALU.is_equal, ALU.mult)
                link(eng.tensor_scalar(gate_tok[0:n, t, :], iota8[0:n, :], top_f[0:n, t, 1:2], w2[0:n, t:t + 1],
                                       ALU.is_equal, ALU.mult))
                last = eng.tensor_tensor(gate_tok[0:n, t, :], gate_tok[0:n, t, :], hit[0:n, t, :], ALU.add)
            last.then_inc(S["gates_ready"], 1)
            eng.wait_ge(S["gbc_kept"], NE)
            with eng.Fori(0, NE // 2) as it:
                for e in range(2):
                    for n in range(FEC):
                        m = FEC * e + n
                        eng.wait_ge(S["pair_done"], it * 56 + (m + 1))
                        eng.tensor_tensor(gated[:, m % 2, :], pb[2 * (m % 2) + 1][:, 0:T], gate_bc[:, 2 * it + e, :],
                                          ALU.mult).then_inc(S["gated_ready"], 1)
                        eng.wait_ge(S["gated_ready"], it * 56 + (m + 1))
                        eng.wait_ge(S["pair_silu"], it * 56 + (m + 1))
                        eng.tensor_tensor(big[:, n, :], silu_m[:, m % 2, :], gated[:, m % 2, :],
                                          ALU.mult).then_inc(S["pair_kept"], 1)
                    for n in range(56):
                        m = 56 * e + n
                        eng.wait_ge(S["down_done"], it * 112 + (m + 1))
                        eng.wait_ge(S["down_kept"], it * 112 + m)
                        add_to_x(pb[n % 4], n % 8, GATE[FFN1], S["down_part"],
                                 it * 112 + (m + 1)).then_inc(S["down_kept"], 1)
            norm(FINAL)


_OUTS = [(1, TP, D), (NB, 1, D), (1, TP, SH, SD), (1, TP, SH, SD), (1, 1, GH, DK, DV), (NB, 1, SH, SD), (NB, 1, SH, SD),
         (1, NB, GH, DK, DV)]


def kernel(**inputs):
    import numpy as _np
    import concourse.bacc as _bacc
    from concourse import mybir as _mybir
    from concourse.bass_utils import run_bass_kernel_spmd as _run

    nc = _bacc.Bacc("TRN2", target_bir_lowering=False, num_devices=1)
    arrays, ins = {}, {}
    for name in inputs:
        a = _np.ascontiguousarray(inputs[name])
        arrays[f"in_{name}"] = a
        ins[name] = nc.dram_tensor(f"in_{name}", a.shape, _mybir.dt.from_np(a.dtype), kind="ExternalInput").ap()
    outs = [nc.dram_tensor(f"out_{i}", s, F32, kind="ExternalOutput").ap() for i, s in enumerate(_OUTS)]
    build(nc, ins, outs)
    r = _run(nc, [arrays], core_ids=[0])
    return tuple(r.results[0][f"out_{i}"] for i in range(len(_OUTS)))
```

```python
from contextlib import ExitStack

import concourse.bass as bass
from concourse import mybir

ALU = mybir.AluOpType
ACT = mybir.ActivationFunctionType
AX = mybir.AxisListType
F32 = mybir.dt.float32
F32R = mybir.dt.float32r
U32 = mybir.dt.uint32
I32 = mybir.dt.int32

P = 128
D = 1024
KC = D // P
TP = 256
NB = 8
T = TP + NB
TT = 3
TOK = [P, P, NB]
NC9 = 1 + NB
LO_ROW = 32
CR = LO_ROW + NC9
GH, DK, DV, C = 4, 128, 256, 64
NCH = TP // C
HALF = C // 2
GR = 16
SH, SD = 16, 64
PAGES = 2
FF, FE, NE = 2816, 3584, 8
FFC, FEC = FF // P, FE // P
EPS = 1e-6
EXP_CAP = 43.0
RING = 3
UNITS = 4
QUART = 1024
AHEAD = UNITS - 1
CAP = 128
TILE = 4096
MIX0, FFN0, KV, MIX1, FFN1, FINAL = range(6)
IN_GLA, IN_GLA_OUT, IN_FFN, IN_KV, IN_Q, IN_SB_OUT = range(6)
SHIFT = {MIX0: 0, FFN0: 24, KV: 96, MIX1: 48, FFN1: 72, FINAL: 112}
SCALE = {MIX0: 8, FFN0: 32, KV: 104, MIX1: 56, FFN1: 80, FINAL: 120}
GAIN = {MIX0: 0, FFN0: 16, KV: 32, MIX1: 8, FFN1: 24, FINAL: 40}
GATE = {MIX0: 16, FFN0: 40, MIX1: 64, FFN1: 88}
GLA_GAIN, GLA_BIAS, VEC_B = 48, 50, 54
N_ADA = 32
STREAM = ([("ada", i) for i in range(N_ADA)] + [("gla_in", i) for i in range(6)] + [("gla_out", i) for i in range(2)]
          + [("ffn_up", i) for i in range(11)] + [("ffn_down", i) for i in range(6)] + [("kv", i) for i in range(4)]
          + [("sb_q", i) for i in range(2)] + [("k_cache", i) for i in range(4)] + [("v_cache", i) for i in range(4)]
          + [("sb_out", i) for i in range(2)])
TILE_AT = {k: n for n, k in enumerate(STREAM)}
BASE = len(STREAM)
PER_E = 21
WORK = 13 * 1024 + 96
SPLIT = [t for t in STREAM if t[0] not in ("k_cache", "v_cache")]
UNIT_AT = {t: 4 * n for n, t in enumerate(SPLIT)}
NU = 4 * len(SPLIT)
BLOCKS = ([("gla_in", i) for i in range(25)] + [("gla_out", i) for i in range(8)] + [("ffn_up", i) for i in range(44)]
          + [("ffn_down", i) for i in range(48)] + [("kv", i) for i in range(16)] + [("sb_q", i) for i in range(8)]
          + [("sb_out", i) for i in range(8)])
BLOCK_AT = {k: n for n, k in enumerate(BLOCKS)}
BY_ACT = ("gla_in", "kv", "sb_q")


def build(nc, A, O, cap=CAP):
    y_prompt, y_sample, k_prompt, v_prompt, gla_prompt, k_sample, v_sample, gla_sample = O
    ctx = ExitStack()
    with ctx:
        def sb(name, shape, dt=F32):
            return ctx.enter_context(nc.sbuf_tensor(name, shape, dt))

        def sem(name):
            return ctx.enter_context(nc.semaphore(name))

        ring = [sb(f"ring{i}", [P, TILE]) for i in range(RING)]
        x = sb("x", [P, KC, T])
        h = sb("h", [P, KC, T])
        w_hi = [sb(f"w_hi{i}", [P, QUART], F32R) for i in range(UNITS)]
        w_lo = [sb(f"w_lo{i}", [P, QUART], F32R) for i in range(UNITS)]
        mod = sb("mod", [P, P, NC9])
        gain = sb("gain", [P, 6, KC, NC9])
        vec_a = sb("vec_a", [P, P])
        vec_b = sb("vec_b", [P, VEC_B])
        rstd = sb("rstd", [P, T])
        ea = sb("ea", [P, GH, NB])
        top_i = sb("top_i", [P, TT, 8], U32)
        most = sb("most", [P, 1], I32)
        wr = sb("wr", [P, KC, GR])
        w_router = sb("w_router", [P, KC, NE])
        sb_bias = sb("sb_bias", [P, SH])
        router_bias = sb("router_bias", [P, NE])
        ident = sb("ident", [P, P])
        ones = sb("ones", [P, P])
        after = sb("after", [P, P])
        before = sb("before", [P, P])
        not_before = sb("not_before", [P, P])
        upto = sb("upto", [C, C])
        sel_to = sb("sel_to", [SH, NB, NB])
        iota = sb("iota", [P, P])
        tmp8 = sb("tmp8", [P, KC, NB])
        psum = ctx.enter_context(nc.psum_tensor("psum", [P, 8 * 512], F32))
        pb = [psum[:, i * 512:(i + 1) * 512] for i in range(8)]

        stages = ctx.enter_context(ExitStack())

        def st_sb(stage, name, shape, dt=F32):
            return stage.enter_context(nc.sbuf_tensor(name, shape, dt))

        hh = st_sb(stages, "hh", [P, KC, T], F32R)
        hl = st_sb(stages, "hl", [P, KC, T], F32R)

        stage = ExitStack()
        big = st_sb(stage, "big", [P, 24, T])
        work = st_sb(stage, "work", [P, WORK])
        stage.close()

        def piece(at, shape, work=work):
            n = 1
            for s in shape[1:]:
                n *= s
            v = work[0:shape[0], at:at + n]
            if len(shape) == 3:
                v = v.rearrange("p (a b) -> p a b", a=shape[1])
            if len(shape) == 4:
                v = v.rearrange("p (a b c) -> p a b c", a=shape[1], b=shape[2])
            return v, at + n

        crow, at = piece(0, [NC9, D])
        csilu, at = piece(at, [NC9, D])
        ada_row, at = piece(at, [CR, 2, 512])
        at = 0
        la, at = piece(at, [P, GH, T])
        orstd = la
        t_abs, at = piece(at, [P, GH, T])
        cum_a, _ = piece(GH * T, [P, 32, HALF])
        ke, _ = piece(GH * T, [P, GH, TP])
        cum, at = piece(at, [P, 32, HALF])
        s0 = [piece(at, [P, GH, DV])[0], piece(at + 1024, [P, GH, DV])[0]]
        qd, at = piece(at, [P, 32, HALF])
        kd, at = piece(at, [P, 32, HALF])
        qo, at = piece(at, [P, 16, HALF])
        ko, at = piece(at, [P, 16, HALF])
        qe, at = piece(at, [P, GH, TP])
        dec, at = piece(at, [P, 16])
        w_gate2, _ = piece(at, [GR, GH * DK])
        vs_tok, _ = piece(at, [NB, D])
        st, at = piece(at, [C, 16, C])
        rT, _ = piece(at, [GR, T])
        vtok = []
        for i in range(2):
            v, at = piece(at, [C, D])
            vtok.append(v)
        ktok, at = piece(at, [C, 2 * GH * DK])
        state = []
        for i in range(2):
            v, at = piece(at, [P, GH, DV])
            state.append(v)
        assert at <= WORK, at
        stage = ExitStack()
        st_sb(stage, "skip", [P, 24 * T + WORK - KC * P])
        c_split = st_sb(stage, "c_split", [P, KC, P], F32R)
        stage.close()
        xtok = big[:, :, :].rearrange("p a b -> p (a b)")[:, 0:TT * D].rearrange("p (t d) -> p t d", t=TT)

        stage = ExitStack()
        act_hi = st_sb(stage, "act_hi", [P, FFC, T], F32R)
        act_lo = st_sb(stage, "act_lo", [P, FFC, T], F32R)
        silu_a = st_sb(stage, "silu_a", [P, 2, T])
        act32 = st_sb(stage, "act32", [P, 2, T])
        stage.close()

        stage = ExitStack()
        kvq = st_sb(stage, "kvq", [P, 24, T])
        work3 = st_sb(stage, "work3", [P, WORK])
        stage.close()
        kvtok, at = piece(0, [P, TT, 2 * D], work3)
        z_buf, at = piece(at, [P, 2, 768], work3)
        l_buf, at = piece(at, [P, 2, 768], work3)
        zs, at = piece(at, [P, PAGES, NB * SH], work3)
        ls, at = piece(at, [P, PAGES, NB * SH], work3)
        prod, _ = piece(at, [P, D], work3)
        os_row, at = piece(at, [SH, D], work3)
        qs_tok, at = piece(at, [NB, D], work3)
        os_tok = qs_tok
        assert at <= WORK, at
        stages.close()

        stage = ExitStack()
        gate_tok = st_sb(stage, "gate_tok", [P, TT, NE])
        chosen = st_sb(stage, "chosen", [P, TT, NE])
        pos = st_sb(stage, "pos", [P, TT, NE])
        logit = st_sb(stage, "logit", [P, TT, NE])
        top = st_sb(stage, "top", [P, TT, 8])
        hit = st_sb(stage, "hit", [P, TT, NE])
        top_f = st_sb(stage, "top_f", [P, TT, 8])
        e2 = st_sb(stage, "e2", [P, 8])
        w1 = st_sb(stage, "w1", [P, 8])
        w2 = st_sb(stage, "w2", [P, 8])
        gathered = ExitStack()
        tok_hi = st_sb(gathered, "tok_hi", [P, TT, D], F32R)
        tok_lo = st_sb(gathered, "tok_lo", [P, TT, D], F32R)
        pick = st_sb(gathered, "pick", [P, NE + 1, TT, CAP], F32R)
        put = st_sb(gathered, "put", [CAP, NE, T])
        xe_hi = st_sb(gathered, "xe_hi", [P, KC, CAP], F32R)
        xe_lo = st_sb(gathered, "xe_lo", [P, KC, CAP], F32R)
        at_hi = st_sb(gathered, "at_hi", [P, FEC, CAP], F32R)
        at_lo = st_sb(gathered, "at_lo", [P, FEC, CAP], F32R)
        silu_e = st_sb(gathered, "silu_e", [CAP, 512])
        act_e = st_sb(gathered, "act_e", [CAP, 512])
        y_e = st_sb(gathered, "y_e", [CAP, D])
        put_tok = y_e[:, 0:2 * TT * CAP].rearrange("p (s t c) -> p s t c", s=2, t=TT)
        gathered.close()
        gate_bc = st_sb(stage, "gate_bc", [P, NE, T])
        gateT = st_sb(stage, "gateT", [NE, T])
        silu_m = st_sb(stage, "silu_m", [P, 2, T])
        gated = st_sb(stage, "gated", [P, 2, T])
        act_m = st_sb(stage, "act_m", [P, FEC, T])
        stage.close()
        stage = ExitStack()
        ytok = st_sb(stage, "ytok", [P, TT, D])
        stage.close()

        def sel(b):
            return ident[0:NB, b:b + 1].to_broadcast([NB, P])

        S = {}

        def named(*names):
            for n in names:
                S[n] = sem(n)

        named("consts", "c_zero", "small_loaded", "x_loaded", "vec_turned", "vec_kept", "c_silu", "c_turned", "c_hi", "c_kept",
              "x_turned", "x_kept", "hi_ready", "lo_ready", "unit_used", "ada_copied", "ada_turned", "ada_part",
              "ada_kept", "gains_ready", "squared", "ss_done", "ms_ready", "root_ready", "scaled", "h_ready", "hs_ready",
              "hh_ready", "hl_ready", "kept_act", "kept_dve", "silu_done", "act_step", "dve_step", "part_added",
              "r_done", "gate_done", "log_sig", "args_ready", "exps_ready", "decayed", "scores_done", "scores_kept",
              "v_turned", "v_kept", "o_done", "o_kept", "u_done", "state_ready", "vs_turned", "vs_kept", "vbc_done",
              "s_updated", "s0_loaded0", "s0_loaded1", "s0_stored0", "s0_stored1", "os_done", "os_kept", "osq_ready",
              "oss_done", "oms_ready", "oroot_ready", "o_ready", "state_stored", "act_ready", "act_hi_ready", "kv_turned",
              "kv_kept", "kv_stored", "qs_turned", "qs_kept", "qbc_done", "z_s_ready", "z_done", "z_ready", "soft_ready",
              "l_ready", "rc_done", "arg_ready", "p_exp", "p_ready", "pv_done", "pv_kept", "rcs_done", "args_s",
              "exps_s", "opv_done", "own_ready", "ot_done", "ot_kept", "otT_done", "otT_kept", "logits_done",
              "gates_exp", "gates_exp_done", "gates_ready", "count_done", "most_ready", "htok_turned", "htok_hi",
              "htok_lo", "pick_ready", "put_ready", "put_turned", "put_kept", "gather_done", "xe_hi_ready",
              "xe_lo_ready", "gate_up_kept", "e_silu", "turned", "at_hi_ready", "at_lo_ready", "y_e_kept",
              "scattered", "added", "down_part", "gateT_done", "gateT_kept", "gbc_done", "gbc_kept", "gate_half_done",
              "pair_done", "pair_silu", "pair_kept", "gated_ready", "down_done", "down_kept", "experts_done",
              "y_turned", "y_kept", "y_stored")
        loaded = [sem(f"ring_loaded{i}") for i in range(RING)]

        lands, count = [], [0] * RING
        for n, (kind, i) in enumerate(STREAM):
            count[n % RING] += 64 if kind in ("k_cache", "v_cache") else 32 if kind == "ffn_up" else 16
            lands.append(count[n % RING])
        LAND0 = list(count)

        def read_out(kind, i):
            if kind == "k_cache":
                return S["z_s_ready"], 2 * i + 2
            if kind == "v_cache":
                return S["opv_done"], 2 * i + 2
            return S["lo_ready"], UNIT_AT[kind, i] + 4

        def quarter(raw, kind, j, ks=4):
            if kind in ("ada", "up"):
                return raw[:].rearrange("p (k c) -> p k c", c=512)[:, 2 * j:2 * j + 2, :]
            if kind == "down":
                return raw[:, j * D:(j + 1) * D].unsqueeze(1)
            if kind == "ffn_up":
                return raw[:].rearrange("p (k s c) -> p k s c", k=KC, s=2)[:, :, j % 2, j // 2 * P:(j // 2 + 1) * P]
            if kind == "ffn_down":
                return raw[:, 0:ks * D].rearrange("p (k c) -> p k c", k=ks)[:, :, j * 256:(j + 1) * 256]
            return raw[:].rearrange("p (k c) -> p k c", k=KC)[:, :, j * P:(j + 1) * P]

        def unit(v, kind, n, ks=4):
            k, c = {"ada": (2, 512), "up": (2, 512), "down": (1, D), "ffn_down": (ks, 256)}.get(kind, (KC, P))
            return v[n % UNITS][:, 0:k * c].rearrange("p (k c) -> p k c", k=k)

        def chunks_of(kind, i):
            return min(4, FFC - 4 * i) if kind == "ffn_down" else 4

        empt, a_n, d_n = [], 0, 0
        for kind, i in BLOCKS:
            if kind in BY_ACT:
                a_n += 1
                empt.append(("kept_act", a_n))
            elif kind == "ffn_up":
                d_n += i % 2
                empt.append(("kept_dve", d_n + 1 - i % 2))
            else:
                d_n += 1
                empt.append(("kept_dve", d_n))

        block = ctx.enter_context(nc.Block())

        def slot(kind, i):
            return ring[TILE_AT[kind, i] % RING]

        def landed(eng, kind, i):
            n = TILE_AT[kind, i]
            eng.wait_ge(loaded[n % RING], lands[n])

        def expert_landed(eng, it, j):
            n = (BASE + j) % RING
            eng.wait_ge(loaded[n], it * (PER_E // RING * 16) + (LAND0[n] + 16 * (j // RING + 1)))

        def cols8(tile, n=512):
            return tile[:, 0:KC * n].rearrange("p (k c) -> p k c", k=KC)

        def rows(w, lo, n, c0=0, c1=D):
            return w[lo:lo + n * P, c0:c1].rearrange("(k p) c -> p k c", p=P)

        @block.sync
        def _(eng):
            for w, lo in ((A["ada_b"].rearrange("l (c p) -> (l c) p", p=P), 0),
                          (A["kv_ada_b"].rearrange("(c p) -> c p", p=P), 96),
                          (A["final_ada_b"].rearrange("(c p) -> c p", p=P), 112)):
                eng.dma_start(h[lo:lo + w.shape[0], 0, 0:P], w).then_inc(S["small_loaded"], 16)
            for w, lo in ((A["norm_mix"].rearrange("l (c p) -> (l c) p", p=P), 0),
                          (A["norm_ffn"].rearrange("l (c p) -> (l c) p", p=P), 16),
                          (A["kv_norm"].rearrange("(c p) -> c p", p=P), 32),
                          (A["final_norm"].rearrange("(c p) -> c p", p=P), 40),
                          (A["gla_norm"].rearrange("l (c p) -> (l c) p", p=P), GLA_GAIN),
                          (A["gla_b_gate"].rearrange("l (c p) -> (l c) p", p=P), GLA_BIAS)):
                eng.dma_start(h[lo:lo + w.shape[0], 1, 0:P], w).then_inc(S["small_loaded"], 16)
            eng.dma_start(crow[0:1, :], A["c_prompt"]).then_inc(S["small_loaded"], 16)
            eng.dma_start(crow[1:NC9, :], A["c_sample"]).then_inc(S["small_loaded"], 16)
            eng.dma_start(wr[:], rows(A["gla_w_in"][0], 0, KC, 3072, 3088)).then_inc(S["small_loaded"], 16)
            eng.dma_start(w_router[:], rows(A["moe_w_router"][0], 0, KC, 0, NE)).then_inc(S["small_loaded"], 16)
            eng.dma_start(w_gate2, A["gla_w_gate2"][0]).then_inc(S["small_loaded"], 16)
            eng.dma_start(sb_bias[:], A["sb_b"][0].partition_broadcast(P)).then_inc(S["small_loaded"], 16)
            eng.dma_start(router_bias[:], A["moe_b_router"][0].partition_broadcast(P)).then_inc(S["small_loaded"], 16)
            for t in range(2):
                eng.dma_start(xtok[:, t, :], A["x_prompt"][0, t * P:(t + 1) * P, :]).then_inc(S["x_loaded"], 16)
            eng.dma_start(xtok[0:NB, 2, :], A["x_sample"].rearrange("b s d -> (b s) d")).then_inc(S["x_loaded"], 16)

            for n, (kind, i) in enumerate(STREAM):
                dst = ring[n % RING]
                if n >= RING:
                    eng.wait_ge(*read_out(*STREAM[n - RING]))
                if kind in ("k_cache", "v_cache"):
                    cache = A["cache_k" if kind == "k_cache" else "cache_v"].rearrange("n s h d -> n s (h d)")
                    for j in range(4):
                        b, page = 2 * i + j // 2, j % 2
                        at_page = eng.value_load(A["page_table"][b:b + 1, page:page + 1], min_val=0,
                                                 max_val=A["cache_k"].shape[0] - 1)
                        eng.dma_start(dst[:, j * D:(j + 1) * D], cache[at_page]).then_inc(loaded[n % RING], 16)
                    continue
                c = i * 512
                if kind == "ada":
                    w, c = ((A["ada_w"][i // 12], (i % 12) * 512) if i < 24 else
                            (A["kv_ada_w"], (i - 24) * 512) if i < 28 else (A["final_ada_w"], (i - 28) * 512))
                    eng.dma_start(cols8(dst), rows(w, 0, KC, c, c + 512)).then_inc(loaded[n % RING], 16)
                elif kind == "ffn_up":
                    w = A["ffn_w_gate_up"][0].rearrange("(k p) (s c) -> p k s c", p=P, s=2)[:, :, :, i * 256:(i + 1) * 256]
                    d4 = dst[:].rearrange("p (k s c) -> p k s c", k=KC, s=2)
                    for s in range(2):
                        eng.dma_start(d4[:, :, s, :], w[:, :, s, :]).then_inc(loaded[n % RING], 16)
                elif kind == "ffn_down":
                    k = min(4, FFC - 4 * i)
                    eng.dma_start(dst[:, 0:k * D].rearrange("p (k c) -> p k c", k=k),
                                  rows(A["ffn_w_down"][0], i * 512, k)).then_inc(loaded[n % RING], 16)
                else:
                    w = {"gla_in": A["gla_w_in"][0], "gla_out": A["gla_w_out"][0], "kv": A["kv_w"],
                         "sb_q": A["sb_w_q"][0], "sb_out": A["sb_w_out"][0]}[kind]
                    eng.dma_start(cols8(dst), rows(w, 0, KC, c, c + 512)).then_inc(loaded[n % RING], 16)

            up, down = A["moe_w_gate_up"][0], A["moe_w_down"][0]

            def load(j, it):
                e, i = j // PER_E, j % PER_E
                dst = ring[(BASE + j) % RING]
                expert = it + e
                if i < 14:
                    c = (i % 2) * FE + (i // 2) * 512
                    src, to = up[expert, :, c:c + 512].rearrange("(k p) c -> p k c", p=P), cols8(dst)
                else:
                    lo = (i - 14) * 512
                    src = down[expert, lo:lo + 512, :].rearrange("(k p) c -> p k c", p=P)
                    to = dst[:].rearrange("p (k c) -> p k c", k=4)
                return to, src

            for j in range(RING):
                eng.wait_ge(*read_out(*STREAM[BASE - RING + j]))
                to, src = load(j, 0)
                eng.dma_start(to, src).then_inc(loaded[(BASE + j) % RING], 16)
            with eng.Fori(0, NE - 1) as it:
                for j in range(RING, PER_E + RING):
                    to, src = load(j, it)
                    value = eng.snap(it * (4 * PER_E) + (NU + 4 * (j - RING) + 4))
                    eng.wait_ge(S["lo_ready"], value)
                    eng.dma_start(to, src).then_inc(loaded[(BASE + j) % RING], 16)
            for j in range(RING, PER_E):
                to, src = load(j, NE - 1)
                eng.wait_ge(S["lo_ready"], (NE - 1) * 4 * PER_E + NU + 4 * (j - RING) + 4)
                eng.dma_start(to, src).then_inc(loaded[(BASE + j) % RING], 16)

        @block.gpsimd
        def _(eng):
            eng.memset(ones[:], 1.0).then_inc(S["consts"], 1)
            eng.memset(ident[:], 0.0).then_inc(S["consts"], 1)
            eng.memset(sel_to[:], 0.0).then_inc(S["consts"], 1)
            eng.memset(not_before[:], -1.0).then_inc(S["consts"], 1)
            eng.wait_ge(S["consts"], 4)
            eng.affine_select(out=ident[:], in_=ident[:], compare_op=ALU.not_equal, fill=1.0, base=0,
                              pattern=[[-1, P]], channel_multiplier=1).then_inc(S["consts"], 1)
            eng.affine_select(out=after[:], in_=ones[:], compare_op=ALU.is_ge, fill=0.0, base=0,
                              pattern=[[-1, P]], channel_multiplier=1).then_inc(S["consts"], 1)
            eng.affine_select(out=before[:], in_=ones[:], compare_op=ALU.is_gt, fill=0.0, base=0,
                              pattern=[[1, P]], channel_multiplier=-1).then_inc(S["consts"], 1)
            eng.affine_select(out=not_before[:], in_=not_before[:], compare_op=ALU.is_gt, fill=0.0, base=0,
                              pattern=[[1, P]], channel_multiplier=-1).then_inc(S["consts"], 1)
            eng.affine_select(out=upto[:], in_=ones[0:C, 0:C], compare_op=ALU.is_ge, fill=0.0, base=0,
                              pattern=[[1, C]], channel_multiplier=-1).then_inc(S["consts"], 1)
            eng.affine_select(out=sel_to[:], in_=sel_to[:], compare_op=ALU.not_equal, fill=1.0, base=0,
                              pattern=[[-1, NB], [1, NB]], channel_multiplier=0).then_inc(S["consts"], 1)
            eng.iota(iota[:], pattern=[[1, P]], base=0, channel_multiplier=0,
                     allow_small_or_imprecise_dtypes=True).then_inc(S["consts"], 1)
            src = A["state_gla"][0].rearrange("b h k v -> b k h v")
            dst = gla_sample[0].rearrange("b h k v -> b k h v")
            eng.wait_ge(S["scores_done"], 1)
            for b in range(NB + 1):
                if b < NB:
                    if b >= 2:
                        eng.wait_ge(S[f"s0_stored{b % 2}"], 16 * (b // 2))
                        eng.wait_ge(S["os_done"], b - 1)
                    eng.dma_start(s0[b % 2], src[b]).then_inc(S[f"s0_loaded{b % 2}"], 16)
                if b >= 1:
                    eng.wait_ge(S["s_updated"], b)
                    eng.dma_start(dst[b - 1], s0[(b - 1) % 2]).then_inc(S[f"s0_stored{(b - 1) % 2}"], 16)
            eng.wait_ge(S["state_ready"], NCH)
            eng.dma_start(gla_prompt[0, 0].rearrange("h k v -> k h v"), state[(NCH - 1) % 2]).then_inc(S["state_stored"], 16)
            eng.wait_ge(S["kv_kept"], 12)
            for t, outs in ((0, (k_prompt, v_prompt)), (1, (k_prompt, v_prompt)), (2, (k_sample, v_sample))):
                for s, o in enumerate(outs):
                    flat = o.rearrange("b s h d -> (b s) (h d)")
                    lo = t * P if t < 2 else 0
                    eng.dma_start(flat[lo:lo + TOK[t], :],
                                  kvtok[0:TOK[t], t, s * D:(s + 1) * D]).then_inc(S["kv_stored"], 16)
            for t in range(TT):
                eng.wait_ge(S["y_kept"], 2 * t + 2)
                dst_y = (y_prompt[0, t * P:(t + 1) * P, :] if t < 2 else y_sample.rearrange("b s d -> (b s) d"))
                eng.dma_start(dst_y, ytok[0:TOK[t], t, :]).then_inc(S["y_stored"], 16)
            eng.wait_ge(S["s0_stored0"], 16 * NB // 2)
            eng.wait_ge(S["s0_stored1"], 16 * NB // 2)
            eng.wait_ge(S["state_stored"], 16)
            eng.wait_ge(S["kv_stored"], 16 * 6)
            eng.wait_ge(S["y_stored"], 16 * TT)

        @block.tensor
        def _(eng):
            eng.wait_ge(S["consts"], 11)
            eng.wait_ge(S["small_loaded"], 16 * 16)
            eng.transpose(pb[4][:, 0:P], h[:, 0, 0:P], ident[:])
            eng.transpose(pb[4][:, P:P + VEC_B], h[0:VEC_B, 1, 0:P], ident[0:VEC_B, 0:VEC_B]).then_inc(S["vec_turned"], 1)
            eng.wait_ge(S["c_silu"], 1)
            for k in range(KC):
                last = eng.transpose(pb[5][:, k * 16:k * 16 + NC9], csilu[:, k * P:(k + 1) * P], ident[0:NC9, 0:NC9])
            last.then_inc(S["c_turned"], 1)
            eng.wait_ge(S["x_loaded"], 16 * TT)
            for k in range(KC):
                if k >= 2:
                    eng.wait_ge(S["x_kept"], k - 1)
                for t in range(TT):
                    n = TOK[t]
                    last = eng.transpose(pb[6 + k % 2][:, t * P:t * P + n], xtok[0:n, t, k * P:(k + 1) * P], ident[0:n, 0:n])
                last.then_inc(S["x_turned"], 1)

            def ada_turn(i):
                eng.wait_ge(S["ada_copied"], i + 1)
                if i >= 2:
                    eng.wait_ge(S["ada_kept"], i - 1)
                for j in range(4):
                    last = eng.transpose(pb[2 + i % 2][:, j * 64:j * 64 + CR], ada_row[:, i % 2, j * P:(j + 1) * P],
                                         ident[0:CR, 0:CR])
                last.then_inc(S["ada_turned"], 1)

            def has_unit(n):
                eng.wait_ge(S["lo_ready"], n + 1)

            eng.wait_ge(S["c_kept"], 1)
            for i in range(N_ADA):
                if i >= 2:
                    eng.wait_ge(S["ada_copied"], i - 1)
                for j in range(4):
                    n = UNIT_AT["ada", i] + j
                    has_unit(n)
                    for k in range(2):
                        eng.matmul(pb[i % 2], c_split[:, 2 * j + k, :], unit(w_hi, "ada", n)[:, k, :],
                                   start=j + k == 0, stop=False)
                        last = eng.matmul(pb[i % 2], c_split[:, 2 * j + k, :], unit(w_lo, "ada", n)[:, k, :],
                                          start=False, stop=j + k == 4)
                    last.then_inc(S["unit_used"], 1)
                if i >= 1:
                    ada_turn(i - 1)
            ada_turn(N_ADA - 1)

            def sum_squares(m):
                for k in range(KC):
                    eng.wait_ge(S["squared"], m * KC + k + 1)
                    last = eng.matmul(pb[7][:, 0:T], ones[:], h[:, k, :], start=k == 0, stop=k == KC - 1)
                last.then_inc(S["ss_done"], 1)

            def free_bank(n):
                if n >= 4:
                    who, value = empt[n - 4]
                    eng.wait_ge(S[who], value)

            def three(to, wh, wl, ah, al, start, stop):
                eng.matmul(to, wh, ah, start=start, stop=False)
                eng.matmul(to, wh, al, start=False, stop=False)
                return eng.matmul(to, wl, ah, start=False, stop=stop)

            def project(kind, n_tiles, m):
                for i in range(n_tiles):
                    for j in range(4):
                        n, u = BLOCK_AT[kind, 4 * i + j], UNIT_AT[kind, i] + j
                        has_unit(u)
                        free_bank(n)
                        wh, wl = unit(w_hi, kind, u), unit(w_lo, kind, u)
                        for k in range(KC):
                            if i == 0 and j == 0:
                                eng.wait_ge(S["hl_ready"], m * KC + k + 1)
                            last = three(pb[n % 4][:, 0:T], wh[:, k, :], wl[:, k, :], hh[:, k, :], hl[:, k, :],
                                         k == 0, k == KC - 1)
                        last.then_inc(S["unit_used"], 1)

            def h_is_ready(m):
                eng.wait_ge(S["h_ready"], m * KC + KC)
                eng.wait_ge(S["hs_ready"], m + 1)

            sum_squares(MIX0)
            project("gla_in", 6, IN_GLA)
            n = BLOCK_AT["gla_in", 24]
            free_bank(n)
            for k in range(KC):
                last = eng.matmul(pb[n % 4][0:GR, 0:T], wr[:, k, :], h[:, k, :], start=k == 0, stop=k == KC - 1)
            last.then_inc(S["r_done"], 1)
            eng.wait_ge(S["kept_act"], 25)
            for g in range(GH):
                last = eng.matmul(pb[4 + g][:, 0:T], w_gate2[:, g * DK:(g + 1) * DK], rT[:], start=True, stop=True)
            last.then_inc(S["gate_done"], 1)
            eng.wait_ge(S["decayed"], 4)
            for c in range(NCH):
                for g in range(GH):
                    u, v = g * NCH + c, c * GH + g
                    to = pb[4 + v // 8][:, (v % 8) * C:(v % 8 + 1) * C]
                    for a in range(2):
                        eng.matmul(to[a * HALF:(a + 1) * HALF, a * HALF:(a + 1) * HALF], kd[:, 2 * u + a, :],
                                   qd[:, 2 * u + a, :], start=True, stop=True)
                    last = eng.matmul(to[0:HALF, HALF:C], ko[:, u, :], qo[:, u, :], start=True, stop=True)
            last.then_inc(S["scores_done"], 1)
            eng.wait_ge(S["decayed"], 6)
            for c in range(NCH):
                if c >= 1:
                    eng.wait_ge(S["v_kept"], 2 * c)
                for j in range(8):
                    eng.transpose(pb[j // 4][0:C, (j % 4) * P:(j % 4 + 1) * P], big[:, 8 + j, c * C:(c + 1) * C], ident[:])
                for g in range(GH):
                    last = eng.transpose(pb[2][0:C, g * DK:(g + 1) * DK], ke[:, g, c * C:(c + 1) * C], ident[:])
                last.then_inc(S["v_turned"], 1)
                eng.wait_ge(S["v_kept"], 2 * c + 2)
                if c == 0:
                    eng.wait_ge(S["scores_kept"], 1)
                if c >= 1:
                    eng.wait_ge(S["o_kept"], c)
                    eng.wait_ge(S["state_ready"], c)
                for g in range(GH):
                    for a in range(2):
                        to = pb[3][:, (2 * g + a) * C:(2 * g + a + 1) * C]
                        last = eng.matmul(to, vtok[c % 2][:, g * DV + a * P:g * DV + (a + 1) * P], st[:, c * GH + g, :],
                                          start=True, stop=c == 0)
                        if c > 0:
                            last = eng.matmul(to, state[(c - 1) % 2][:, g, a * P:(a + 1) * P], qe[:, g, c * C:(c + 1) * C],
                                              start=False, stop=True)
                last.then_inc(S["o_done"], 1)
                for g in range(GH):
                    last = eng.matmul(pb[6 + g // 2][:, (g % 2) * DV:(g % 2 + 1) * DV],
                                      ktok[:, (c % 2) * 512 + g * DK:(c % 2) * 512 + (g + 1) * DK],
                                      vtok[c % 2][:, g * DV:(g + 1) * DV], start=True, stop=True)
                last.then_inc(S["u_done"], 1)
            eng.wait_ge(S["v_kept"], 2 * NCH)
            for j in range(8):
                last = eng.transpose(pb[j // 4][0:NB, (j % 4) * P:(j % 4 + 1) * P], big[:, 8 + j, TP:T], ident[:])
            last.then_inc(S["vs_turned"], 1)
            eng.wait_ge(S["vs_kept"], 1)
            eng.wait_ge(S["state_ready"], NCH)
            eng.wait_ge(S["o_kept"], NCH)
            for b in range(NB + 1):
                if b < NB:
                    if b >= 2:
                        eng.wait_ge(S["s_updated"], b - 1)
                    for a in range(2):
                        last = eng.matmul(pb[4 + 2 * (b % 2) + a], sel(b), vs_tok[:, a * 512:(a + 1) * 512],
                                          start=True, stop=True)
                    last.then_inc(S["vbc_done"], 1)
                if b >= 1:
                    eng.wait_ge(S["s_updated"], b)
                    for g in range(GH):
                        for a in range(2):
                            at8 = (2 * g + a) * NB + b - 1
                            last = eng.matmul(pb[3][:, at8:at8 + 1], s0[(b - 1) % 2][:, g, a * P:(a + 1) * P],
                                              big[:, g, TP + b - 1:TP + b], start=True, stop=True)
                    last.then_inc(S["os_done"], 1)
            for g in range(GH):
                eng.wait_ge(S["osq_ready"], g + 1)
                for a in range(2):
                    last = eng.matmul(pb[4 + g][:, 0:T], ones[:], big[:, 2 * g + a, :], start=a == 0, stop=a == 1)
            last.then_inc(S["oss_done"], 1)
            project("gla_out", 2, IN_GLA_OUT)

            sum_squares(FFN0)
            project("ffn_up", 11, IN_FFN)
            for i in range(6):
                ks = chunks_of("ffn_down", i)
                if i == 0:
                    eng.wait_ge(S["act_ready"], FFC)
                for j in range(8):
                    n, u = BLOCK_AT["ffn_down", 8 * i + j], UNIT_AT["ffn_down", i] + j // 2
                    if j % 2 == 0:
                        has_unit(u)
                        wh, wl = unit(w_hi, "ffn_down", u, ks), unit(w_lo, "ffn_down", u, ks)
                    free_bank(n)
                    c = j % 2 * P
                    for k in range(ks):
                        last = three(pb[n % 4][:, 0:T], wh[:, k, c:c + P], wl[:, k, c:c + P], act_hi[:, 4 * i + k, :],
                                     act_lo[:, 4 * i + k, :], k == 0, k == ks - 1)
                    if j % 2 == 1:
                        last.then_inc(S["unit_used"], 1)

            sum_squares(KV)
            project("kv", 4, IN_KV)
            for t in range(TT):
                n = TOK[t]
                for q in range(4):
                    i = 4 * t + q
                    if i == 0:
                        eng.wait_ge(S["kept_act"], empt[BLOCK_AT["kv", 15]][1])
                    if i >= 2:
                        eng.wait_ge(S["kv_kept"], i - 1)
                    for j in range(4):
                        last = eng.transpose(pb[4 + i % 2][0:n, j * P:(j + 1) * P], kvq[:, 4 * q + j, t * P:t * P + n], ident[:])
                    last.then_inc(S["kv_turned"], 1)
            sum_squares(MIX1)
            project("sb_q", 2, IN_Q)
            eng.wait_ge(S["kept_act"], empt[BLOCK_AT["sb_q", 7]][1])
            for j in range(8):
                last = eng.transpose(pb[4 + j // 4][0:NB, (j % 4) * P:(j % 4 + 1) * P], kvq[:, 16 + j, TP:T], ident[:])
            last.then_inc(S["qs_turned"], 1)
            eng.wait_ge(S["qs_kept"], 1)
            for b in range(NB):
                if b >= 2:
                    eng.wait_ge(S["z_s_ready"], b - 1)
                for a in range(2):
                    last = eng.matmul(pb[4 + 2 * (b % 2) + a], sel(b), qs_tok[:, a * 512:(a + 1) * 512],
                                      start=True, stop=True)
                last.then_inc(S["qbc_done"], 1)

            def z_products(g):
                if g >= 2:
                    eng.wait_ge(S["z_ready"], g - 1)
                for a in range(2):
                    to = pb[2 * (g % 2) + a]
                    k, q = kvq[a * SD:(a + 1) * SD, g, 0:TP], kvq[a * SD:(a + 1) * SD, 16 + g, 0:TP]
                    eng.matmul(to[:, 0:P], k[:, 0:P], q[:, 0:P], start=True, stop=True)
                    eng.matmul(to[:, P:2 * P], k[:, P:TP], q[:, P:TP], start=True, stop=True)
                    last = eng.matmul(to[:, 2 * P:3 * P], k[:, 0:P], q[:, P:TP], start=True, stop=True)
                last.then_inc(S["z_done"], 1)

            def later_sums(g):
                eng.wait_ge(S["l_ready"], g + 1)
                if g >= 1:
                    eng.wait_ge(S["arg_ready"], g)
                lg = l_buf[:, g % 2, :]
                eng.matmul(pb[4], after[:], lg[:, 0:512], start=True, stop=True)
                eng.matmul(pb[5][:, 0:256], after[:], lg[:, 512:768], start=True, stop=False)
                eng.matmul(pb[5][:, 0:256], ones[:], lg[:, 256:512], start=False, stop=True).then_inc(S["rc_done"], 1)

            def values(g):
                eng.wait_ge(S["p_ready"], g + 1)
                if g >= 2:
                    eng.wait_ge(S["pv_kept"], g - 1)
                pg = z_buf[:, g % 2, :]
                for a in range(2):
                    lo = D + (2 * g + a) * SD
                    to = pb[6 + g % 2][a * SD:(a + 1) * SD, :]
                    eng.matmul(to[:, 0:P], kvtok[:, 0, lo:lo + SD], pg[:, a * P:(a + 1) * P], start=True, stop=True)
                    eng.matmul(to[:, P:TP], kvtok[:, 0, lo:lo + SD], pg[:, 512 + a * P:512 + (a + 1) * P],
                               start=True, stop=False)
                    last = eng.matmul(to[:, P:TP], kvtok[:, 1, lo:lo + SD], pg[:, 256 + a * P:256 + (a + 1) * P],
                                      start=False, stop=True)
                last.then_inc(S["pv_done"], 1)

            eng.wait_ge(S["kv_kept"], 12)
            eng.wait_ge(S["z_s_ready"], NB)
            G = SH // 2
            for g in range(G + 2):
                if g < G:
                    z_products(g)
                if 1 <= g <= G:
                    later_sums(g - 1)
                if g >= 2:
                    values(g - 2)
            eng.wait_ge(S["l_ready"], G + 1)
            eng.wait_ge(S["arg_ready"], G)
            eng.matmul(pb[4][:, 0:128], after[:], ls[:, 0, :], start=True, stop=False, skip_group_check=True)
            eng.matmul(pb[4][:, 0:128], ones[:], ls[:, 1, :], start=False, stop=True, skip_group_check=True)
            eng.matmul(pb[4][:, 128:256], after[:], ls[:, 1, :], start=True, stop=True).then_inc(S["rcs_done"], 1)
            eng.wait_ge(S["exps_s"], 1)
            eng.wait_ge(S["z_ready"], G)
            for b in range(NB + 1):
                if b < NB:
                    if b % 2 == 0:
                        landed(eng, "v_cache", b // 2)
                    if b >= 1:
                        eng.wait_ge(S["own_ready"], b)
                    vt = slot("v_cache", b // 2)
                    for a in range(2):
                        for page in range(PAGES):
                            lo = ((b % 2) * 2 + page) * D + a * 512
                            last = eng.matmul(pb[a][0:SH, :], zs[:, page, b * SH:(b + 1) * SH], vt[:, lo:lo + 512],
                                              start=page == 0, stop=page == 1)
                    last.then_inc(S["opv_done"], 1)
                if b >= 1:
                    eng.wait_ge(S["own_ready"], b)
                    for a in range(2):
                        last = eng.matmul(pb[2 + a][0:NB, :], sel_to[:, b - 1, :], os_row[:, a * 512:(a + 1) * 512],
                                          start=b == 1, stop=b == NB, skip_group_check=True)
                    last.then_inc(S["ot_done"], 1)
            eng.wait_ge(S["ot_kept"], 1)
            eng.wait_ge(S["pv_kept"], G)
            for j in range(8):
                last = eng.transpose(pb[5][:, j * 8:(j + 1) * 8], os_tok[:, j * P:(j + 1) * P], ident[0:NB, 0:NB])
            last.then_inc(S["otT_done"], 1)
            project("sb_out", 2, IN_SB_OUT)

            sum_squares(FFN1)
            for t in range(TT):
                if t == 0:
                    h_is_ready(FFN1)
                for k in range(KC):
                    last = eng.matmul(pb[4][0:TOK[t], t * NE:(t + 1) * NE], h[:, k, t * P:t * P + TOK[t]], w_router[:, k, :],
                                      start=k == 0, stop=k == KC - 1)
            last.then_inc(S["logits_done"], 1)
            eng.wait_ge(S["gates_ready"], 1)
            for t in range(TT):
                n = TOK[t]
                to = pb[5][0:n, t * NE:(t + 1) * NE]
                eng.matmul(to, before[0:n, 0:n], chosen[0:n, t, :], start=True, stop=t == 0)
                for s in range(t):
                    eng.matmul(to, ones[:, 0:n], chosen[:, s, :], start=False, stop=s == t - 1)
            for t in range(TT):
                n = TOK[t]
                last = eng.matmul(pb[5][:, TT * NE:(TT + 1) * NE], ones[0:n, :], chosen[0:n, t, :], start=t == 0, stop=t == 2)
            last.then_inc(S["count_done"], 1)
            eng.wait_ge(S["most_ready"], 1)
            busiest = eng.value_load(most[0:1, 0:1], min_val=0, max_val=T)
            with eng.If(busiest > cap):
                for t in range(TT):
                    n = TOK[t]
                    last = eng.transpose(pb[4][0:NE, t * P:t * P + n], gate_tok[0:n, t, :], ident[0:n, 0:n])
                last.then_inc(S["gateT_done"], 1)
                eng.wait_ge(S["gateT_kept"], 1)
                for e in range(NE):
                    if e >= 2:
                        eng.wait_ge(S["gbc_kept"], e - 1)
                    eng.matmul(pb[6 + e % 2][:, 0:T], sel(e), gateT[:], start=True, stop=True).then_inc(S["gbc_done"], 1)
                with eng.Fori(0, NE) as it:
                    for p in range(7):
                        ws = []
                        for s in range(2):
                            expert_landed(eng, it, 2 * p + s)
                            ws.append(cols8(ring[(BASE + 2 * p + s) % RING]))
                        for q in range(4):
                            n = 4 * p + q
                            if n >= 2:
                                eng.wait_ge(S["pair_kept"], it * FEC + (n - 1))
                            else:
                                eng.wait_ge(S["down_kept"], it * 56 + 1)
                            for s in range(2):
                                for k in range(KC):
                                    last = eng.matmul(pb[2 * (n % 2) + s][:, 0:T], ws[s][:, k, q * P:(q + 1) * P], h[:, k, :],
                                                      start=k == 0, stop=k == KC - 1)
                                last.then_inc(S["gate_half_done" if s == 0 else "pair_done"], 1)
                    eng.wait_ge(S["pair_kept"], it * FEC + FEC)
                    for i in range(7):
                        expert_landed(eng, it, 14 + i)
                        w = ring[(BASE + 14 + i) % RING][:].rearrange("p (k c) -> p k c", k=4)
                        for dc in range(8):
                            n = 8 * i + dc
                            if n >= 4:
                                eng.wait_ge(S["down_kept"], it * 56 + (n - 2))
                            for k in range(4):
                                last = eng.matmul(pb[n % 4][:, 0:T], w[:, k, dc * P:(dc + 1) * P], act_m[:, 4 * i + k, :],
                                                  start=k == 0, stop=k == 3)
                            last.then_inc(S["down_done"], 1)
            with eng.Else():
                for k in range(KC):
                    if k >= 2:
                        eng.wait_ge(S["htok_lo"], TT * (k - 1))
                    for t in range(TT):
                        n = TOK[t]
                        last = eng.transpose(pb[6 + k % 2][0:n, t * P:(t + 1) * P], h[:, k, t * P:t * P + n], ident[:])
                    last.then_inc(S["htok_turned"], 1)
                for e in range(NE):
                    eng.wait_ge(S["put_ready"], e + 1)
                    if e >= 2:
                        eng.wait_ge(S["put_kept"], e - 1)
                    for t in range(TT):
                        n = TOK[t]
                        last = eng.transpose(pb[2 + e % 2][:, t * P:t * P + n], put_tok[0:n, e % 2, t, :], ident[0:n, 0:n])
                    last.then_inc(S["put_turned"], 1)
                eng.wait_ge(S["put_kept"], NE)
                eng.wait_ge(S["pick_ready"], NE + 1)
                eng.wait_ge(S["htok_lo"], TT * KC)

                def gather(e):
                    for a in range(2):
                        to = pb[7 - 3 * a]
                        for k in range(4):
                            for t in range(TT):
                                n = TOK[t]
                                for s, part in enumerate((tok_hi, tok_lo)):
                                    last = eng.matmul(to[:, k * CAP:(k + 1) * CAP],
                                                      part[0:n, t, (4 * a + k) * P:(4 * a + k + 1) * P], pick[0:n, e, t, :],
                                                      start=t + s == 0, stop=t + s == TT)
                        last.then_inc(S["gather_done"], 1)

                def turn(p):
                    for j in range(4):
                        last = eng.transpose(pb[4 if p % 2 == 0 else 7][:, j * CAP:(j + 1) * CAP], act_e[:, j * P:(j + 1) * P],
                                             ident[:])
                    last.then_inc(S["turned"], 1)

                gather(0)
                with eng.Fori(0, NE) as it:
                    eng.wait_ge(S["xe_lo_ready"], it * 2 + 2)
                    for j in range(4 * PER_E):
                        n = NU + j
                        eng.wait_ge(S["lo_ready"], it * (4 * PER_E) + (n + 1))
                        if j < 56:
                            p, s, q = j // 8, j % 8 // 4, j % 4
                            if s == 0 and q == 0:
                                if p >= 2:
                                    eng.wait_ge(S["gate_up_kept"], it * 7 + (p - 1))
                                else:
                                    eng.wait_ge(S["added"], it * 8 + 1)
                            wh, wl = unit(w_hi, "up", n), unit(w_lo, "up", n)
                            for k in range(2):
                                c = 2 * q + k
                                last = three(pb[2 * (p % 2) + s], xe_hi[:, c, :], xe_lo[:, c, :], wh[:, k, :], wl[:, k, :],
                                             c == 0, c == KC - 1)
                        else:
                            c = j - 56
                            if c % 4 == 0:
                                eng.wait_ge(S["at_lo_ready"], it * 7 + (c // 4 + 1))
                            wh, wl = unit(w_hi, "down", n), unit(w_lo, "down", n)
                            for a in range(2):
                                last = three(pb[5 + a], at_hi[:, c, :], at_lo[:, c, :], wh[:, 0, a * 512:(a + 1) * 512],
                                             wl[:, 0, a * 512:(a + 1) * 512], c == 0, c == FEC - 1)
                        last.then_inc(S["unit_used"], 1)
                        if j % 8 == 3 and 11 <= j <= 59:
                            p = (j - 11) // 8
                            eng.wait_ge(S["gate_up_kept"], it * 7 + (p + 1))
                            if p >= 2:
                                eng.wait_ge(S["at_lo_ready"], it * 7 + (p - 1))
                            turn(p)
                        if j == 75:
                            eng.wait_ge(S["at_lo_ready"], it * 7 + 7)
                            gather(it + 1)
                    eng.wait_ge(S["y_e_kept"], it + 1)
                    for k in range(KC):
                        if k >= 4:
                            eng.wait_ge(S["added"], it * 8 + (k - 2))
                        eng.matmul(pb[k % 4][:, 0:T], y_e[:, k * P:(k + 1) * P], put[:, it, :], start=True,
                                   stop=True).then_inc(S["scattered"], 1)

            sum_squares(FINAL)
            for t in range(TT):
                n = TOK[t]
                for a in range(2):
                    i = 2 * t + a
                    if i == 0:
                        h_is_ready(FINAL)
                    if i >= 2:
                        eng.wait_ge(S["y_kept"], i - 1)
                    for j in range(4):
                        last = eng.transpose(pb[4 + i % 2][0:n, j * P:(j + 1) * P], h[:, 4 * a + j, t * P:t * P + n], ident[:])
                    last.then_inc(S["y_turned"], 1)

        @block.scalar
        def _(eng):
            steps = [0]

            def link(ins):
                steps[0] += 1
                ins.then_inc(S["act_step"], 1)
                eng.wait_ge(S["act_step"], steps[0])

            def split(m, late=False):
                if m >= NU or (m - UNIT_AT["sb_out", 0] in range(AHEAD) and not late):
                    return
                kind, i = SPLIT[m // 4]
                ks = chunks_of(kind, i)
                if m % 4 == 0:
                    landed(eng, kind, i)
                if m >= UNITS:
                    eng.wait_ge(S["unit_used"], m - UNITS + 1)
                eng.copy(unit(w_hi, kind, m, ks), quarter(slot(kind, i), kind, m % 4, ks)).then_inc(S["hi_ready"], 1)

            for m in range(AHEAD):
                split(m)
            eng.wait_ge(S["small_loaded"], 16 * 16)
            eng.activation(csilu, crow, ACT.Silu).then_inc(S["c_silu"], 1)
            eng.wait_ge(S["c_turned"], 1)
            eng.wait_ge(S["c_zero"], 1)
            eng.copy(c_split[:, :, 0:NC9], pb[5][:, 0:P].rearrange("p (k c) -> p k c", c=16)[:, :, 0:NC9]).then_inc(S["c_hi"], 1)
            for i in range(N_ADA):
                for j in range(4):
                    split(UNIT_AT["ada", i] + j + AHEAD)
                eng.wait_ge(S["unit_used"], UNIT_AT["ada", i] + 4)
                if i >= 2:
                    eng.wait_ge(S["ada_turned"], i - 1)
                eng.copy(ada_row[:, i % 2, :], pb[i % 2][0:CR, :]).then_inc(S["ada_copied"], 1)

            def norm(m, splits=True):
                for k in range(KC):
                    eng.activation(h[:, k, :], x[:, k, :], ACT.Square).then_inc(S["squared"], 1)
                eng.wait_ge(S["ms_ready"], m + 1)
                eng.activation(rstd[:], rstd[:], ACT.Sqrt).then_inc(S["root_ready"], 1)
                for k in range(KC + 1):
                    if k < KC:
                        eng.wait_ge(S["scaled"], m * KC + k + 1)
                        eng.activation(h[:, k, 0:TP], h[:, k, 0:TP], ACT.Identity, bias=mod[:, SHIFT[m] + k, 0:1],
                                       scale=gain[:, m, k, 0:1]).then_inc(S["h_ready"], 1)
                    if splits and k >= 1:
                        eng.wait_ge(S["h_ready"], m * KC + k)
                        if k == 1:
                            eng.wait_ge(S["hs_ready"], m + 1)
                        eng.copy(hh[:, k - 1, :], h[:, k - 1, :]).then_inc(S["hh_ready"], 1)

            def block(kind, i):
                u = UNIT_AT[kind, i // 4] + i % 4
                split(u + AHEAD)
                eng.wait_ge(S["unit_used"], u + 1)
                return pb[BLOCK_AT[kind, i] % 4][:, 0:T]

            def split_during(kind, n_tiles):
                for u in range(4 * n_tiles):
                    split(UNIT_AT[kind, 0] + u + AHEAD)

            eng.wait_ge(S["x_kept"], KC)
            eng.wait_ge(S["vec_kept"], 2)
            eng.wait_ge(S["gains_ready"], 6)
            norm(MIX0)
            for i in range(24):
                got = block("gla_in", i)
                if i < 4:
                    ins = eng.activation(big[:, i, :], got, ACT.Copy, scale=float(DK) ** -0.5)
                else:
                    ins = eng.activation(big[:, i, :], got, ACT.Copy if i < 16 else ACT.Silu)
                ins.then_inc(S["kept_act"], 1)
            eng.wait_ge(S["r_done"], 1)
            eng.copy(rT, pb[BLOCK_AT["gla_in", 24] % 4][0:GR, 0:T]).then_inc(S["kept_act"], 1)
            eng.wait_ge(S["gate_done"], 1)
            for g in range(GH):
                eng.activation(la[:, g, :], pb[4 + g][:, 0:T], ACT.Identity, bias=vec_b[:, GLA_BIAS + g:GLA_BIAS + g + 1])
                last = eng.activation(t_abs[:, g, :], pb[4 + g][:, 0:T], ACT.Abs,
                                      bias=vec_b[:, GLA_BIAS + g:GLA_BIAS + g + 1])
            link(last)
            link(eng.activation(t_abs, t_abs, ACT.Exp, scale=-1.0))
            eng.activation(t_abs, t_abs, ACT.Ln, bias=1.0).then_inc(S["log_sig"], 1)
            eng.wait_ge(S["args_ready"], 1)
            ends = cum.rearrange("p (u s) t -> p u s t", s=2)[:, :, 1, HALF - 1]
            for to, arg in ((qd, qd), (kd, kd), (qo, qo), (ko, ko),
                            (qe, cum.rearrange("p u t -> p (u t)").rearrange("p (h t) -> p h t", h=GH)),
                            (ke, ke), (dec, ends), (ea[:], la[:, :, TP:T])):
                eng.activation(to, arg, ACT.Exp).then_inc(S["exps_ready"], 1)
            for c in range(NCH):
                eng.wait_ge(S["v_turned"], c + 1)
                if c >= 2:
                    eng.wait_ge(S["u_done"], c - 1)
                eng.copy(vtok[c % 2][:, 0:512], pb[0][0:C, :])
                eng.copy(vtok[c % 2][:, 512:D], pb[1][0:C, :]).then_inc(S["v_kept"], 1)
                eng.copy(ktok[:, (c % 2) * 512:(c % 2 + 1) * 512], pb[2][0:C, :]).then_inc(S["v_kept"], 1)
            eng.wait_ge(S["vs_turned"], 1)
            eng.wait_ge(S["o_done"], NCH)
            eng.copy(vs_tok[:, 0:512], pb[0][0:NB, :])
            eng.copy(vs_tok[:, 512:D], pb[1][0:NB, :]).then_inc(S["vs_kept"], 1)
            eng.wait_ge(S["os_kept"], 1)
            for g in range(GH):
                eng.activation(big[:, 2 * g:2 * g + 2, :], h[:, 2 * g:2 * g + 2, :], ACT.Square).then_inc(S["osq_ready"], 1)
            eng.wait_ge(S["oms_ready"], 1)
            eng.activation(orstd, orstd, ACT.Sqrt).then_inc(S["oroot_ready"], 1)

            for k in range(KC):
                eng.wait_ge(S["o_ready"], k + 1)
                eng.copy(hh[:, k, :], h[:, k, :]).then_inc(S["hh_ready"], 1)
            split_during("gla_out", 2)
            eng.wait_ge(S["kept_dve"], empt[BLOCK_AT["gla_out", 7]][1])
            norm(FFN0)
            eng.wait_ge(S["s0_stored0"], 16 * NB // 2)
            eng.wait_ge(S["s0_stored1"], 16 * NB // 2)
            eng.wait_ge(S["state_stored"], 16)
            for i in range(FFC + 1):
                if i < FFC:
                    got = block("ffn_up", 2 * i)
                    if i >= 2:
                        eng.wait_ge(S["kept_dve"], empt[BLOCK_AT["ffn_up", 2 * i - 4]][1])
                    eng.activation(silu_a[:, i % 2, :], got, ACT.Silu).then_inc(S["silu_done"], 1)
                    split(UNIT_AT["ffn_up", 0] + 2 * i + 1 + AHEAD)
                if i >= 1:
                    eng.wait_ge(S["kept_dve"], empt[BLOCK_AT["ffn_up", 2 * i - 2]][1])
                    eng.copy(act_hi[:, i - 1, :], act32[:, (i - 1) % 2, :]).then_inc(S["act_hi_ready"], 1)
            split_during("ffn_down", 6)
            eng.wait_ge(S["kept_dve"], empt[BLOCK_AT["ffn_down", 47]][1])
            norm(KV)
            for i in range(16):
                eng.copy(kvq[:, i, :], block("kv", i)).then_inc(S["kept_act"], 1)
            for i in range(12):
                t, q = i // 4, i % 4
                eng.wait_ge(S["kv_turned"], i + 1)
                eng.copy(kvtok[0:TOK[t], t, q * 512:(q + 1) * 512], pb[4 + i % 2][0:TOK[t], :]).then_inc(S["kv_kept"], 1)
            norm(MIX1)
            for i in range(8):
                eng.copy(kvq[:, 16 + i, :], block("sb_q", i)).then_inc(S["kept_act"], 1)
            eng.wait_ge(S["qs_turned"], 1)
            eng.copy(qs_tok[:, 0:512], pb[4][0:NB, :])
            eng.copy(qs_tok[:, 512:D], pb[5][0:NB, :]).then_inc(S["qs_kept"], 1)

            def soft(g, z, to):
                eng.wait_ge(S["z_ready"], g + 1)
                if 2 <= g < SH // 2:
                    eng.wait_ge(S["rc_done"], g - 1)
                link(eng.activation(to, z, ACT.Abs))
                link(eng.activation(to, to, ACT.Exp, scale=-1.0))
                eng.activation(to, to, ACT.Ln, bias=1.0).then_inc(S["soft_ready"], 1)

            G = SH // 2
            for g in range(G + 2):
                if g < G:
                    soft(g, z_buf[:, g % 2, :], l_buf[:, g % 2, :])
                if 1 <= g <= G:
                    eng.wait_ge(S["arg_ready"], g)
                    zg = z_buf[:, (g - 1) % 2, :]
                    eng.activation(zg, zg, ACT.Exp).then_inc(S["p_exp"], 1)
                if g >= 2:
                    eng.wait_ge(S["pv_done"], g - 1)
                    eng.copy(h[:, g - 2, 0:TP], pb[6 + g % 2][:, 0:TP]).then_inc(S["pv_kept"], 1)
            soft(G, zs, ls)
            eng.wait_ge(S["args_s"], 1)
            eng.activation(zs, zs, ACT.Exp).then_inc(S["exps_s"], 1)
            for m in range(AHEAD):
                split(UNIT_AT["sb_out", 0] + m, late=True)
            eng.wait_ge(S["otT_done"], 1)
            eng.copy(h[:, :, TP:T], pb[5][:, 0:64].rearrange("p (k b) -> p k b", b=NB)).then_inc(S["otT_kept"], 1)
            eng.wait_ge(S["otT_kept"], 1)
            eng.wait_ge(S["pv_kept"], G)
            for k in range(KC):
                eng.copy(hh[:, k, :], h[:, k, :]).then_inc(S["hh_ready"], 1)
            split_during("sb_out", 2)

            eng.wait_ge(S["kept_dve"], empt[-1][1])
            norm(FFN1, splits=False)
            eng.wait_ge(S["gates_exp"], 1)
            for t in range(TT):
                last = eng.activation(e2[0:TOK[t], t:t + 1], e2[0:TOK[t], t:t + 1], ACT.Exp)
            last.then_inc(S["gates_exp_done"], 1)
            eng.wait_ge(S["most_ready"], 1)
            busiest = eng.value_load(most[0:1, 0:1], min_val=0, max_val=T)
            with eng.If(busiest > cap):
                eng.wait_ge(S["gateT_done"], 1)
                eng.copy(gateT[:], pb[4][0:NE, 0:T]).then_inc(S["gateT_kept"], 1)
                for e in range(NE):
                    eng.wait_ge(S["gbc_done"], e + 1)
                    eng.copy(gate_bc[:, e, :], pb[6 + e % 2][:, 0:T]).then_inc(S["gbc_kept"], 1)
                with eng.Fori(0, NE) as it:
                    for n in range(FEC):
                        eng.wait_ge(S["gate_half_done"], it * FEC + (n + 1))
                        eng.activation(silu_m[:, n % 2, :], pb[2 * (n % 2)][:, 0:T], ACT.Silu).then_inc(S["pair_silu"], 1)
            with eng.Else():
                for k in range(KC):
                    eng.wait_ge(S["htok_turned"], k + 1)
                    for t in range(TT):
                        n = TOK[t]
                        eng.copy(tok_hi[0:n, t, k * P:(k + 1) * P],
                                 pb[6 + k % 2][0:n, t * P:(t + 1) * P]).then_inc(S["htok_hi"], 1)
                for e in range(NE):
                    eng.wait_ge(S["put_turned"], e + 1)
                    eng.copy(put[:, e, :], pb[2 + e % 2][:, 0:T]).then_inc(S["put_kept"], 1)

                def keep_gathered(done):
                    for a in range(2):
                        eng.wait_ge(S["gather_done"], done + (a + 1))
                        eng.copy(xe_hi[:, 4 * a:4 * a + 4, :],
                                 pb[7 - 3 * a].rearrange("p (k c) -> p k c", k=4)).then_inc(S["xe_hi_ready"], 1)

                keep_gathered(0)
                with eng.Fori(0, NE) as it:
                    for j in range(4 * PER_E):
                        n = NU + j
                        if j % 4 == 0:
                            expert_landed(eng, it, j // 4)
                        eng.wait_ge(S["unit_used"], it * (4 * PER_E) + (n - UNITS + 1))
                        kind = "up" if j < 56 else "down"
                        eng.copy(unit(w_hi, kind, n), quarter(ring[(BASE + j // 4) % RING], kind, j % 4)).then_inc(S["hi_ready"], 1)
                        if j % 8 == 7 and j < 56:
                            p = j // 8
                            if p >= 1:
                                eng.wait_ge(S["gate_up_kept"], it * 7 + p)
                            eng.activation(silu_e[:], pb[2 * (p % 2)], ACT.Silu).then_inc(S["e_silu"], 1)
                        if j % 8 == 7 and 15 <= j <= 63:
                            p = (j - 15) // 8
                            eng.wait_ge(S["turned"], it * 7 + (p + 1))
                            eng.copy(at_hi[:, 4 * p:4 * p + 4, :], pb[4 if p % 2 == 0 else 7]
                                     .rearrange("p (k c) -> p k c", k=4)).then_inc(S["at_hi_ready"], 1)
                        if j == 79:
                            keep_gathered(it * 2 + 2)
                    eng.wait_ge(S["unit_used"], it * (4 * PER_E) + (NU + 4 * PER_E))
                    eng.copy(y_e[:], psum[:, 5 * 512:7 * 512]).then_inc(S["y_e_kept"], 1)
            eng.wait_ge(S["experts_done"], 1)
            norm(FINAL, splits=False)
            for i in range(6):
                t, a = i // 2, i % 2
                eng.wait_ge(S["y_turned"], i + 1)
                eng.copy(ytok[0:TOK[t], t, a * 512:(a + 1) * 512], pb[4 + i % 2][0:TOK[t], :]).then_inc(S["y_kept"], 1)

        @block.vector
        def _(eng):
            steps = [0]

            def link(ins):
                steps[0] += 1
                ins.then_inc(S["dve_step"], 1)
                eng.wait_ge(S["dve_step"], steps[0])

            def split(m, late=False):
                if m >= NU or (m - UNIT_AT["sb_out", 0] in range(AHEAD) and not late):
                    return
                kind, i = SPLIT[m // 4]
                ks = chunks_of(kind, i)
                eng.wait_ge(S["hi_ready"], m + 1)
                eng.tensor_tensor(unit(w_lo, kind, m, ks), quarter(slot(kind, i), kind, m % 4, ks),
                                  unit(w_hi, kind, m, ks), ALU.subtract).then_inc(S["lo_ready"], 1)

            eng.memset(c_split[:].bitcast(F32), 0.0).then_inc(S["c_zero"], 1)
            for m in range(AHEAD):
                split(m)
            eng.wait_ge(S["vec_turned"], 1)
            eng.tensor_copy(vec_a[:], pb[4][:, 0:P]).then_inc(S["vec_kept"], 1)
            eng.tensor_copy(vec_b[:], pb[4][:, P:P + VEC_B]).then_inc(S["vec_kept"], 1)
            eng.wait_ge(S["c_hi"], 1)
            eng.tensor_tensor(c_split[:, :, LO_ROW:CR], pb[5][:, 0:P].rearrange("p (k c) -> p k c", c=16)[:, :, 0:NC9],
                              c_split[:, :, 0:NC9], ALU.subtract).then_inc(S["c_kept"], 1)
            for k in range(KC):
                eng.wait_ge(S["x_turned"], k + 1)
                eng.tensor_copy(x[:, k, :], pb[6 + k % 2][:, 0:T]).then_inc(S["x_kept"], 1)
            eng.wait_ge(S["vec_kept"], 2)
            for i in range(N_ADA + 1):
                for j in range(4 if i < N_ADA else 0):
                    split(UNIT_AT["ada", i] + j + AHEAD)
                if i == 0:
                    continue
                eng.wait_ge(S["ada_turned"], i)
                to, got = mod[:, 4 * i - 4:4 * i, :], pb[2 + (i - 1) % 2][:, 0:256].rearrange("p (k c) -> p k c", c=64)
                eng.tensor_tensor(to, got[:, :, 0:NC9], vec_a[:, 4 * i - 4:4 * i].unsqueeze(2).to_broadcast([P, 4, NC9]),
                                  ALU.add).then_inc(S["ada_part"], 1)
                eng.wait_ge(S["ada_part"], i)
                eng.tensor_tensor(to, to, got[:, :, LO_ROW:CR], ALU.add).then_inc(S["ada_kept"], 1)
            eng.wait_ge(S["ada_kept"], N_ADA)
            for m in range(6):
                eng.scalar_tensor_tensor(gain[:, m, :, :], mod[:, SCALE[m]:SCALE[m] + KC, :], 1.0,
                                         vec_b[:, GAIN[m]:GAIN[m] + KC].unsqueeze(2).to_broadcast([P, KC, NC9]),
                                         ALU.add, ALU.mult).then_inc(S["gains_ready"], 1)
            eng.wait_ge(S["gains_ready"], 6)

            def norm(m):
                eng.wait_ge(S["ss_done"], m + 1)
                eng.tensor_scalar(rstd[:], pb[7][:, 0:T], 1.0 / D, EPS, ALU.mult, ALU.add).then_inc(S["ms_ready"], 1)
                eng.wait_ge(S["root_ready"], m + 1)
                link(eng.reciprocal(rstd[:], rstd[:]))
                hs = h[:, :, TP:T]
                link(eng.tensor_tensor(hs, x[:, :, TP:T], rstd[:, TP:T].unsqueeze(1).to_broadcast([P, KC, NB]), ALU.mult))
                link(eng.tensor_tensor(hs, hs, gain[:, m, :, 1:NC9], ALU.mult))
                eng.tensor_tensor(hs, hs, mod[:, SHIFT[m]:SHIFT[m] + KC, 1:NC9], ALU.add).then_inc(S["hs_ready"], 1)
                for k in range(KC):
                    eng.tensor_tensor(h[:, k, 0:TP], x[:, k, 0:TP], rstd[:, 0:TP], ALU.mult).then_inc(S["scaled"], 1)

            def low_parts(m):
                for k in range(KC):
                    eng.wait_ge(S["hh_ready"], m * KC + k + 1)
                    eng.tensor_tensor(hl[:, k, :], h[:, k, :], hh[:, k, :], ALU.subtract).then_inc(S["hl_ready"], 1)

            def split_during(kind, n_tiles):
                for u in range(4 * n_tiles):
                    split(UNIT_AT[kind, 0] + u + AHEAD)

            def add_to_x(got, k, gate, parted, value):
                xs, ts = x[:, k, TP:T], tmp8[:, k, :]
                eng.scalar_tensor_tensor(x[:, k, 0:TP], got[:, 0:TP], mod[:, gate + k, 0:1], x[:, k, 0:TP], ALU.mult, ALU.add)
                eng.tensor_tensor(ts, got[:, TP:T], mod[:, gate + k, 1:NC9], ALU.mult).then_inc(parted, 1)
                eng.wait_ge(parted, value)
                return eng.tensor_tensor(xs, xs, ts, ALU.add)

            parts = [0]

            def add_block(kind, i, gate):
                n = BLOCK_AT[kind, i]
                per = 8 if kind == "ffn_down" else 4
                u = UNIT_AT[kind, i // per] + i % per * 4 // per
                if per == 4 or i % 2 == 0:
                    split(u + AHEAD)
                eng.wait_ge(S["unit_used"], u + 1)
                if empt[n][1] > 1:
                    eng.wait_ge(S["kept_dve"], empt[n][1] - 1)
                parts[0] += 1
                add_to_x(pb[n % 4], i % 8, gate, S["part_added"], parts[0]).then_inc(S["kept_dve"], 1)

            norm(MIX0)
            low_parts(IN_GLA)
            split_during("gla_in", 6)
            eng.wait_ge(S["log_sig"], 1)
            link(eng.scalar_tensor_tensor(la, la, 0.0, t_abs, ALU.min, ALU.subtract))
            link(eng.tensor_scalar(la, la, 1.0 / 16.0, None, ALU.mult))
            four = lambda v: v.rearrange("p (h c s) t -> p h c (s t)", h=GH, c=NCH)
            src = la[:, :, 0:TP].rearrange("p h (c t) -> p h c t", t=C)
            for n, d in enumerate((1, 2, 4, 8, 16, 32)):
                dst = four(cum_a if n % 2 == 0 else cum)
                eng.tensor_copy(dst[:, :, :, 0:d], src[:, :, :, 0:d])
                link(eng.tensor_tensor(dst[:, :, :, d:C], src[:, :, :, d:C], src[:, :, :, 0:C - d], ALU.add))
                src = dst
            mid = cum[:, :, HALF // 2 - 1:HALF // 2].to_broadcast([P, 32, HALF])
            link(eng.tensor_tensor(qd, cum, mid, ALU.subtract))
            eng.tensor_scalar(kd, qd, -1.0, EXP_CAP, ALU.mult, ALU.min)
            halves = cum.rearrange("p (u s) t -> p u s t", s=2)
            seam = halves[:, :, 0, HALF - 1:HALF].to_broadcast([P, 16, HALF])
            eng.tensor_tensor(qo, halves[:, :, 1, :], seam, ALU.subtract)
            link(eng.tensor_tensor(ko, seam, halves[:, :, 0, :], ALU.subtract))
            chunks = cum.rearrange("p (u s) t -> p u (s t)", s=2)
            eng.tensor_tensor(ke.rearrange("p h t -> p (h t)").rearrange("p (u t) -> p u t", u=16),
                              chunks[:, :, C - 1:C].to_broadcast([P, 16, C]), chunks, ALU.subtract)
            eng.tensor_scalar(qd, qd, EXP_CAP, None, ALU.min).then_inc(S["args_ready"], 1)
            q, k = big[:, 0:GH, 0:TP], big[:, GH:2 * GH, 0:TP]
            by_head = lambda v: v.rearrange("p (h u) t -> p h (u t)", h=GH)
            side = lambda v, s: v.rearrange("p h (c s t) -> p h c s t", c=NCH, s=2)[:, :, :, s, :]
            by_chunk = lambda v: v.rearrange("p (h c) t -> p h c t", h=GH)
            for n, (v, w) in enumerate(((by_head(qd), q), (by_head(kd), k), (by_chunk(qo), side(q, 1)),
                                        (by_chunk(ko), side(k, 0)), (qe, q), (ke, k))):
                eng.wait_ge(S["exps_ready"], n + 1)
                eng.tensor_tensor(v, v, w, ALU.mult).then_inc(S["decayed"], 1)
            link(eng.memset(st[HALF:C, :, 0:HALF], 0.0))
            eng.wait_ge(S["scores_done"], 1)
            for n in range(2):
                got = pb[4 + n].rearrange("p (u t) -> p u t", t=C)
                eng.tensor_tensor(st[:, 8 * n:8 * n + 8, HALF:C], got[0:C, :, HALF:C],
                                  upto[:, HALF:C].unsqueeze(1).to_broadcast([C, 8, HALF]), ALU.mult)
                last = eng.tensor_tensor(st[0:HALF, 8 * n:8 * n + 8, 0:HALF], got[0:HALF, :, 0:HALF],
                                         upto[0:HALF, 0:HALF].unsqueeze(1).to_broadcast([HALF, 8, HALF]), ALU.mult)
            last.then_inc(S["scores_kept"], 1)
            for c in range(NCH):
                eng.wait_ge(S["o_done"], c + 1)
                eng.tensor_copy(h[:, :, c * C:(c + 1) * C], pb[3].rearrange("p (k t) -> p k t", t=C)).then_inc(S["o_kept"], 1)
                eng.wait_ge(S["u_done"], c + 1)
                u = psum[:, 6 * 512:8 * 512].rearrange("p (g v) -> p g v", g=GH)
                if c == 0:
                    eng.tensor_copy(state[0], u).then_inc(S["state_ready"], 1)
                    continue
                eng.wait_ge(S["state_ready"], c)
                eng.wait_ge(S["exps_ready"], 7)
                for g in range(GH):
                    last = eng.scalar_tensor_tensor(state[c % 2][:, g, :], state[(c - 1) % 2][:, g, :],
                                                    dec[:, g * NCH + c:g * NCH + c + 1], u[:, g, :], ALU.mult, ALU.add)
                last.then_inc(S["state_ready"], 1)
            eng.wait_ge(S["exps_ready"], 8)
            for b in range(NB):
                eng.wait_ge(S[f"s0_loaded{b % 2}"], 16 * (b // 2 + 1))
                s = s0[b % 2]
                for g in range(GH):
                    last = eng.tensor_scalar(s[:, g, :], s[:, g, :], ea[:, g, b:b + 1], None, ALU.mult)
                link(last)
                eng.wait_ge(S["vbc_done"], b + 1)
                v = psum[:, (4 + 2 * (b % 2)) * 512:(6 + 2 * (b % 2)) * 512].rearrange("p (g v) -> p g v", g=GH)
                for g in range(GH):
                    last = eng.scalar_tensor_tensor(s[:, g, :], v[:, g, :], big[:, GH + g, TP + b:TP + b + 1], s[:, g, :],
                                                    ALU.mult, ALU.add)
                last.then_inc(S["s_updated"], 1)
            eng.wait_ge(S["os_done"], NB)
            eng.tensor_copy(h[:, :, TP:T], pb[3][:, 0:64].rearrange("p (k b) -> p k b", b=NB)).then_inc(S["os_kept"], 1)
            eng.wait_ge(S["oss_done"], 1)
            for g in range(GH):
                last = eng.tensor_scalar(orstd[:, g, :], pb[4 + g][:, 0:T], 1.0 / DV, EPS, ALU.mult, ALU.add)
            last.then_inc(S["oms_ready"], 1)
            eng.wait_ge(S["oroot_ready"], 1)
            link(eng.reciprocal(orstd, orstd))
            for j in range(KC):
                link(eng.scalar_tensor_tensor(h[:, j, :], h[:, j, :], vec_b[:, GLA_GAIN + j % 2:GLA_GAIN + j % 2 + 1],
                                              orstd[:, j // 2, :], ALU.mult, ALU.mult))
                eng.tensor_tensor(h[:, j, :], h[:, j, :], big[:, 16 + j, :], ALU.mult).then_inc(S["o_ready"], 1)
            low_parts(IN_GLA_OUT)
            for i in range(8):
                add_block("gla_out", i, GATE[MIX0])

            norm(FFN0)
            low_parts(IN_FFN)
            eng.wait_ge(S["s0_stored0"], 16 * NB // 2)
            eng.wait_ge(S["s0_stored1"], 16 * NB // 2)
            eng.wait_ge(S["state_stored"], 16)
            for i in range(FFC + 1):
                if i < FFC:
                    n, u = BLOCK_AT["ffn_up", 2 * i + 1], UNIT_AT["ffn_up", 0] + 2 * i
                    split(u + AHEAD)
                    split(u + 1 + AHEAD)
                    eng.wait_ge(S["unit_used"], u + 2)
                    eng.wait_ge(S["silu_done"], i + 1)
                    if i >= 2:
                        eng.wait_ge(S["act_ready"], i - 1)
                    eng.tensor_tensor(act32[:, i % 2, :], silu_a[:, i % 2, :], pb[n % 4][:, 0:T], ALU.mult).then_inc(S["kept_dve"], 1)
                if i >= 1:
                    eng.wait_ge(S["act_hi_ready"], i)
                    eng.tensor_tensor(act_lo[:, i - 1, :], act32[:, (i - 1) % 2, :], act_hi[:, i - 1, :],
                                      ALU.subtract).then_inc(S["act_ready"], 1)
            for i in range(48):
                add_block("ffn_down", i, GATE[FFN0])
            norm(KV)
            low_parts(IN_KV)
            split_during("kv", 4)
            norm(MIX1)
            low_parts(IN_Q)
            split_during("sb_q", 2)

            for b in range(NB):
                if b % 2 == 0:
                    landed(eng, "k_cache", b // 2)
                eng.wait_ge(S["qbc_done"], b + 1)
                qb = psum[:, (4 + 2 * (b % 2)) * 512:(6 + 2 * (b % 2)) * 512]
                for page in range(PAGES):
                    lo = ((b % 2) * 2 + page) * D
                    link(eng.tensor_tensor(prod, slot("k_cache", b // 2)[:, lo:lo + D], qb, ALU.mult))
                    last = eng.tensor_reduce(zs[:, page, b * SH:(b + 1) * SH], prod.rearrange("p (h d) -> p h d", h=SH),
                                             AX.X, ALU.add)
                    if page == 0:
                        link(last)
                last.then_inc(S["z_s_ready"], 1)
                eng.wait_ge(S["z_s_ready"], b + 1)

            G = SH // 2
            scale = float(SD) ** -0.5
            mask4 = lambda v: v[:].unsqueeze(1).to_broadcast([P, 4, P])
            as4 = lambda v: v.rearrange("p (a t) -> p a t", t=P)
            for g in range(G + 1):
                if g < G:
                    eng.wait_ge(S["z_done"], g + 1)
                    if g >= 2:
                        eng.wait_ge(S["pv_done"], g - 1)
                    zg = z_buf[:, g % 2, :]
                    for a in range(2):
                        bias = sb_bias[:, 2 * g + a:2 * g + a + 1]
                        of_head = lambda v: v.rearrange("p (s a t) -> p s a t", s=2, a=2)[:, :, a, :]
                        got = pb[2 * (g % 2) + a]
                        eng.tensor_scalar(of_head(zg[:, 0:512]), got[:, 0:2 * P].rearrange("p (s t) -> p s t", s=2), scale, bias,
                                          ALU.mult, ALU.add)
                        last = eng.tensor_scalar(zg[:, 512 + a * P:512 + (a + 1) * P],
                                                 got[:, 2 * P:3 * P], scale, bias, ALU.mult, ALU.add)
                    last.then_inc(S["z_ready"], 1)
                if g >= 1:
                    zg = z_buf[:, (g - 1) % 2, :]
                    eng.wait_ge(S["rc_done"], g)
                    eng.tensor_tensor(zg[:, 0:512], zg[:, 0:512], pb[4], ALU.add)
                    eng.tensor_tensor(zg[:, 512:768], zg[:, 512:768], pb[5][:, 0:256], ALU.add).then_inc(S["arg_ready"], 1)
                if g < G:
                    zg, lg = z_buf[:, g % 2, :], l_buf[:, g % 2, :]
                    eng.wait_ge(S["soft_ready"], g + 1)
                    link(eng.scalar_tensor_tensor(lg, zg, 0.0, lg, ALU.max, ALU.add))
                    eng.tensor_tensor(as4(lg[:, 0:512]), as4(lg[:, 0:512]), mask4(not_before), ALU.mult)
                    eng.tensor_scalar(lg[:, 512:768], lg[:, 512:768], -1.0, None, ALU.mult).then_inc(S["l_ready"], 1)
                    link(eng.tensor_tensor(as4(zg[:, 0:512]), as4(zg[:, 0:512]), mask4(before), ALU.mult))
                if g >= 1:
                    zg = z_buf[:, (g - 1) % 2, :]
                    eng.wait_ge(S["p_exp"], g)
                    eng.tensor_tensor(as4(zg[:, 0:512]), as4(zg[:, 0:512]), mask4(before), ALU.mult).then_inc(S["p_ready"], 1)
            rows16 = lambda v: v.rearrange("p a b -> p (a b)").rearrange("p (a b) -> p a b", b=SH)
            eng.scalar_tensor_tensor(rows16(zs), rows16(zs), scale,
                                     sb_bias[:].unsqueeze(1).to_broadcast([P, PAGES * NB, SH]),
                                     ALU.mult, ALU.add).then_inc(S["z_ready"], 1)
            eng.wait_ge(S["soft_ready"], G + 1)
            link(eng.scalar_tensor_tensor(ls, zs, 0.0, ls, ALU.max, ALU.add))
            eng.tensor_scalar(ls, ls, -1.0, None, ALU.mult).then_inc(S["l_ready"], 1)
            eng.wait_ge(S["rcs_done"], 1)
            eng.tensor_tensor(zs, zs, pb[4][:, 0:256].rearrange("p (a b) -> p a b", a=PAGES), ALU.add).then_inc(S["args_s"], 1)
            own = ident[0:SH, 0:SH].unsqueeze(2).to_broadcast([SH, SH, SD])
            for b in range(NB):
                eng.wait_ge(S["opv_done"], b + 1)
                if b >= 1:
                    eng.wait_ge(S["ot_done"], b)
                eng.tensor_tensor(os_row.rearrange("p (h d) -> p h d", h=SH),
                                  psum[0:SH, 0:D].rearrange("p (h d) -> p h d", h=SH), own, ALU.mult).then_inc(S["own_ready"], 1)
            eng.wait_ge(S["ot_done"], NB)
            eng.tensor_copy(os_tok, psum[0:NB, D:2 * D]).then_inc(S["ot_kept"], 1)
            for m in range(AHEAD):
                split(UNIT_AT["sb_out", 0] + m, late=True)
            low_parts(IN_SB_OUT)
            for i in range(8):
                add_block("sb_out", i, GATE[MIX1])

            norm(FFN1)
            eng.wait_ge(S["kv_stored"], 16 * 6)
            eng.wait_ge(S["logits_done"], 1)
            for t in range(TT):
                n = TOK[t]
                lg, tp = logit[0:n, t, :], top[0:n, t, :]
                link(eng.tensor_tensor(lg, pb[4][0:n, t * NE:(t + 1) * NE], router_bias[0:n, :], ALU.add))
                link(eng.max(tp, lg))
                link(eng.max_index(top_i[0:n, t, :], tp, lg))
                eng.tensor_copy(top_f[0:n, t, :], top_i[0:n, t, :])
                link(eng.tensor_tensor(e2[0:n, t:t + 1], tp[:, 1:2], tp[:, 0:1], ALU.subtract))
            eng.nop().then_inc(S["gates_exp"], 1)
            eng.wait_ge(S["gates_exp_done"], 1)
            for t in range(TT):
                n = TOK[t]
                link(eng.tensor_scalar(w1[0:n, t:t + 1], e2[0:n, t:t + 1], 1.0, None, ALU.add))
                link(eng.reciprocal(w1[0:n, t:t + 1], w1[0:n, t:t + 1]))
                link(eng.tensor_tensor(w2[0:n, t:t + 1], e2[0:n, t:t + 1], w1[0:n, t:t + 1], ALU.mult))
                eng.tensor_scalar(hit[0:n, t, :], iota[0:n, 0:NE], top_f[0:n, t, 0:1], w1[0:n, t:t + 1], ALU.is_equal, ALU.mult)
                eng.tensor_scalar(logit[0:n, t, :], iota[0:n, 0:NE], top_f[0:n, t, 0:1], None, ALU.is_equal)
                eng.tensor_scalar(chosen[0:n, t, :], iota[0:n, 0:NE], top_f[0:n, t, 1:2], None, ALU.is_equal)
                link(eng.tensor_scalar(gate_tok[0:n, t, :], iota[0:n, 0:NE], top_f[0:n, t, 1:2], w2[0:n, t:t + 1],
                                       ALU.is_equal, ALU.mult))
                eng.tensor_tensor(gate_tok[0:n, t, :], gate_tok[0:n, t, :], hit[0:n, t, :], ALU.add)
                last = eng.tensor_tensor(chosen[0:n, t, :], chosen[0:n, t, :], logit[0:n, t, :], ALU.add)
            last.then_inc(S["gates_ready"], 1)
            eng.wait_ge(S["gates_ready"], 1)
            eng.wait_ge(S["count_done"], 1)
            for t in range(TT):
                eng.tensor_copy(pos[0:TOK[t], t, :], pb[5][0:TOK[t], t * NE:(t + 1) * NE])
            link(eng.tensor_reduce(w1[:, 7:8], pb[5][:, TT * NE:(TT + 1) * NE], AX.X, ALU.max))
            eng.tensor_copy(most[:], w1[:, 7:8]).then_inc(S["most_ready"], 1)
            eng.wait_ge(S["most_ready"], 1)
            busiest = eng.value_load(most[0:1, 0:1], min_val=0, max_val=T)
            with eng.If(busiest > cap):
                eng.nop().then_inc(S["down_kept"], 1)
                eng.wait_ge(S["gbc_kept"], NE)
                with eng.Fori(0, NE) as it:
                    for n in range(FEC):
                        eng.wait_ge(S["pair_done"], it * FEC + (n + 1))
                        eng.tensor_tensor(gated[:, n % 2, :], pb[2 * (n % 2) + 1][:, 0:T], gate_bc[:, it, :],
                                          ALU.mult).then_inc(S["gated_ready"], 1)
                        eng.wait_ge(S["gated_ready"], it * FEC + (n + 1))
                        eng.wait_ge(S["pair_silu"], it * FEC + (n + 1))
                        eng.tensor_tensor(act_m[:, n, :], silu_m[:, n % 2, :], gated[:, n % 2, :],
                                          ALU.mult).then_inc(S["pair_kept"], 1)
                        if n % 4 == 3:
                            eng.nop().then_inc(S["lo_ready"], 4)
                            eng.nop().then_inc(S["lo_ready"], 4)
                    for n in range(56):
                        eng.wait_ge(S["down_done"], it * 56 + (n + 1))
                        eng.wait_ge(S["down_kept"], it * 56 + (n + 1))
                        add_to_x(pb[n % 4], n % 8, GATE[FFN1], S["down_part"], it * 56 + (n + 1)).then_inc(S["down_kept"], 1)
                        if n % 8 == 7:
                            eng.nop().then_inc(S["lo_ready"], 4)
                eng.wait_ge(S["down_kept"], NE * 56 + 1)
            with eng.Else():
                eng.nop().then_inc(S["added"], 1)
                for k in range(KC):
                    for t in range(TT):
                        n = TOK[t]
                        to = tok_lo[0:n, t, k * P:(k + 1) * P]
                        eng.wait_ge(S["htok_hi"], TT * k + TT)
                        eng.tensor_tensor(to, pb[6 + k % 2][0:n, t * P:(t + 1) * P], tok_hi[0:n, t, k * P:(k + 1) * P],
                                          ALU.subtract).then_inc(S["htok_lo"], 1)
                for e in range(NE):
                    if e >= 2:
                        eng.wait_ge(S["put_turned"], e - 1)
                    for t in range(TT):
                        n = TOK[t]
                        last = eng.tensor_scalar(put_tok[0:n, e % 2, t, :], iota[0:n, :], pos[0:n, t, e:e + 1],
                                                 gate_tok[0:n, t, e:e + 1], ALU.is_equal, ALU.mult)
                    last.then_inc(S["put_ready"], 1)
                    for t in range(TT):
                        n = TOK[t]
                        last = eng.tensor_scalar(pick[0:n, e, t, :], iota[0:n, :], pos[0:n, t, e:e + 1],
                                                 chosen[0:n, t, e:e + 1], ALU.is_equal, ALU.mult)
                    last.then_inc(S["pick_ready"], 1)
                eng.memset(pick[:, NE, :, :].bitcast(F32), 0.0).then_inc(S["pick_ready"], 1)

                def keep_gathered(done):
                    for a in range(2):
                        eng.wait_ge(S["xe_hi_ready"], done + (a + 1))
                        eng.tensor_tensor(xe_lo[:, 4 * a:4 * a + 4, :], pb[7 - 3 * a].rearrange("p (k c) -> p k c", k=4),
                                          xe_hi[:, 4 * a:4 * a + 4, :], ALU.subtract).then_inc(S["xe_lo_ready"], 1)

                keep_gathered(0)
                with eng.Fori(0, NE) as it:
                    for j in range(4 * PER_E):
                        n = NU + j
                        kind = "up" if j < 56 else "down"
                        eng.wait_ge(S["hi_ready"], it * (4 * PER_E) + (n + 1))
                        eng.tensor_tensor(unit(w_lo, kind, n), quarter(ring[(BASE + j // 4) % RING], kind, j % 4),
                                          unit(w_hi, kind, n), ALU.subtract).then_inc(S["lo_ready"], 1)
                        if j % 8 == 3 and 11 <= j <= 59:
                            p = (j - 11) // 8
                            eng.wait_ge(S["unit_used"], it * (4 * PER_E) + (NU + 8 * p + 8))
                            eng.wait_ge(S["e_silu"], it * 7 + (p + 1))
                            if p >= 1:
                                eng.wait_ge(S["turned"], it * 7 + p)
                            eng.tensor_tensor(act_e[:], silu_e[:], pb[2 * (p % 2) + 1], ALU.mult).then_inc(S["gate_up_kept"], 1)
                        if j % 8 == 7 and 15 <= j <= 63:
                            p = (j - 15) // 8
                            eng.wait_ge(S["at_hi_ready"], it * 7 + (p + 1))
                            eng.tensor_tensor(at_lo[:, 4 * p:4 * p + 4, :],
                                              pb[4 if p % 2 == 0 else 7].rearrange("p (k c) -> p k c", k=4),
                                              at_hi[:, 4 * p:4 * p + 4, :], ALU.subtract).then_inc(S["at_lo_ready"], 1)
                        if j == 79:
                            keep_gathered(it * 2 + 2)
                    for k in range(KC):
                        eng.wait_ge(S["scattered"], it * 8 + (k + 1))
                        add_to_x(pb[k % 4], k, GATE[FFN1], S["down_part"], it * 8 + (k + 1)).then_inc(S["added"], 1)
                eng.wait_ge(S["added"], NE * 8 + 1)
            eng.nop().then_inc(S["experts_done"], 1)
            norm(FINAL)


_OUTS = [(1, TP, D), (NB, 1, D), (1, TP, SH, SD), (1, TP, SH, SD), (1, 1, GH, DK, DV), (NB, 1, SH, SD), (NB, 1, SH, SD),
         (1, NB, GH, DK, DV)]


def kernel(**inputs):
    import numpy as _np
    import concourse.bacc as _bacc
    from concourse import mybir as _mybir
    from concourse.bass_utils import run_bass_kernel_spmd as _run

    nc = _bacc.Bacc("TRN2", target_bir_lowering=False, num_devices=1)
    arrays, ins = {}, {}
    for name in inputs:
        a = _np.ascontiguousarray(inputs[name])
        arrays[f"in_{name}"] = a
        ins[name] = nc.dram_tensor(f"in_{name}", a.shape, _mybir.dt.from_np(a.dtype), kind="ExternalInput").ap()
    outs = [nc.dram_tensor(f"out_{i}", s, F32, kind="ExternalOutput").ap() for i, s in enumerate(_OUTS)]
    build(nc, ins, outs)
    r = _run(nc, [arrays], core_ids=[0])
    return tuple(r.results[0][f"out_{i}"] for i in range(len(_OUTS)))
```

```python
from contextlib import ExitStack

import concourse.bass as bass
from concourse import mybir

ALU = mybir.AluOpType
ACT = mybir.ActivationFunctionType
AX = mybir.AxisListType
F32 = mybir.dt.float32
F32R = mybir.dt.float32r
U32 = mybir.dt.uint32
I32 = mybir.dt.int32

P = 128
D = 1024
KC = D // P
TP = 256
NB = 8
T = TP + NB
TT = 3
TOK = [P, P, NB]
NC9 = 1 + NB
LO_ROW = 32
CR = LO_ROW + NC9
GH, DK, DV, C = 4, 128, 256, 64
NCH = TP // C
HALF = C // 2
GR = 16
SH, SD = 16, 64
PAGES = 2
FF, FE, NE = 2816, 3584, 8
FFC, FEC = FF // P, FE // P
EPS = 1e-6
EXP_CAP = 43.0
S0 = 3
RING = 3
UNITS = 4
QUART = 1024
AHEAD = UNITS - 1
CAP = 128
SCATTER_AT, ADD_AT, PUT_AT = 4, 8, 32
TILE = 4096
MIX0, FFN0, KV, MIX1, FFN1, FINAL = range(6)
IN_GLA, IN_GLA_OUT, IN_FFN, IN_KV, IN_Q, IN_SB_OUT = range(6)
IN_OF = {FFN0: IN_FFN, KV: IN_KV, MIX1: IN_Q}
SHORT, SHORT_IN = list(IN_OF), list(IN_OF.values())
LONG_NO = {MIX0: 0, FFN1: 1, FINAL: 2}
ROOT_NO = {MIX0: 0, FFN0: 1, KV: 2, FFN1: 3, FINAL: 4}
SHIFT = {MIX0: 0, FFN0: 24, KV: 96, MIX1: 48, FFN1: 72, FINAL: 112}
SCALE = {MIX0: 8, FFN0: 32, KV: 104, MIX1: 56, FFN1: 80, FINAL: 120}
GAIN = {MIX0: 0, FFN0: 16, KV: 32, MIX1: 8, FFN1: 24, FINAL: 40}
GATE = {MIX0: 16, FFN0: 40, MIX1: 64, FFN1: 88}
GLA_GAIN, GLA_BIAS, VEC_B = 48, 50, 54
ADA_ORDER = [*range(12), *range(24, 28), *range(12, 24), *range(28, 32)]
ADA_GROUPS = ((0, (0, 1)), (4, (4, 5)), (9, (0, 1)), (20, (4, 5)), (28, (2, 3)))
ADA_STARTS = [start for start, _ in ADA_GROUPS]
ADA_BANKS = [[banks for start, banks in ADA_GROUPS if start <= i][-1][i % 2] for i in range(len(ADA_ORDER))]
ADA_NEEDED = {MIX0: 4, FFN0: 12, KV: 16, MIX1: 20, FFN1: 28, FINAL: 32}
STREAM = ([("ada", i) for i in range(4)] + [("gla_in", i) for i in range(6)] + [("ada", i) for i in range(4, 20)]
          + [("gla_out", i) for i in range(2)]
          + [t for i in range(11) for t in ([("ffn_up", i)] + ([("ada", 19 + i)] if 1 <= i <= 8 else []))]
          + [("ffn_down", i) for i in range(6)]
          + [("kv", i) for i in range(4)] + [("sb_q", i) for i in range(2)] + [("k_cache", i) for i in range(4)]
          + [("v_cache", i) for i in range(4)] + [("sb_out", i) for i in range(2)]
          + [("ada", i) for i in range(28, 32)])
TILE_AT = {k: n for n, k in enumerate(STREAM)}
BASE = len(STREAM)
PER_E = 21
WORK = 13 * 1024 + 96
SPLIT = [t for t in STREAM if t[0] not in ("k_cache", "v_cache")]
UNIT_AT = {t: 4 * n for n, t in enumerate(SPLIT)}
LATE = range(UNIT_AT["sb_out", 0], UNIT_AT["sb_out", 0] + AHEAD)
NU = 4 * len(SPLIT)
BLOCKS = ([("gla_in", i) for i in range(24)] + [("gla_out", i) for i in range(8)] + [("ffn_up", i) for i in range(44)]
          + [("ffn_down", i) for i in range(48)] + [("kv", i) for i in range(16)] + [("sb_q", i) for i in range(8)]
          + [("sb_out", i) for i in range(8)])
BLOCK_AT = {k: n for n, k in enumerate(BLOCKS)}
BY_ACT = ("gla_in", "kv", "sb_q")


def build(nc, A, O, cap=CAP):
    y_prompt, y_sample, k_prompt, v_prompt, gla_prompt, k_sample, v_sample, gla_sample = O
    ctx = ExitStack()
    with ctx:
        def sb(name, shape, dt=F32):
            return ctx.enter_context(nc.sbuf_tensor(name, shape, dt))

        def sem(name):
            return ctx.enter_context(nc.semaphore(name))

        ring = [sb(f"ring{i}", [P, TILE]) for i in range(RING)]
        x = sb("x", [P, KC, T])
        h = sb("h", [P, KC, T])
        w_hi = [sb(f"w_hi{i}", [P, QUART], F32R) for i in range(UNITS)]
        w_lo = [sb(f"w_lo{i}", [P, QUART], F32R) for i in range(UNITS)]
        mod = sb("mod", [P, P, NC9])
        gain = sb("gain", [P, 6, KC, NC9])
        vec_a = sb("vec_a", [P, P])
        vec_b = sb("vec_b", [P, VEC_B])
        rstd = sb("rstd", [P, T])
        ea = sb("ea", [P, GH, NB])
        top_i = sb("top_i", [P, TT, 8], U32)
        most = sb("most", [P, 1], I32)
        w_router = sb("w_router", [P, KC, NE])
        sb_bias = sb("sb_bias", [P, SH])
        router_bias = sb("router_bias", [P, NE])
        ident = sb("ident", [P, P])
        ones = sb("ones", [P, P])
        after = sb("after", [P, P])
        before = sb("before", [P, P])
        not_before = sb("not_before", [P, P])
        upto = sb("upto", [C, C])
        sel_to = sb("sel_to", [SH, NB, NB])
        iota = sb("iota", [P, P])
        tmp8 = sb("tmp8", [P, KC, NB])
        c_split = sb("c_split", [P, KC, CR + 1], F32R)
        ada_row = sb("ada_row", [CR, 2, 512])
        psum = ctx.enter_context(nc.psum_tensor("psum", [P, 8 * 512], F32))
        pb = [psum[:, i * 512:(i + 1) * 512] for i in range(8)]

        stages = ctx.enter_context(ExitStack())

        def st_sb(stage, name, shape, dt=F32):
            return stage.enter_context(nc.sbuf_tensor(name, shape, dt))

        hh = st_sb(stages, "hh", [P, KC, T], F32R)
        hl = st_sb(stages, "hl", [P, KC, T], F32R)

        stage = ExitStack()
        big = st_sb(stage, "big", [P, 24, T])
        work = st_sb(stage, "work", [P, WORK])
        stage.close()

        def piece(at, shape, work=work):
            n = 1
            for s in shape[1:]:
                n *= s
            v = work[0:shape[0], at:at + n]
            if len(shape) == 3:
                v = v.rearrange("p (a b) -> p a b", a=shape[1])
            if len(shape) == 4:
                v = v.rearrange("p (a b c) -> p a b c", a=shape[1], b=shape[2])
            return v, at + n

        crow, at = piece(0, [NC9, D])
        csilu, at = piece(at, [NC9, D])
        at = 0
        la, at = piece(at, [P, GH, T])
        orstd = la
        t_abs, at = piece(at, [P, GH, T])
        cum_a, _ = piece(GH * T, [P, 32, HALF])
        ke, _ = piece(GH * T, [P, GH, TP])
        cum, at = piece(at, [P, 32, HALF])
        s0 = [piece(at + i * GH * DV, [P, GH, DV])[0] for i in range(S0)]
        qd, at = piece(at, [P, 32, HALF])
        kd, at = piece(at, [P, 32, HALF])
        qo, at = piece(at, [P, 16, HALF])
        ko, at = piece(at, [P, 16, HALF])
        qe, at = piece(at, [P, GH, TP])
        dec, at = piece(at, [P, 16])
        w_gate2, _ = piece(at, [GR, GH * DK])
        wr, _ = piece(at + GH * DK, [P, KC, GR])
        vs_tok, _ = piece(at, [NB, D])
        st, at = piece(at, [C, 16, C])
        rT, _ = piece(at, [GR, T])
        vtok = []
        for i in range(2):
            v, at = piece(at, [C, D])
            vtok.append(v)
        ktok, at = piece(at, [C, 2 * GH * DK])
        state = []
        for i in range(2):
            v, at = piece(at, [P, GH, DV])
            state.append(v)
        assert at <= WORK, at
        xtok = big[:, :, :].rearrange("p a b -> p (a b)")[:, 0:TT * D].rearrange("p (t d) -> p t d", t=TT)

        stage = ExitStack()
        act_hi = st_sb(stage, "act_hi", [P, FFC, T], F32R)
        act_lo = st_sb(stage, "act_lo", [P, FFC, T], F32R)
        silu_a = st_sb(stage, "silu_a", [P, 2, T])
        act32 = st_sb(stage, "act32", [P, 2, T])
        stage.close()

        stage = ExitStack()
        kvq = st_sb(stage, "kvq", [P, 24, T])
        work3 = st_sb(stage, "work3", [P, WORK])
        stage.close()
        kvtok, at = piece(0, [P, TT, 2 * D], work3)
        z_buf, at = piece(at, [P, 3, 768], work3)
        l_buf, at = piece(at, [P, 3, 768], work3)
        zs, at = piece(at, [P, PAGES, NB * SH], work3)
        ls, at = piece(at, [P, PAGES, NB * SH], work3)
        prod, _ = piece(at, [P, D], work3)
        prod1 = [piece(TT * 2 * D + i * D, [P, D], work3)[0] for i in range(2)]
        q_rows = [piece(TT * 2 * D + (2 + i) * D, [P, D], work3)[0] for i in range(2)]
        os_row, at = piece(at, [SH, D], work3)
        qs_tok, at = piece(at, [NB, D], work3)
        os_tok = qs_tok
        assert at <= WORK, at
        stages.close()

        stage = ExitStack()
        gate_tok = st_sb(stage, "gate_tok", [P, TT, NE])
        chosen = st_sb(stage, "chosen", [P, TT, NE])
        pos = st_sb(stage, "pos", [P, TT, NE])
        logit = st_sb(stage, "logit", [P, TT, NE])
        top = st_sb(stage, "top", [P, TT, 8])
        hit = st_sb(stage, "hit", [P, TT, NE])
        top_f = st_sb(stage, "top_f", [P, TT, 8])
        e2 = st_sb(stage, "e2", [P, 8])
        w1 = st_sb(stage, "w1", [P, 8])
        w2 = st_sb(stage, "w2", [P, 8])
        gathered = ExitStack()
        tok_hi = st_sb(gathered, "tok_hi", [P, TT, D], F32R)
        tok_lo = st_sb(gathered, "tok_lo", [P, TT, D], F32R)
        pick = st_sb(gathered, "pick", [P, TT, CAP], F32R)
        put_tok = st_sb(gathered, "put_tok", [P, TT, CAP])
        put = st_sb(gathered, "put", [CAP, T])
        xe_hi = st_sb(gathered, "xe_hi", [P, KC, CAP], F32R)
        xe_lo = st_sb(gathered, "xe_lo", [P, KC, CAP], F32R)
        at_hi = st_sb(gathered, "at_hi", [P, FEC, CAP], F32R)
        at_lo = st_sb(gathered, "at_lo", [P, FEC, CAP], F32R)
        silu_e = st_sb(gathered, "silu_e", [CAP, 512])
        act_e = st_sb(gathered, "act_e", [CAP, 512])
        y_e = st_sb(gathered, "y_e", [CAP, D])
        gathered.close()
        gate_bc = st_sb(stage, "gate_bc", [P, NE, T])
        gateT = st_sb(stage, "gateT", [NE, T])
        silu_m = st_sb(stage, "silu_m", [P, 2, T])
        gated = st_sb(stage, "gated", [P, 2, T])
        act_m = st_sb(stage, "act_m", [P, FEC, T])
        stage.close()
        stage = ExitStack()
        ytok = st_sb(stage, "ytok", [P, TT, D])
        stage.close()

        ADA_C, ADA_S, ADA_F = (4 * start for start in ADA_STARTS[1:4])

        Q_BANKS = (0, 2, 6)

        def sel(b):
            return ident[0:NB, b:b + 1].to_broadcast([NB, P])

        S = {}

        def named(*names):
            for n in names:
                S[n] = sem(n)

        named("consts", "c_zero", "small_loaded", "c_loaded", "x_loaded", "vec_turned", "vec_kept",
              "c_silu", "c_turned", "c_hi", "c_kept",
              "x_turned", "x_kept", "hi_ready", "lo_ready", "unit_used", "ada_copied", "ada_turned", "ada_part",
              "ada_kept", "gains_ready", "squared", "ss_done", "ms_ready", "root_ready", "scaled", "h_ready", "hs_ready",
              "hh_ready", "hsh_ready", "hsl_ready", "hl_ready", "kept_act", "kept_dve", "silu_done", "act_step", "dve_step",
              "part_added",
              "r_done", "r_kept", "out_gates", "gate_done", "log_sig", "args_ready", "exps_ready", "decayed",
              "scores_done", "scores_kept",
              "v_turned", "v_kept", "o_done", "o_kept", "u_done", "state_ready", "vs_turned", "vs_kept", "vbc_done",
              "s_updated", *(f"s0_{what}{i}" for i in range(S0) for what in ("loaded", "stored")),
              "os_done", "os_kept", "osq_ready",
              "oss_done", "oms_ready", "oroot_ready", "o_ready", "state_stored", "act_ready", "act_hi_ready", "kv_turned",
              "kv_kept", "kv_stored", "qs_turned", "qs_kept", "qbc_done", "z_s_ready",
              "prod0_ready", "q_kept", "prod1_ready", "z_done", "z_ready", "soft_ready",
              "l_ready", "rc_done", "arg_ready", "p_exp", "p_ready", "pv_done", "pv_kept", "rcs_done", "args_s",
              "exps_s", "opv_done", "own_ready", "ot_done", "ot_kept", "otT_done", "otT_kept", "logits_done",
              "gates_exp", "gates_exp_done", "gates_ready", "count_done", "most_ready", "htok_turned", "htok_hi",
              "htok_lo", "pick_ready", "put_ready", "put_turned", "put_kept", "gather_done", "rows_kept",
              "xe_turned", "xe_hi_ready",
              "xe_lo_ready", "gate_up_kept", "e_silu", "turned", "at_hi_ready", "at_lo_ready", "y_e_kept",
              "scattered", "added", "down_part", "gateT_done", "gateT_kept", "gbc_done", "gbc_kept", "gate_half_done",
              "pair_done", "pair_silu", "pair_kept", "gated_ready", "down_done", "down_kept", "experts_done",
              "y_turned", "y_kept", "y_stored")
        loaded = [sem(f"ring_loaded{i}") for i in range(RING)]

        lands, count = [], [0] * RING
        for n, (kind, i) in enumerate(STREAM):
            count[n % RING] += 64 if kind in ("k_cache", "v_cache") else 32 if kind == "ffn_up" else 16
            lands.append(count[n % RING])
        LAND0 = list(count)

        def read_out(kind, i):
            if kind == "k_cache":
                return S["z_s_ready"], 2 * i + 2
            if kind == "v_cache":
                return S["opv_done"], 2 * i + 2
            return S["lo_ready"], UNIT_AT[kind, i] + 4

        def quarter(raw, kind, j, ks=4):
            if kind in ("ada", "up"):
                return raw[:].rearrange("p (k c) -> p k c", c=512)[:, 2 * j:2 * j + 2, :]
            if kind == "down":
                return raw[:, j * D:(j + 1) * D].unsqueeze(1)
            if kind == "ffn_up":
                return raw[:].rearrange("p (k s c) -> p k s c", k=KC, s=2)[:, :, j % 2, j // 2 * P:(j // 2 + 1) * P]
            if kind == "ffn_down":
                return raw[:, 0:ks * D].rearrange("p (k c) -> p k c", k=ks)[:, :, j * 256:(j + 1) * 256]
            return raw[:].rearrange("p (k c) -> p k c", k=KC)[:, :, j * P:(j + 1) * P]

        def unit(v, kind, n, ks=4):
            k, c = {"ada": (2, 512), "up": (2, 512), "down": (1, D), "ffn_down": (ks, 256)}.get(kind, (KC, P))
            return v[n % UNITS][:, 0:k * c].rearrange("p (k c) -> p k c", k=k)

        def chunks_of(kind, i):
            return min(4, FFC - 4 * i) if kind == "ffn_down" else 4

        empt, a_n, d_n = [], 0, 0
        for kind, i in BLOCKS:
            if kind in BY_ACT:
                a_n += 1
                empt.append(("kept_act", a_n))
            elif kind == "ffn_up":
                d_n += i % 2
                empt.append(("kept_dve", d_n + 1 - i % 2))
            else:
                d_n += 1
                empt.append(("kept_dve", d_n))

        block = ctx.enter_context(nc.Block())

        def slot(kind, i):
            return ring[TILE_AT[kind, i] % RING]

        def landed(eng, kind, i):
            n = TILE_AT[kind, i]
            eng.wait_ge(loaded[n % RING], lands[n])

        def expert_landed(eng, it, j):
            n = (BASE + j) % RING
            eng.wait_ge(loaded[n], it * (PER_E // RING * 16) + (LAND0[n] + 16 * (j // RING + 1)))

        def cols8(tile, n=512):
            return tile[:, 0:KC * n].rearrange("p (k c) -> p k c", k=KC)

        def rows(w, lo, n, c0=0, c1=D):
            return w[lo:lo + n * P, c0:c1].rearrange("(k p) c -> p k c", p=P)

        @block.sync
        def _(eng):
            eng.dma_start(crow[0:1, :], A["c_prompt"]).then_inc(S["c_loaded"], 16)
            eng.dma_start(crow[1:NC9, :], A["c_sample"]).then_inc(S["c_loaded"], 16)
            pages = {}
            for n, (kind, i) in enumerate(STREAM):
                dst = ring[n % RING]
                if (kind, i) == ("ffn_down", 0):
                    for b in range(NB):
                        for page in range(PAGES):
                            pages[b, page] = eng.value_load(A["page_table"][b:b + 1, page:page + 1], min_val=0,
                                                            max_val=A["cache_k"].shape[0] - 1)
                if n >= RING:
                    eng.wait_ge(*read_out(*STREAM[n - RING]))
                if kind in ("k_cache", "v_cache"):
                    cache = A["cache_k" if kind == "k_cache" else "cache_v"].rearrange("n s h d -> n s (h d)")
                    for j in range(4):
                        b, page = 2 * i + j // 2, j % 2
                        eng.dma_start(dst[:, j * D:(j + 1) * D], cache[pages[b, page]]).then_inc(loaded[n % RING], 16)
                    continue
                c = i * 512
                if kind == "ada":
                    o = ADA_ORDER[i]
                    w, c = ((A["ada_w"][o // 12], (o % 12) * 512) if o < 24 else
                            (A["kv_ada_w"], (o - 24) * 512) if o < 28 else (A["final_ada_w"], (o - 28) * 512))
                    eng.dma_start(cols8(dst), rows(w, 0, KC, c, c + 512)).then_inc(loaded[n % RING], 16)
                elif kind == "ffn_up":
                    w = A["ffn_w_gate_up"][0].rearrange("(k p) (s c) -> p k s c", p=P, s=2)[:, :, :, i * 256:(i + 1) * 256]
                    d4 = dst[:].rearrange("p (k s c) -> p k s c", k=KC, s=2)
                    for s in range(2):
                        eng.dma_start(d4[:, :, s, :], w[:, :, s, :]).then_inc(loaded[n % RING], 16)
                elif kind == "ffn_down":
                    k = min(4, FFC - 4 * i)
                    eng.dma_start(dst[:, 0:k * D].rearrange("p (k c) -> p k c", k=k),
                                  rows(A["ffn_w_down"][0], i * 512, k)).then_inc(loaded[n % RING], 16)
                else:
                    w = {"gla_in": A["gla_w_in"][0], "gla_out": A["gla_w_out"][0], "kv": A["kv_w"],
                         "sb_q": A["sb_w_q"][0], "sb_out": A["sb_w_out"][0]}[kind]
                    eng.dma_start(cols8(dst), rows(w, 0, KC, c, c + 512)).then_inc(loaded[n % RING], 16)

            up, down = A["moe_w_gate_up"][0], A["moe_w_down"][0]

            def load(j, it):
                e, i = j // PER_E, j % PER_E
                dst = ring[(BASE + j) % RING]
                expert = it + e
                if i < 14:
                    c = (i % 2) * FE + (i // 2) * 512
                    src, to = up[expert, :, c:c + 512].rearrange("(k p) c -> p k c", p=P), cols8(dst)
                else:
                    lo = (i - 14) * 512
                    src = down[expert, lo:lo + 512, :].rearrange("(k p) c -> p k c", p=P)
                    to = dst[:].rearrange("p (k c) -> p k c", k=4)
                return to, src

            for j in range(RING):
                eng.wait_ge(*read_out(*STREAM[BASE - RING + j]))
                to, src = load(j, 0)
                eng.dma_start(to, src).then_inc(loaded[(BASE + j) % RING], 16)
            with eng.Fori(0, NE - 1) as it:
                for j in range(RING, PER_E + RING):
                    to, src = load(j, it)
                    value = eng.snap(it * (4 * PER_E) + (NU + 4 * (j - RING) + 4))
                    eng.wait_ge(S["lo_ready"], value)
                    eng.dma_start(to, src).then_inc(loaded[(BASE + j) % RING], 16)
            for j in range(RING, PER_E):
                to, src = load(j, NE - 1)
                eng.wait_ge(S["lo_ready"], (NE - 1) * 4 * PER_E + NU + 4 * (j - RING) + 4)
                eng.dma_start(to, src).then_inc(loaded[(BASE + j) % RING], 16)

        @block.gpsimd
        def _(eng):
            eng.memset(ones[:], 1.0).then_inc(S["consts"], 1)
            eng.memset(ident[:], 0.0).then_inc(S["consts"], 1)
            eng.memset(sel_to[:], 0.0).then_inc(S["consts"], 1)
            eng.memset(not_before[:], -1.0).then_inc(S["consts"], 1)
            eng.wait_ge(S["consts"], 4)
            eng.affine_select(out=ident[:], in_=ident[:], compare_op=ALU.not_equal, fill=1.0, base=0,
                              pattern=[[-1, P]], channel_multiplier=1).then_inc(S["consts"], 1)
            eng.affine_select(out=after[:], in_=ones[:], compare_op=ALU.is_ge, fill=0.0, base=0,
                              pattern=[[-1, P]], channel_multiplier=1).then_inc(S["consts"], 1)
            eng.affine_select(out=before[:], in_=ones[:], compare_op=ALU.is_gt, fill=0.0, base=0,
                              pattern=[[1, P]], channel_multiplier=-1).then_inc(S["consts"], 1)
            eng.affine_select(out=not_before[:], in_=not_before[:], compare_op=ALU.is_gt, fill=0.0, base=0,
                              pattern=[[1, P]], channel_multiplier=-1).then_inc(S["consts"], 1)
            eng.affine_select(out=upto[:], in_=ones[0:C, 0:C], compare_op=ALU.is_ge, fill=0.0, base=0,
                              pattern=[[1, C]], channel_multiplier=-1).then_inc(S["consts"], 1)
            eng.affine_select(out=sel_to[:], in_=sel_to[:], compare_op=ALU.not_equal, fill=1.0, base=0,
                              pattern=[[-1, NB], [1, NB]], channel_multiplier=0).then_inc(S["consts"], 1)
            eng.iota(iota[:], pattern=[[1, P]], base=0, channel_multiplier=0,
                     allow_small_or_imprecise_dtypes=True).then_inc(S["consts"], 1)
            for w, lo in ((A["ada_b"].rearrange("l (c p) -> (l c) p", p=P), 0),
                          (A["kv_ada_b"].rearrange("(c p) -> c p", p=P), 96),
                          (A["final_ada_b"].rearrange("(c p) -> c p", p=P), 112)):
                eng.dma_start(h[lo:lo + w.shape[0], 0, 0:P], w).then_inc(S["small_loaded"], 16)
            for w, lo in ((A["norm_mix"].rearrange("l (c p) -> (l c) p", p=P), 0),
                          (A["norm_ffn"].rearrange("l (c p) -> (l c) p", p=P), 16),
                          (A["kv_norm"].rearrange("(c p) -> c p", p=P), 32),
                          (A["final_norm"].rearrange("(c p) -> c p", p=P), 40),
                          (A["gla_norm"].rearrange("l (c p) -> (l c) p", p=P), GLA_GAIN),
                          (A["gla_b_gate"].rearrange("l (c p) -> (l c) p", p=P), GLA_BIAS)):
                eng.dma_start(h[lo:lo + w.shape[0], 1, 0:P], w).then_inc(S["small_loaded"], 16)
            eng.dma_start(wr[:], rows(A["gla_w_in"][0], 0, KC, 3072, 3088)).then_inc(S["small_loaded"], 16)
            eng.dma_start(w_router[:], rows(A["moe_w_router"][0], 0, KC, 0, NE)).then_inc(S["small_loaded"], 16)
            eng.dma_start(w_gate2, A["gla_w_gate2"][0]).then_inc(S["small_loaded"], 16)
            eng.dma_start(sb_bias[:], A["sb_b"][0].partition_broadcast(P)).then_inc(S["small_loaded"], 16)
            eng.dma_start(router_bias[:], A["moe_b_router"][0].partition_broadcast(P)).then_inc(S["small_loaded"], 16)
            src = A["state_gla"][0].rearrange("b h k v -> b k h v")
            dst = gla_sample[0].rearrange("b h k v -> b k h v")
            eng.wait_ge(S["scores_done"], 1)
            for b in range(NB + S0 - 1):
                if b < NB:
                    if b >= S0:
                        eng.wait_ge(S[f"s0_stored{b % S0}"], 16 * (b // S0))
                        eng.wait_ge(S["os_done"], b - S0 + 1)
                    eng.dma_start(s0[b % S0], src[b]).then_inc(S[f"s0_loaded{b % S0}"], 16)
                done = b - S0 + 1
                if done >= 0:
                    eng.wait_ge(S["s_updated"], done + 1)
                    eng.dma_start(dst[done], s0[done % S0]).then_inc(S[f"s0_stored{done % S0}"], 16)
            eng.wait_ge(S["state_ready"], NCH)
            eng.dma_start(gla_prompt[0, 0].rearrange("h k v -> k h v"), state[(NCH - 1) % 2]).then_inc(S["state_stored"], 16)
            for b in range(NB):
                if b % 2 == 0:
                    landed(eng, "k_cache", b // 2)
                eng.wait_ge(S["q_kept"], b + 1)
                if b >= 2:
                    eng.wait_ge(S["z_s_ready"], b - 1)
                lo = ((b % 2) * 2 + 1) * D
                eng.tensor_tensor(prod1[b % 2], slot("k_cache", b // 2)[:, lo:lo + D],
                                  q_rows[b % 2], ALU.mult).then_inc(S["prod1_ready"], 1)
            eng.wait_ge(S["kv_kept"], 12)
            for t, outs in ((0, (k_prompt, v_prompt)), (1, (k_prompt, v_prompt)), (2, (k_sample, v_sample))):
                for s, o in enumerate(outs):
                    flat = o.rearrange("b s h d -> (b s) (h d)")
                    lo = t * P if t < 2 else 0
                    eng.dma_start(flat[lo:lo + TOK[t], :],
                                  kvtok[0:TOK[t], t, s * D:(s + 1) * D]).then_inc(S["kv_stored"], 16)
            eng.wait_ge(S["most_ready"], 1)
            busiest = eng.value_load(most[0:1, 0:1], min_val=0, max_val=T)
            with eng.If(busiest <= cap):
                for e in range(NE):
                    if e >= 1:
                        eng.wait_ge(S["gather_done"], 2 * e)
                    for t in range(TT):
                        n = TOK[t]
                        last = eng.tensor_scalar(pick[0:n, t, :], iota[0:n, :], pos[0:n, t, e:e + 1],
                                                 chosen[0:n, t, e:e + 1], ALU.is_equal, ALU.mult)
                    last.then_inc(S["pick_ready"], 1)
                    if e >= 1:
                        eng.wait_ge(S["put_turned"], e)
                    for t in range(TT):
                        n = TOK[t]
                        last = eng.tensor_scalar(put_tok[0:n, t, :], iota[0:n, :], pos[0:n, t, e:e + 1],
                                                 gate_tok[0:n, t, e:e + 1], ALU.is_equal, ALU.mult)
                    last.then_inc(S["put_ready"], 1)
                eng.wait_ge(S["gather_done"], 2 * NE)
                eng.memset(pick[:].bitcast(F32), 0.0).then_inc(S["pick_ready"], 1)
            for t in range(TT):
                eng.wait_ge(S["y_kept"], 2 * t + 2)
                dst_y = (y_prompt[0, t * P:(t + 1) * P, :] if t < 2 else y_sample.rearrange("b s d -> (b s) d"))
                eng.dma_start(dst_y, ytok[0:TOK[t], t, :]).then_inc(S["y_stored"], 16)
            for i in range(S0):
                eng.wait_ge(S[f"s0_stored{i}"], 16 * len(range(i, NB, S0)))
            eng.wait_ge(S["state_stored"], 16)
            eng.wait_ge(S["kv_stored"], 16 * 6)
            eng.wait_ge(S["y_stored"], 16 * TT)

        @block.tensor
        def _(eng):
            eng.wait_ge(S["consts"], 11)
            eng.wait_ge(S["c_silu"], 1)
            for k in range(KC):
                last = eng.transpose(pb[5][:, k * 16:k * 16 + NC9], csilu[:, k * P:(k + 1) * P], ident[0:NC9, 0:NC9])
            last.then_inc(S["c_turned"], 1)
            eng.wait_ge(S["x_loaded"], 16 * TT)
            for k in range(KC):
                if k >= 2:
                    eng.wait_ge(S["x_kept"], k - 1)
                for t in range(TT):
                    n = TOK[t]
                    last = eng.transpose(pb[6 + k % 2][:, t * P:t * P + n], xtok[0:n, t, k * P:(k + 1) * P], ident[0:n, 0:n])
                last.then_inc(S["x_turned"], 1)

            def has_unit(n):
                eng.wait_ge(S["lo_ready"], n + 1)

            def ada_turn(i):
                eng.wait_ge(S["ada_copied"], i + 1)
                for j in range(4):
                    last = eng.transpose(pb[ADA_BANKS[i]][:, j * 64:j * 64 + CR], ada_row[:, i % 2, j * P:(j + 1) * P],
                                         ident[0:CR, 0:CR])
                last.then_inc(S["ada_turned"], 1)

            def ada(lo, hi, ends=False):
                for u in range(lo, hi):
                    i, j, n = u // 4, u % 4, UNIT_AT["ada", u // 4] + u % 4
                    if j == 0 and i >= 1 and i in ADA_STARTS:
                        eng.wait_ge(S["ada_kept"], i)
                    elif j == 0 and i >= 2:
                        eng.wait_ge(S["ada_kept"], i - 1)
                    has_unit(n)
                    for k in range(2):
                        c = c_split[:, 2 * j + k, 0:CR]
                        to = pb[ADA_BANKS[i]][0:CR, :]
                        eng.matmul(to, c, unit(w_hi, "ada", n)[:, k, :], start=j + k == 0, stop=False)
                        last = eng.matmul(to, c, unit(w_lo, "ada", n)[:, k, :], start=False, stop=j + k == 4)
                    last.then_inc(S["unit_used"], 1)
                    if j == 1 and i not in ADA_STARTS:
                        ada_turn(i - 1)
                if ends:
                    ada_turn(hi // 4 - 1)

            eng.wait_ge(S["c_kept"], 1)
            ada(0, 4)
            eng.wait_ge(S["small_loaded"], 16 * 14)
            eng.transpose(pb[4][:, 0:P], h[:, 0, 0:P], ident[:])
            eng.transpose(pb[4][:, P:P + VEC_B], h[0:VEC_B, 1, 0:P], ident[0:VEC_B, 0:VEC_B]).then_inc(S["vec_turned"], 1)
            ada(4, 16, ends=True)

            def sum_squares(m):
                for k in range(KC):
                    eng.wait_ge(S["squared"], ROOT_NO[m] * KC + k + 1)
                    last = eng.matmul(pb[7][:, 0:T], ones[:], h[:, k, :], start=k == 0, stop=k == KC - 1)
                last.then_inc(S["ss_done"], 1)

            def free_bank(n):
                if n >= 4:
                    who, value = empt[n - 4]
                    eng.wait_ge(S[who], value)

            def three(to, wh, wl, ah, al, start, stop):
                eng.matmul(to, wh, ah, start=start, stop=False)
                eng.matmul(to, wh, al, start=False, stop=False)
                return eng.matmul(to, wl, ah, start=False, stop=stop)

            def project(kind, n_tiles, m, first=0):
                for i in range(first, n_tiles):
                    for j in range(4):
                        n, u = BLOCK_AT[kind, 4 * i + j], UNIT_AT[kind, i] + j
                        has_unit(u)
                        free_bank(n)
                        wh, wl = unit(w_hi, kind, u), unit(w_lo, kind, u)
                        for k in range(KC):
                            if i == 0 and j == 0:
                                if k == 0 and m in SHORT_IN:
                                    eng.wait_ge(S["hsl_ready"], SHORT_IN.index(m) + 1)
                                eng.wait_ge(S["hl_ready"], m * KC + k + 1)
                            last = three(pb[n % 4][:, 0:T], wh[:, k, :], wl[:, k, :], hh[:, k, :], hl[:, k, :],
                                         k == 0, k == KC - 1)
                        last.then_inc(S["unit_used"], 1)

            def h_is_ready(m):
                eng.wait_ge(S["h_ready"], LONG_NO[m] * KC + KC)
                eng.wait_ge(S["hs_ready"], m + 1)

            sum_squares(MIX0)
            h_is_ready(MIX0)
            for k in range(KC):
                last = eng.matmul(pb[5][0:GR, 0:T], wr[:, k, :], h[:, k, :], start=k == 0, stop=k == KC - 1)
            last.then_inc(S["r_done"], 1)
            project("gla_in", 1, IN_GLA)
            eng.wait_ge(S["r_kept"], 1)
            for g in range(GH):
                last = eng.matmul(pb[4 + g][:, 0:T], w_gate2[:, g * DK:(g + 1) * DK], rT[:], start=True, stop=True)
            last.then_inc(S["gate_done"], 1)
            project("gla_in", 6, IN_GLA, first=1)
            eng.wait_ge(S["decayed"], 4)
            for c in range(NCH):
                for g in range(GH):
                    u, v = g * NCH + c, c * GH + g
                    to = pb[4 + v // 8][:, (v % 8) * C:(v % 8 + 1) * C]
                    for a in range(2):
                        eng.matmul(to[a * HALF:(a + 1) * HALF, a * HALF:(a + 1) * HALF], kd[:, 2 * u + a, :],
                                   qd[:, 2 * u + a, :], start=True, stop=True)
                    last = eng.matmul(to[0:HALF, HALF:C], ko[:, u, :], qo[:, u, :], start=True, stop=True)
            last.then_inc(S["scores_done"], 1)
            eng.wait_ge(S["decayed"], 6)
            eng.wait_ge(S["kept_act"], 24)
            for c in range(NCH):
                if c >= 1:
                    eng.wait_ge(S["v_kept"], 2 * c)
                for j in range(8):
                    eng.transpose(pb[j // 4][0:C, (j % 4) * P:(j % 4 + 1) * P], big[:, 8 + j, c * C:(c + 1) * C], ident[:])
                for g in range(GH):
                    last = eng.transpose(pb[2][0:C, g * DK:(g + 1) * DK], ke[:, g, c * C:(c + 1) * C], ident[:])
                last.then_inc(S["v_turned"], 1)
                if c == 0:
                    eng.wait_ge(S["scores_kept"], 1)
                ada(ADA_C + 4 * c, ADA_C + 4 * c + 2)
                eng.wait_ge(S["v_kept"], 2 * c + 2)
                if c >= 1:
                    eng.wait_ge(S["o_kept"], c)
                    eng.wait_ge(S["state_ready"], c)
                for g in range(GH):
                    for a in range(2):
                        to = pb[3][:, (2 * g + a) * C:(2 * g + a + 1) * C]
                        last = eng.matmul(to, vtok[c % 2][:, g * DV + a * P:g * DV + (a + 1) * P], st[:, c * GH + g, :],
                                          start=True, stop=c == 0)
                        if c > 0:
                            last = eng.matmul(to, state[(c - 1) % 2][:, g, a * P:(a + 1) * P], qe[:, g, c * C:(c + 1) * C],
                                              start=False, stop=True)
                last.then_inc(S["o_done"], 1)
                for g in range(GH):
                    last = eng.matmul(pb[6 + g // 2][:, (g % 2) * DV:(g % 2 + 1) * DV],
                                      ktok[:, (c % 2) * 512 + g * DK:(c % 2) * 512 + (g + 1) * DK],
                                      vtok[c % 2][:, g * DV:(g + 1) * DV], start=True, stop=True)
                last.then_inc(S["u_done"], 1)
                ada(ADA_C + 4 * c + 2, ADA_C + 4 * c + 4)
            ada(32, 36, ends=True)
            eng.wait_ge(S["v_kept"], 2 * NCH)
            for j in range(8):
                last = eng.transpose(pb[j // 4][0:NB, (j % 4) * P:(j % 4 + 1) * P], big[:, 8 + j, TP:T], ident[:])
            last.then_inc(S["vs_turned"], 1)
            eng.wait_ge(S["vs_kept"], 1)
            eng.wait_ge(S["state_ready"], NCH)
            eng.wait_ge(S["o_kept"], NCH)
            eng.wait_ge(S["ada_kept"], 9)
            for b in range(NB + 1):
                if b < NB:
                    if b >= 2:
                        eng.wait_ge(S["s_updated"], b - 1)
                    for a in range(2):
                        last = eng.matmul(pb[4 + 2 * (b % 2) + a], sel(b), vs_tok[:, a * 512:(a + 1) * 512],
                                          start=True, stop=True)
                    last.then_inc(S["vbc_done"], 1)
                ada(ADA_S + 4 * b, ADA_S + 4 * b + 1)
                if b >= 1:
                    eng.wait_ge(S["s_updated"], b)
                    for g in range(GH):
                        for a in range(2):
                            at8 = (2 * g + a) * NB + b - 1
                            last = eng.matmul(pb[3][:, at8:at8 + 1], s0[(b - 1) % S0][:, g, a * P:(a + 1) * P],
                                              big[:, g, TP + b - 1:TP + b], start=True, stop=True)
                    last.then_inc(S["os_done"], 1)
                ada(ADA_S + 4 * b + 1, ADA_S + 4 * b + 4)
            for g in range(GH):
                eng.wait_ge(S["osq_ready"], g + 1)
                for a in range(2):
                    last = eng.matmul(pb[4 + g][:, 0:T], ones[:], big[:, 2 * g + a, :], start=a == 0, stop=a == 1)
            last.then_inc(S["oss_done"], 1)
            ada(72, 80, ends=True)
            eng.wait_ge(S["ada_kept"], 20)
            project("gla_out", 2, IN_GLA_OUT)

            sum_squares(FFN0)
            for i in range(11):
                project("ffn_up", i + 1, IN_FFN, first=i)
                if 1 <= i <= 8:
                    ada(ADA_F + 4 * i - 4, ADA_F + 4 * i, ends=i == 8)
            for i in range(6):
                ks = chunks_of("ffn_down", i)
                if i == 0:
                    eng.wait_ge(S["act_ready"], FFC)
                for j in range(8):
                    n, u = BLOCK_AT["ffn_down", 8 * i + j], UNIT_AT["ffn_down", i] + j // 2
                    if j % 2 == 0:
                        has_unit(u)
                        wh, wl = unit(w_hi, "ffn_down", u, ks), unit(w_lo, "ffn_down", u, ks)
                    free_bank(n)
                    c = j % 2 * P
                    for k in range(ks):
                        last = three(pb[n % 4][:, 0:T], wh[:, k, c:c + P], wl[:, k, c:c + P], act_hi[:, 4 * i + k, :],
                                     act_lo[:, 4 * i + k, :], k == 0, k == ks - 1)
                    if j % 2 == 1:
                        last.then_inc(S["unit_used"], 1)

            sum_squares(KV)
            project("kv", 4, IN_KV)
            project("sb_q", 2, IN_Q)

            def turn_kv(i):
                t, q = i // 4, i % 4
                n = TOK[t]
                if i >= 2:
                    eng.wait_ge(S["kv_kept"], i - 1)
                for j in range(4):
                    last = eng.transpose(pb[4 + i % 2][0:n, j * P:(j + 1) * P], kvq[:, 4 * q + j, t * P:t * P + n], ident[:])
                last.then_inc(S["kv_turned"], 1)

            eng.wait_ge(S["kept_act"], empt[BLOCK_AT["sb_q", 7]][1])
            for j in range(8):
                last = eng.transpose(pb[4 + j // 4][0:NB, (j % 4) * P:(j % 4 + 1) * P], kvq[:, 16 + j, TP:T], ident[:])
            last.then_inc(S["qs_turned"], 1)
            eng.wait_ge(S["qs_kept"], 1)
            for b in range(NB):
                if b >= 3:
                    eng.wait_ge(S["q_kept"], b - 2)
                for a in range(2):
                    last = eng.matmul(pb[Q_BANKS[b % 3] + a], sel(b), qs_tok[:, a * 512:(a + 1) * 512],
                                      start=True, stop=True)
                last.then_inc(S["qbc_done"], 1)
                if 1 <= b <= 6:
                    turn_kv(2 * b - 2)
                    turn_kv(2 * b - 1)

            def z_products(g):
                if g >= 2:
                    eng.wait_ge(S["z_ready"], g - 1)
                for a in range(2):
                    to = pb[2 * (g % 2) + a]
                    k, q = kvq[a * SD:(a + 1) * SD, g, 0:TP], kvq[a * SD:(a + 1) * SD, 16 + g, 0:TP]
                    eng.matmul(to[:, 0:P], k[:, 0:P], q[:, 0:P], start=True, stop=True)
                    eng.matmul(to[:, P:2 * P], k[:, P:TP], q[:, P:TP], start=True, stop=True)
                    last = eng.matmul(to[:, 2 * P:3 * P], k[:, 0:P], q[:, P:TP], start=True, stop=True)
                last.then_inc(S["z_done"], 1)

            def later_sums(g):
                eng.wait_ge(S["l_ready"], g + 1)
                if g >= 1:
                    eng.wait_ge(S["arg_ready"], g)
                lg = l_buf[:, g % 3, :]
                eng.matmul(pb[4], after[:], lg[:, 0:512], start=True, stop=True)
                eng.matmul(pb[5][:, 0:256], after[:], lg[:, 512:768], start=True, stop=False)
                eng.matmul(pb[5][:, 0:256], ones[:], lg[:, 256:512], start=False, stop=True).then_inc(S["rc_done"], 1)

            def values(g):
                eng.wait_ge(S["p_ready"], g + 1)
                if g >= 2:
                    eng.wait_ge(S["pv_kept"], g - 1)
                pg = z_buf[:, g % 3, :]
                for a in range(2):
                    lo = D + (2 * g + a) * SD
                    to = pb[6 + g % 2][a * SD:(a + 1) * SD, :]
                    eng.matmul(to[:, 0:P], kvtok[:, 0, lo:lo + SD], pg[:, a * P:(a + 1) * P], start=True, stop=True)
                    eng.matmul(to[:, P:TP], kvtok[:, 0, lo:lo + SD], pg[:, 512 + a * P:512 + (a + 1) * P],
                               start=True, stop=False)
                    last = eng.matmul(to[:, P:TP], kvtok[:, 1, lo:lo + SD], pg[:, 256 + a * P:256 + (a + 1) * P],
                                      start=False, stop=True)
                last.then_inc(S["pv_done"], 1)

            eng.wait_ge(S["kv_kept"], 12)
            eng.wait_ge(S["z_s_ready"], NB)
            G = SH // 2
            z_products(0)
            z_products(1)
            for g in range(G + 1):
                if g < G:
                    later_sums(g)
                if g >= 1:
                    values(g - 1)
                if g + 2 < G:
                    z_products(g + 2)
            eng.wait_ge(S["l_ready"], G + 1)
            eng.wait_ge(S["arg_ready"], G)
            eng.matmul(pb[4][:, 0:128], after[:], ls[:, 0, :], start=True, stop=False, skip_group_check=True)
            eng.matmul(pb[4][:, 0:128], ones[:], ls[:, 1, :], start=False, stop=True, skip_group_check=True)
            eng.matmul(pb[4][:, 128:256], after[:], ls[:, 1, :], start=True, stop=True).then_inc(S["rcs_done"], 1)
            eng.wait_ge(S["exps_s"], 1)
            eng.wait_ge(S["z_ready"], G)
            eng.wait_ge(S["pv_kept"], G)
            for b in range(NB + 1):
                if b < NB:
                    if b % 2 == 0:
                        landed(eng, "v_cache", b // 2)
                    if b >= 2:
                        eng.wait_ge(S["own_ready"], b - 1)
                    vt = slot("v_cache", b // 2)
                    for a in range(2):
                        for page in range(PAGES):
                            lo = ((b % 2) * 2 + page) * D + a * 512
                            last = eng.matmul(pb[6 * (b % 2) + a][0:SH, :], zs[:, page, b * SH:(b + 1) * SH], vt[:, lo:lo + 512],
                                              start=page == 0, stop=page == 1)
                    last.then_inc(S["opv_done"], 1)
                if b >= 1:
                    eng.wait_ge(S["own_ready"], b)
                    for a in range(2):
                        last = eng.matmul(pb[2 + a][0:NB, :], sel_to[:, b - 1, :], os_row[:, a * 512:(a + 1) * 512],
                                          start=b == 1, stop=b == NB, skip_group_check=True)
                    last.then_inc(S["ot_done"], 1)
            eng.wait_ge(S["ot_kept"], 1)
            eng.wait_ge(S["pv_kept"], G)
            for j in range(8):
                last = eng.transpose(pb[5][:, j * 8:(j + 1) * 8], os_tok[:, j * P:(j + 1) * P], ident[0:NB, 0:NB])
            last.then_inc(S["otT_done"], 1)
            project("sb_out", 2, IN_SB_OUT)

            sum_squares(FFN1)
            eng.wait_ge(S["kept_dve"], empt[-1][1])
            ada(112, 120)
            for t in range(TT):
                if t == 0:
                    h_is_ready(FFN1)
                for k in range(KC):
                    last = eng.matmul(pb[4][0:TOK[t], t * NE:(t + 1) * NE], h[:, k, t * P:t * P + TOK[t]], w_router[:, k, :],
                                      start=k == 0, stop=k == KC - 1)
            last.then_inc(S["logits_done"], 1)
            ada(120, 128, ends=True)
            eng.wait_ge(S["gates_ready"], 1)
            for t in range(TT):
                n = TOK[t]
                to = pb[5][0:n, t * NE:(t + 1) * NE]
                eng.matmul(to, before[0:n, 0:n], chosen[0:n, t, :], start=True, stop=t == 0)
                for s in range(t):
                    eng.matmul(to, ones[:, 0:n], chosen[:, s, :], start=False, stop=s == t - 1)
            for t in range(TT):
                n = TOK[t]
                last = eng.matmul(pb[5][:, TT * NE:(TT + 1) * NE], ones[0:n, :], chosen[0:n, t, :], start=t == 0, stop=t == 2)
            last.then_inc(S["count_done"], 1)
            eng.wait_ge(S["most_ready"], 1)
            busiest = eng.value_load(most[0:1, 0:1], min_val=0, max_val=T)
            with eng.If(busiest > cap):
                for t in range(TT):
                    n = TOK[t]
                    last = eng.transpose(pb[4][0:NE, t * P:t * P + n], gate_tok[0:n, t, :], ident[0:n, 0:n])
                last.then_inc(S["gateT_done"], 1)
                eng.wait_ge(S["gateT_kept"], 1)
                for e in range(NE):
                    if e >= 2:
                        eng.wait_ge(S["gbc_kept"], e - 1)
                    eng.matmul(pb[6 + e % 2][:, 0:T], sel(e), gateT[:], start=True, stop=True).then_inc(S["gbc_done"], 1)
                with eng.Fori(0, NE) as it:
                    for p in range(7):
                        ws = []
                        for s in range(2):
                            expert_landed(eng, it, 2 * p + s)
                            ws.append(cols8(ring[(BASE + 2 * p + s) % RING]))
                        for q in range(4):
                            n = 4 * p + q
                            if n >= 2:
                                eng.wait_ge(S["pair_kept"], it * FEC + (n - 1))
                            else:
                                eng.wait_ge(S["down_kept"], it * 56 + 1)
                            for s in range(2):
                                for k in range(KC):
                                    last = eng.matmul(pb[2 * (n % 2) + s][:, 0:T], ws[s][:, k, q * P:(q + 1) * P], h[:, k, :],
                                                      start=k == 0, stop=k == KC - 1)
                                last.then_inc(S["gate_half_done" if s == 0 else "pair_done"], 1)
                    eng.wait_ge(S["pair_kept"], it * FEC + FEC)
                    for i in range(7):
                        expert_landed(eng, it, 14 + i)
                        w = ring[(BASE + 14 + i) % RING][:].rearrange("p (k c) -> p k c", k=4)
                        for dc in range(8):
                            n = 8 * i + dc
                            if n >= 4:
                                eng.wait_ge(S["down_kept"], it * 56 + (n - 2))
                            for k in range(4):
                                last = eng.matmul(pb[n % 4][:, 0:T], w[:, k, dc * P:(dc + 1) * P], act_m[:, 4 * i + k, :],
                                                  start=k == 0, stop=k == 3)
                            last.then_inc(S["down_done"], 1)
            with eng.Else():
                for i in range(2 * TT):
                    t, a = i // 2, i % 2
                    if i >= 2:
                        eng.wait_ge(S["htok_lo"], i - 1)
                    for j in range(4):
                        last = eng.transpose(pb[7 - 3 * a][0:TOK[t], j * P:(j + 1) * P], h[:, 4 * a + j, t * P:t * P + TOK[t]],
                                             ident[:])
                    last.then_inc(S["htok_turned"], 1)
                eng.wait_ge(S["pick_ready"], 1)
                eng.wait_ge(S["htok_lo"], 2 * TT)

                def gather(e):
                    for a in range(2):
                        for t in range(TT):
                            n = TOK[t]
                            for s, part in enumerate((tok_hi, tok_lo)):
                                last = eng.matmul(pb[7 - 3 * a], pick[0:n, t, :], part[0:n, t, a * 512:(a + 1) * 512],
                                                  start=t + s == 0, stop=t + s == TT)
                        last.then_inc(S["gather_done"], 1)

                def turn_gathered(done):
                    for a in range(2):
                        eng.wait_ge(S["rows_kept"], done + (a + 1))
                        for k in range(4):
                            last = eng.transpose(pb[7 - 3 * a][:, k * CAP:(k + 1) * CAP], y_e[:, (4 * a + k) * P:(4 * a + k + 1) * P],
                                                 ident[:])
                        last.then_inc(S["xe_turned"], 1)

                def turn(p):
                    for j in range(4):
                        last = eng.transpose(pb[4 if p % 2 == 0 else 7][:, j * CAP:(j + 1) * CAP], act_e[:, j * P:(j + 1) * P],
                                             ident[:])
                    last.then_inc(S["turned"], 1)

                def scatter(k, done):
                    if k == 0:
                        eng.wait_ge(S["y_e_kept"], done + 1)
                    eng.wait_ge(S["added"], done * 8 + max(k, 1))
                    eng.matmul(pb[5 + k % 2][:, 0:T], y_e[:, k * P:(k + 1) * P], put[:], start=True,
                               stop=True).then_inc(S["scattered"], 1)

                gather(0)
                turn_gathered(0)
                with eng.Fori(0, NE) as it:
                    eng.wait_ge(S["xe_lo_ready"], it * 2 + 2)
                    for j in range(4 * PER_E):
                        n = NU + j
                        eng.wait_ge(S["lo_ready"], it * (4 * PER_E) + (n + 1))
                        if j < 56:
                            p, s, q = j // 8, j % 8 // 4, j % 4
                            if s == 0 and q == 0:
                                if p >= 2:
                                    eng.wait_ge(S["gate_up_kept"], it * 7 + (p - 1))
                            wh, wl = unit(w_hi, "up", n), unit(w_lo, "up", n)
                            for k in range(2):
                                c = 2 * q + k
                                last = three(pb[2 * (p % 2) + s], xe_hi[:, c, :], xe_lo[:, c, :], wh[:, k, :], wl[:, k, :],
                                             c == 0, c == KC - 1)
                        else:
                            c = j - 56
                            if c % 4 == 0:
                                eng.wait_ge(S["at_lo_ready"], it * 7 + (c // 4 + 1))
                            wh, wl = unit(w_hi, "down", n), unit(w_lo, "down", n)
                            for a in range(2):
                                last = three(pb[5 + a], at_hi[:, c, :], at_lo[:, c, :], wh[:, 0, a * 512:(a + 1) * 512],
                                             wl[:, 0, a * 512:(a + 1) * 512], c == 0, c == FEC - 1)
                        last.then_inc(S["unit_used"], 1)
                        if j % 8 == 3 and 11 <= j <= 59:
                            p = (j - 11) // 8
                            eng.wait_ge(S["gate_up_kept"], it * 7 + (p + 1))
                            if p >= 2:
                                eng.wait_ge(S["at_lo_ready"], it * 7 + (p - 1))
                            turn(p)
                        if SCATTER_AT <= j < SCATTER_AT + KC:
                            scatter(j - SCATTER_AT, it)
                        if j == PUT_AT:
                            eng.wait_ge(S["put_ready"], it + 1)
                            eng.wait_ge(S["added"], it * 8 + 9)
                            for t in range(TT):
                                n = TOK[t]
                                last = eng.transpose(pb[5][:, t * P:t * P + n], put_tok[0:n, t, :], ident[0:n, 0:n])
                            last.then_inc(S["put_turned"], 1)
                        if j == 56 - 1:
                            eng.wait_ge(S["put_kept"], it + 1)
                        if j == 75:
                            eng.wait_ge(S["at_lo_ready"], it * 7 + 7)
                            eng.wait_ge(S["pick_ready"], it + 2)
                            gather(it + 1)
                        if j == 77:
                            turn_gathered(it * 2 + 2)
                for k in range(KC):
                    scatter(k, NE)

            sum_squares(FINAL)
            for t in range(TT):
                n = TOK[t]
                for a in range(2):
                    i = 2 * t + a
                    if i == 0:
                        h_is_ready(FINAL)
                    if i >= 2:
                        eng.wait_ge(S["y_kept"], i - 1)
                    for j in range(4):
                        last = eng.transpose(pb[4 + i % 2][0:n, j * P:(j + 1) * P], h[:, 4 * a + j, t * P:t * P + n], ident[:])
                    last.then_inc(S["y_turned"], 1)

        @block.scalar
        def _(eng):
            steps = [0]

            def link(ins):
                steps[0] += 1
                ins.then_inc(S["act_step"], 1)
                eng.wait_ge(S["act_step"], steps[0])

            def split(m, late=False):
                if m >= NU or m in LATE and not late:
                    return
                kind, i = SPLIT[m // 4]
                ks = chunks_of(kind, i)
                if m % 4 == 0:
                    landed(eng, kind, i)
                if m >= UNITS:
                    eng.wait_ge(S["unit_used"], m - UNITS + 1)
                eng.copy(unit(w_hi, kind, m, ks), quarter(slot(kind, i), kind, m % 4, ks)).then_inc(S["hi_ready"], 1)

            for t in range(2):
                eng.dma_start(xtok[:, t, :], A["x_prompt"][0, t * P:(t + 1) * P, :]).then_inc(S["x_loaded"], 16)
            eng.dma_start(xtok[0:NB, 2, :], A["x_sample"].rearrange("b s d -> (b s) d")).then_inc(S["x_loaded"], 16)
            eng.wait_ge(S["c_loaded"], 32)
            eng.activation(csilu, crow, ACT.Silu).then_inc(S["c_silu"], 1)
            eng.wait_ge(S["c_turned"], 1)
            eng.wait_ge(S["c_zero"], 1)
            eng.copy(c_split[:, :, 0:NC9], pb[5][:, 0:P].rearrange("p (k c) -> p k c", c=16)[:, :, 0:NC9]).then_inc(S["c_hi"], 1)
            for m in range(AHEAD):
                split(m)

            def ada_copy(i):
                eng.wait_ge(S["unit_used"], UNIT_AT["ada", i] + 4)
                if i >= 2:
                    eng.wait_ge(S["ada_turned"], i - 1)
                eng.copy(ada_row[:, i % 2, :], pb[ADA_BANKS[i]][0:CR, :]).then_inc(S["ada_copied"], 1)

            def ada(lo, hi, ends=False):
                for u in range(lo, hi):
                    i, j = u // 4, u % 4
                    if j == 0 and i not in ADA_STARTS:
                        ada_copy(i - 1)
                    split(UNIT_AT["ada", i] + j + AHEAD)
                if ends:
                    ada_copy(hi // 4 - 1)

            ada(0, 16, ends=True)

            def norm(m, splits=True, during=(), after=None):
                if m in ROOT_NO:
                    eng.preload_act_table_set("sqrt_and_others")
                for k in range(KC if m in ROOT_NO else 0):
                    if after:
                        eng.wait_ge(after[0], after[1] - KC + k + 1)
                    eng.activation(h[:, k, :], x[:, k, :], ACT.Square).then_inc(S["squared"], 1)
                ada(*during or (0, 0))
                eng.wait_ge(S["gains_ready"], m + 1)
                if m in ROOT_NO:
                    eng.wait_ge(S["ms_ready"], ROOT_NO[m] + 1)
                    eng.activation(rstd[:], rstd[:], ACT.Sqrt).then_inc(S["root_ready"], 1)
                else:
                    eng.wait_ge(S["unit_used"], UNIT_AT["kv", 3] + 4)
                if m in SHORT:
                    eng.wait_ge(S["hs_ready"], m + 1)
                    eng.copy(hh[:, :, TP:T], h[:, :, TP:T]).then_inc(S["hsh_ready"], 1)
                    for k in range(KC):
                        eng.wait_ge(S["scaled"], m * KC + k + 1)
                        eng.activation(hh[:, k, 0:TP], h[:, k, 0:TP], ACT.Identity,
                                       bias=mod[:, SHIFT[m] + k, 0:1]).then_inc(S["hh_ready"], 1)
                    return
                for k in range(KC + 1):
                    if k < KC:
                        eng.wait_ge(S["scaled"], m * KC + k + 1)
                        eng.activation(h[:, k, 0:TP], h[:, k, 0:TP], ACT.Identity, bias=mod[:, SHIFT[m] + k, 0:1],
                                       scale=gain[:, m, k, 0:1]).then_inc(S["h_ready"], 1)
                    if splits and k >= 1:
                        eng.wait_ge(S["h_ready"], LONG_NO[m] * KC + k)
                        if k == 1:
                            eng.wait_ge(S["hs_ready"], m + 1)
                        eng.copy(hh[:, k - 1, :], h[:, k - 1, :]).then_inc(S["hh_ready"], 1)

            def block(kind, i):
                u = UNIT_AT[kind, i // 4] + i % 4
                split(u + AHEAD)
                eng.wait_ge(S["unit_used"], u + 1)
                return pb[BLOCK_AT[kind, i] % 4][:, 0:T]

            def split_during(kind, n_tiles, first=0):
                for u in range(4 * first, 4 * n_tiles):
                    split(UNIT_AT[kind, 0] + u + AHEAD)

            eng.wait_ge(S["x_kept"], KC)
            eng.wait_ge(S["vec_kept"], 2)
            norm(MIX0)
            eng.wait_ge(S["r_done"], 1)
            eng.copy(rT, pb[5][0:GR, 0:T]).then_inc(S["r_kept"], 1)

            def log_sigmoid():
                eng.preload_act_table_set("natural_log_exp_and_others")
                eng.wait_ge(S["gate_done"], 1)
                for g in range(GH):
                    eng.activation(la[:, g, :], pb[4 + g][:, 0:T], ACT.Identity, bias=vec_b[:, GLA_BIAS + g:GLA_BIAS + g + 1])
                    last = eng.activation(t_abs[:, g, :], pb[4 + g][:, 0:T], ACT.Abs,
                                          bias=vec_b[:, GLA_BIAS + g:GLA_BIAS + g + 1])
                link(last)
                link(eng.activation(t_abs, t_abs, ACT.Exp, scale=-1.0))
                eng.activation(t_abs, t_abs, ACT.Ln, bias=1.0).then_inc(S["log_sig"], 1)

            ends = cum.rearrange("p (u s) t -> p u s t", s=2)[:, :, 1, HALF - 1]
            factors = ((qd, qd), (kd, kd), (qo, qo), (ko, ko),
                       (qe, cum.rearrange("p u t -> p (u t)").rearrange("p (h t) -> p h t", h=GH)),
                       (ke, ke), (dec, ends), (ea[:], la[:, :, TP:T]))
            for i in range(24):
                if i == 5:
                    log_sigmoid()
                if i >= 15 and i - 15 < 8:
                    eng.wait_ge(S["args_ready"], 1)
                    eng.activation(*factors[i - 15], ACT.Exp).then_inc(S["exps_ready"], 1)
                got = block("gla_in", i)
                if i < 4:
                    ins = eng.activation(big[:, i, :], got, ACT.Copy, scale=float(DK) ** -0.5)
                else:
                    ins = eng.copy(big[:, i, :], got)
                ins.then_inc(S["kept_act"], 1)
            for c in range(NCH):
                eng.wait_ge(S["v_turned"], c + 1)
                if c >= 2:
                    eng.wait_ge(S["u_done"], c - 1)
                eng.copy(vtok[c % 2][:, 0:512], pb[0][0:C, :])
                eng.copy(vtok[c % 2][:, 512:D], pb[1][0:C, :]).then_inc(S["v_kept"], 1)
                eng.copy(ktok[:, (c % 2) * 512:(c % 2 + 1) * 512], pb[2][0:C, :]).then_inc(S["v_kept"], 1)
                ada(ADA_C + 4 * c, ADA_C + 4 * c + 4)
            ada(32, 36, ends=True)
            eng.wait_ge(S["vs_turned"], 1)
            eng.wait_ge(S["o_done"], NCH)
            eng.copy(vs_tok[:, 0:512], pb[0][0:NB, :])
            eng.copy(vs_tok[:, 512:D], pb[1][0:NB, :]).then_inc(S["vs_kept"], 1)
            ada(ADA_S, ADA_S + 4 * (NB + 1))
            eng.activation(big[:, 16:24, :], big[:, 16:24, :], ACT.Silu).then_inc(S["out_gates"], 1)
            eng.wait_ge(S["os_kept"], 1)
            for g in range(GH):
                eng.activation(big[:, 2 * g:2 * g + 2, :], h[:, 2 * g:2 * g + 2, :], ACT.Square).then_inc(S["osq_ready"], 1)
            ada(72, 76)
            eng.wait_ge(S["oms_ready"], 1)
            eng.activation(orstd, orstd, ACT.Sqrt).then_inc(S["oroot_ready"], 1)

            ada(76, 80, ends=True)
            for k in range(KC):
                eng.wait_ge(S["o_ready"], k + 1)
                eng.copy(hh[:, k, :], h[:, k, :]).then_inc(S["hh_ready"], 1)
            split_during("gla_out", 2)
            norm(FFN0, after=(S["kept_dve"], empt[BLOCK_AT["gla_out", 7]][1]))
            for i in range(S0):
                eng.wait_ge(S[f"s0_stored{i}"], 16 * len(range(i, NB, S0)))
            eng.wait_ge(S["state_stored"], 16)
            for i in range(FFC + 1):
                if i < FFC:
                    got = block("ffn_up", 2 * i)
                    if i >= 2:
                        eng.wait_ge(S["kept_dve"], empt[BLOCK_AT["ffn_up", 2 * i - 4]][1])
                    eng.activation(silu_a[:, i % 2, :], got, ACT.Silu).then_inc(S["silu_done"], 1)
                    split(UNIT_AT["ffn_up", i // 2] + i % 2 * 2 + 1 + AHEAD)
                if i >= 1:
                    eng.wait_ge(S["kept_dve"], empt[BLOCK_AT["ffn_up", 2 * i - 2]][1])
                    eng.copy(act_hi[:, i - 1, :], act32[:, (i - 1) % 2, :]).then_inc(S["act_hi_ready"], 1)
                if i % 2 == 1 and 3 <= i <= 17:
                    ada(ADA_F + 2 * i - 6, ADA_F + 2 * i - 2, ends=i == 17)
            split_during("ffn_down", 6)
            norm(KV, after=(S["kept_dve"], empt[BLOCK_AT["ffn_down", 47]][1]))
            for i in range(16):
                eng.copy(kvq[:, i, :], block("kv", i)).then_inc(S["kept_act"], 1)
            norm(MIX1)
            for i in range(8):
                eng.copy(kvq[:, 16 + i, :], block("sb_q", i)).then_inc(S["kept_act"], 1)
            eng.wait_ge(S["qs_turned"], 1)
            eng.copy(qs_tok[:, 0:512], pb[4][0:NB, :])
            eng.copy(qs_tok[:, 512:D], pb[5][0:NB, :]).then_inc(S["qs_kept"], 1)

            for b in range(NB):
                eng.wait_ge(S["qbc_done"], b + 1)
                if b >= 2:
                    eng.wait_ge(S["prod0_ready"], b - 1)
                    eng.wait_ge(S["prod1_ready"], b - 1)
                eng.copy(q_rows[b % 2], psum[:, Q_BANKS[b % 3] * 512:(Q_BANKS[b % 3] + 2) * 512]).then_inc(S["q_kept"], 1)
                for i in range(2 * b - 2, 2 * b) if 1 <= b <= 6 else ():
                    t, q = i // 4, i % 4
                    eng.wait_ge(S["kv_turned"], i + 1)
                    eng.copy(kvtok[0:TOK[t], t, q * 512:(q + 1) * 512], pb[4 + i % 2][0:TOK[t], :]).then_inc(S["kv_kept"], 1)

            def soft(g, z, to):
                eng.wait_ge(S["z_ready"], g + 1)
                if 3 <= g < SH // 2:
                    eng.wait_ge(S["rc_done"], g - 2)
                link(eng.activation(to, z, ACT.Abs))
                link(eng.activation(to, to, ACT.Exp, scale=-1.0))
                eng.activation(to, to, ACT.Ln, bias=1.0).then_inc(S["soft_ready"], 1)

            G = SH // 2
            eng.preload_act_table_set("natural_log_exp_and_others")
            soft(0, z_buf[:, 0, :], l_buf[:, 0, :])
            for g in range(G + 1):
                if g + 1 < G:
                    soft(g + 1, z_buf[:, (g + 1) % 3, :], l_buf[:, (g + 1) % 3, :])
                if g < G:
                    zg = z_buf[:, g % 3, :]
                    eng.wait_ge(S["arg_ready"], g + 1)
                    eng.activation(zg, zg, ACT.Exp).then_inc(S["p_exp"], 1)
                if g >= 1:
                    eng.wait_ge(S["pv_done"], g)
                    eng.copy(h[:, g - 1, 0:TP], pb[6 + (g - 1) % 2][:, 0:TP]).then_inc(S["pv_kept"], 1)
            soft(G, zs, ls)
            eng.wait_ge(S["args_s"], 1)
            eng.activation(zs, zs, ACT.Exp).then_inc(S["exps_s"], 1)
            for m in range(AHEAD):
                split(UNIT_AT["sb_out", 0] + m, late=True)
            eng.wait_ge(S["otT_done"], 1)
            eng.copy(h[:, :, TP:T], pb[5][:, 0:64].rearrange("p (k b) -> p k b", b=NB)).then_inc(S["otT_kept"], 1)
            eng.wait_ge(S["otT_kept"], 1)
            eng.wait_ge(S["pv_kept"], G)
            for k in range(KC):
                eng.copy(hh[:, k, :], h[:, k, :]).then_inc(S["hh_ready"], 1)
            split_during("sb_out", 2)

            norm(FFN1, splits=False, after=(S["kept_dve"], empt[-1][1]), during=(112, 116))
            ada(116, 124)
            eng.wait_ge(S["gates_exp"], 1)
            eng.activation(e2[:, 0:TT], e2[:, 0:TT], ACT.Exp).then_inc(S["gates_exp_done"], 1)
            ada(124, 128, ends=True)
            eng.wait_ge(S["most_ready"], 1)
            busiest = eng.value_load(most[0:1, 0:1], min_val=0, max_val=T)
            with eng.If(busiest > cap):
                eng.wait_ge(S["gateT_done"], 1)
                eng.copy(gateT[:], pb[4][0:NE, 0:T]).then_inc(S["gateT_kept"], 1)
                for e in range(NE):
                    eng.wait_ge(S["gbc_done"], e + 1)
                    eng.copy(gate_bc[:, e, :], pb[6 + e % 2][:, 0:T]).then_inc(S["gbc_kept"], 1)
                with eng.Fori(0, NE) as it:
                    for n in range(FEC):
                        eng.wait_ge(S["gate_half_done"], it * FEC + (n + 1))
                        eng.activation(silu_m[:, n % 2, :], pb[2 * (n % 2)][:, 0:T], ACT.Silu).then_inc(S["pair_silu"], 1)
            with eng.Else():
                for i in range(2 * TT):
                    t, a = i // 2, i % 2
                    eng.wait_ge(S["htok_turned"], i + 1)
                    eng.copy(tok_hi[0:TOK[t], t, a * 512:(a + 1) * 512], pb[7 - 3 * a][0:TOK[t], :]).then_inc(S["htok_hi"], 1)

                def keep_rows(done):
                    for a in range(2):
                        eng.wait_ge(S["gather_done"], done + (a + 1))
                        eng.copy(y_e[:, a * 512:(a + 1) * 512], pb[7 - 3 * a]).then_inc(S["rows_kept"], 1)

                def keep_gathered(done):
                    for a in range(2):
                        eng.wait_ge(S["xe_turned"], done + (a + 1))
                        eng.copy(xe_hi[:, 4 * a:4 * a + 4, :],
                                 pb[7 - 3 * a].rearrange("p (k c) -> p k c", k=4)).then_inc(S["xe_hi_ready"], 1)

                keep_rows(0)
                keep_gathered(0)
                with eng.Fori(0, NE) as it:
                    for j in range(4 * PER_E):
                        n = NU + j
                        if j % 4 == 0:
                            expert_landed(eng, it, j // 4)
                        eng.wait_ge(S["unit_used"], it * (4 * PER_E) + (n - UNITS + 1))
                        kind = "up" if j < 56 else "down"
                        eng.copy(unit(w_hi, kind, n), quarter(ring[(BASE + j // 4) % RING], kind, j % 4)).then_inc(S["hi_ready"], 1)
                        if j == UNITS - 1:
                            eng.wait_ge(S["added"], it * 8 + 1)
                            eng.copy(y_e[:], psum[:, 5 * 512:7 * 512]).then_inc(S["y_e_kept"], 1)
                        if j == PUT_AT + 4:
                            eng.wait_ge(S["put_turned"], it + 1)
                            eng.copy(put[:], pb[5][:, 0:T]).then_inc(S["put_kept"], 1)
                        if j % 8 == 7 and j < 56:
                            p = j // 8
                            if p >= 1:
                                eng.wait_ge(S["gate_up_kept"], it * 7 + p)
                            eng.activation(silu_e[:], pb[2 * (p % 2)], ACT.Silu).then_inc(S["e_silu"], 1)
                        if j % 8 == 7 and 15 <= j <= 63:
                            p = (j - 15) // 8
                            eng.wait_ge(S["turned"], it * 7 + (p + 1))
                            eng.copy(at_hi[:, 4 * p:4 * p + 4, :], pb[4 if p % 2 == 0 else 7]
                                     .rearrange("p (k c) -> p k c", k=4)).then_inc(S["at_hi_ready"], 1)
                        if j == 79:
                            keep_rows(it * 2 + 2)
                        if j == 81:
                            keep_gathered(it * 2 + 2)
                eng.wait_ge(S["unit_used"], NE * (4 * PER_E) + NU)
                eng.copy(y_e[:], psum[:, 5 * 512:7 * 512]).then_inc(S["y_e_kept"], 1)
            eng.wait_ge(S["experts_done"], 1)
            norm(FINAL, splits=False)
            for i in range(6):
                t, a = i // 2, i % 2
                eng.wait_ge(S["y_turned"], i + 1)
                eng.copy(ytok[0:TOK[t], t, a * 512:(a + 1) * 512], pb[4 + i % 2][0:TOK[t], :]).then_inc(S["y_kept"], 1)

        @block.vector
        def _(eng):
            steps = [0]

            def link(ins):
                steps[0] += 1
                ins.then_inc(S["dve_step"], 1)
                eng.wait_ge(S["dve_step"], steps[0])

            def split(m, late=False):
                if m >= NU or m in LATE and not late:
                    return
                kind, i = SPLIT[m // 4]
                ks = chunks_of(kind, i)
                eng.wait_ge(S["hi_ready"], m + 1)
                eng.tensor_tensor(unit(w_lo, kind, m, ks), quarter(slot(kind, i), kind, m % 4, ks),
                                  unit(w_hi, kind, m, ks), ALU.subtract).then_inc(S["lo_ready"], 1)

            eng.memset(c_split[:].bitcast(F32), 0.0).then_inc(S["c_zero"], 1)
            eng.wait_ge(S["c_hi"], 1)
            eng.tensor_tensor(c_split[:, :, LO_ROW:CR], pb[5][:, 0:P].rearrange("p (k c) -> p k c", c=16)[:, :, 0:NC9],
                              c_split[:, :, 0:NC9], ALU.subtract).then_inc(S["c_kept"], 1)
            for m in range(AHEAD):
                split(m)
            for k in range(KC):
                eng.wait_ge(S["x_turned"], k + 1)
                eng.tensor_copy(x[:, k, :], pb[6 + k % 2][:, 0:T]).then_inc(S["x_kept"], 1)
            def ada_add(i):
                o = ADA_ORDER[i]
                eng.wait_ge(S["ada_turned"], i + 1)
                to, got = mod[:, 4 * o:4 * o + 4, :], pb[ADA_BANKS[i]][:, 0:256].rearrange("p (k c) -> p k c", c=64)
                eng.tensor_tensor(to, got[:, :, 0:NC9], vec_a[:, 4 * o:4 * o + 4].unsqueeze(2).to_broadcast([P, 4, NC9]),
                                  ALU.add).then_inc(S["ada_part"], 1)
                eng.wait_ge(S["ada_part"], i + 1)
                eng.tensor_tensor(to, to, got[:, :, LO_ROW:CR], ALU.add).then_inc(S["ada_kept"], 1)

            def ada(lo, hi, ends=False):
                for u in range(lo, hi):
                    i, j = u // 4, u % 4
                    split(UNIT_AT["ada", i] + j + AHEAD)
                    if j == 3 and i not in ADA_STARTS:
                        ada_add(i - 1)
                if ends:
                    ada_add(hi // 4 - 1)

            ada(0, 4)
            eng.wait_ge(S["vec_turned"], 1)
            eng.tensor_copy(vec_a[:], pb[4][:, 0:P]).then_inc(S["vec_kept"], 1)
            eng.tensor_copy(vec_b[:], pb[4][:, P:P + VEC_B]).then_inc(S["vec_kept"], 1)
            eng.wait_ge(S["vec_kept"], 2)
            ada(4, 16, ends=True)

            def norm(m):
                eng.wait_ge(S["ada_kept"], ADA_NEEDED[m])
                eng.scalar_tensor_tensor(gain[:, m, :, :], mod[:, SCALE[m]:SCALE[m] + KC, :], 1.0,
                                         vec_b[:, GAIN[m]:GAIN[m] + KC].unsqueeze(2).to_broadcast([P, KC, NC9]),
                                         ALU.add, ALU.mult).then_inc(S["gains_ready"], 1)
                eng.wait_ge(S["gains_ready"], m + 1)
                if m in ROOT_NO:
                    eng.wait_ge(S["ss_done"], ROOT_NO[m] + 1)
                    eng.tensor_scalar(rstd[:], pb[7][:, 0:T], 1.0 / D, EPS, ALU.mult, ALU.add).then_inc(S["ms_ready"], 1)
                    eng.wait_ge(S["root_ready"], ROOT_NO[m] + 1)
                    link(eng.reciprocal(rstd[:], rstd[:]))
                else:
                    eng.wait_ge(S["unit_used"], UNIT_AT["kv", 3] + 4)
                hs = h[:, :, TP:T]
                link(eng.tensor_tensor(hs, x[:, :, TP:T], rstd[:, TP:T].unsqueeze(1).to_broadcast([P, KC, NB]), ALU.mult))
                link(eng.tensor_tensor(hs, hs, gain[:, m, :, 1:NC9], ALU.mult))
                eng.tensor_tensor(hs, hs, mod[:, SHIFT[m]:SHIFT[m] + KC, 1:NC9], ALU.add).then_inc(S["hs_ready"], 1)
                if m in SHORT:
                    for k in range(KC + 1):
                        if k < KC:
                            eng.scalar_tensor_tensor(h[:, k, 0:TP], x[:, k, 0:TP], gain[:, m, k, 0:1], rstd[:, 0:TP],
                                                     ALU.mult, ALU.mult).then_inc(S["scaled"], 1)
                        if k == 0:
                            eng.wait_ge(S["hsh_ready"], SHORT.index(m) + 1)
                            eng.wait_ge(S["hs_ready"], m + 1)
                            eng.tensor_tensor(hl[:, :, TP:T], hs, hh[:, :, TP:T], ALU.subtract).then_inc(S["hsl_ready"], 1)
                            continue
                        done = IN_OF[m] * KC + k
                        eng.wait_ge(S["hh_ready"], done)
                        eng.scalar_tensor_tensor(hl[:, k - 1, 0:TP], h[:, k - 1, 0:TP], mod[:, SHIFT[m] + k - 1, 0:1],
                                                 hh[:, k - 1, 0:TP], ALU.add, ALU.subtract).then_inc(S["hl_ready"], 1)
                    return
                for k in range(KC):
                    eng.tensor_tensor(h[:, k, 0:TP], x[:, k, 0:TP], rstd[:, 0:TP], ALU.mult).then_inc(S["scaled"], 1)

            def low_parts(m):
                for k in range(KC):
                    eng.wait_ge(S["hh_ready"], m * KC + k + 1)
                    eng.tensor_tensor(hl[:, k, :], h[:, k, :], hh[:, k, :], ALU.subtract).then_inc(S["hl_ready"], 1)

            def split_during(kind, n_tiles, first=0):
                for u in range(4 * first, 4 * n_tiles):
                    split(UNIT_AT[kind, 0] + u + AHEAD)

            def add_to_x(got, k, gate, parted, value):
                xs, ts = x[:, k, TP:T], tmp8[:, k, :]
                eng.scalar_tensor_tensor(x[:, k, 0:TP], got[:, 0:TP], mod[:, gate + k, 0:1], x[:, k, 0:TP], ALU.mult, ALU.add)
                eng.tensor_tensor(ts, got[:, TP:T], mod[:, gate + k, 1:NC9], ALU.mult).then_inc(parted, 1)
                eng.wait_ge(parted, value)
                return eng.tensor_tensor(xs, xs, ts, ALU.add)

            parts = [0]

            def add_block(kind, i, gate):
                n = BLOCK_AT[kind, i]
                per = 8 if kind == "ffn_down" else 4
                u = UNIT_AT[kind, i // per] + i % per * 4 // per
                if per == 4 or i % 2 == 0:
                    split(u + AHEAD)
                eng.wait_ge(S["unit_used"], u + 1)
                if empt[n][1] > 1:
                    eng.wait_ge(S["kept_dve"], empt[n][1] - 1)
                parts[0] += 1
                add_to_x(pb[n % 4], i % 8, gate, S["part_added"], parts[0]).then_inc(S["kept_dve"], 1)

            norm(MIX0)
            low_parts(IN_GLA)
            split_during("gla_in", 2)
            eng.wait_ge(S["log_sig"], 1)
            link(eng.scalar_tensor_tensor(la, la, 0.0, t_abs, ALU.min, ALU.subtract))
            link(eng.tensor_scalar(la, la, 1.0 / 16.0, None, ALU.mult))
            four = lambda v: v.rearrange("p (h c s) t -> p h c (s t)", h=GH, c=NCH)
            u_in = UNIT_AT["gla_in", 2] + AHEAD
            split(u_in)
            split(u_in + 1)
            src = la[:, :, 0:TP].rearrange("p h (c t) -> p h c t", t=C)
            for n, d in enumerate((1, 2, 4, 8, 16, 32)):
                dst = four(cum_a if n % 2 == 0 else cum)
                eng.tensor_copy(dst[:, :, :, 0:d], src[:, :, :, 0:d])
                link(eng.tensor_tensor(dst[:, :, :, d:C], src[:, :, :, d:C], src[:, :, :, 0:C - d], ALU.add))
                src = dst
                if n % 2 == 1:
                    split(u_in + 2 + n // 2)
            mid = cum[:, :, HALF // 2 - 1:HALF // 2].to_broadcast([P, 32, HALF])
            link(eng.tensor_tensor(qd, cum, mid, ALU.subtract))
            eng.tensor_scalar(kd, qd, -1.0, EXP_CAP, ALU.mult, ALU.min)
            halves = cum.rearrange("p (u s) t -> p u s t", s=2)
            seam = halves[:, :, 0, HALF - 1:HALF].to_broadcast([P, 16, HALF])
            eng.tensor_tensor(qo, halves[:, :, 1, :], seam, ALU.subtract)
            link(eng.tensor_tensor(ko, seam, halves[:, :, 0, :], ALU.subtract))
            chunks = cum.rearrange("p (u s) t -> p u (s t)", s=2)
            eng.tensor_tensor(ke.rearrange("p h t -> p (h t)").rearrange("p (u t) -> p u t", u=16),
                              chunks[:, :, C - 1:C].to_broadcast([P, 16, C]), chunks, ALU.subtract)
            eng.tensor_scalar(qd, qd, EXP_CAP, None, ALU.min).then_inc(S["args_ready"], 1)
            for u in range(5, 9):
                split(u_in + u)
            eng.wait_ge(S["kept_act"], 8)
            q, k = big[:, 0:GH, 0:TP], big[:, GH:2 * GH, 0:TP]
            by_head = lambda v: v.rearrange("p (h u) t -> p h (u t)", h=GH)
            side = lambda v, s: v.rearrange("p h (c s t) -> p h c s t", c=NCH, s=2)[:, :, :, s, :]
            by_chunk = lambda v: v.rearrange("p (h c) t -> p h c t", h=GH)
            for n, (v, w) in enumerate(((by_head(qd), q), (by_head(kd), k), (by_chunk(qo), side(q, 1)),
                                        (by_chunk(ko), side(k, 0)), (qe, q), (ke, k))):
                eng.wait_ge(S["exps_ready"], n + 1)
                eng.tensor_tensor(v, v, w, ALU.mult).then_inc(S["decayed"], 1)
                split(u_in + 9 + n)
            split(u_in + 15)
            link(eng.memset(st[HALF:C, :, 0:HALF], 0.0))
            eng.wait_ge(S["scores_done"], 1)
            for n in range(2):
                got = pb[4 + n].rearrange("p (u t) -> p u t", t=C)
                eng.tensor_tensor(st[:, 8 * n:8 * n + 8, HALF:C], got[0:C, :, HALF:C],
                                  upto[:, HALF:C].unsqueeze(1).to_broadcast([C, 8, HALF]), ALU.mult)
                last = eng.tensor_tensor(st[0:HALF, 8 * n:8 * n + 8, 0:HALF], got[0:HALF, :, 0:HALF],
                                         upto[0:HALF, 0:HALF].unsqueeze(1).to_broadcast([HALF, 8, HALF]), ALU.mult)
            last.then_inc(S["scores_kept"], 1)
            for c in range(NCH):
                ada(ADA_C + 4 * c, ADA_C + 4 * c + 2)
                eng.wait_ge(S["o_done"], c + 1)
                eng.tensor_copy(h[:, :, c * C:(c + 1) * C], pb[3].rearrange("p (k t) -> p k t", t=C)).then_inc(S["o_kept"], 1)
                eng.wait_ge(S["u_done"], c + 1)
                u = psum[:, 6 * 512:8 * 512].rearrange("p (g v) -> p g v", g=GH)
                if c == 0:
                    eng.tensor_copy(state[0], u).then_inc(S["state_ready"], 1)
                    ada(ADA_C + 2, ADA_C + 4)
                    continue
                eng.wait_ge(S["state_ready"], c)
                eng.wait_ge(S["exps_ready"], 7)
                for g in range(GH):
                    last = eng.scalar_tensor_tensor(state[c % 2][:, g, :], state[(c - 1) % 2][:, g, :],
                                                    dec[:, g * NCH + c:g * NCH + c + 1], u[:, g, :], ALU.mult, ALU.add)
                last.then_inc(S["state_ready"], 1)
                ada(ADA_C + 4 * c + 2, ADA_C + 4 * c + 4)
            ada(32, 36, ends=True)
            eng.wait_ge(S["exps_ready"], 8)
            for b in range(NB):
                eng.wait_ge(S[f"s0_loaded{b % S0}"], 16 * (b // S0 + 1))
                s = s0[b % S0]
                for g in range(GH):
                    last = eng.tensor_scalar(s[:, g, :], s[:, g, :], ea[:, g, b:b + 1], None, ALU.mult)
                link(last)
                ada(ADA_S + 4 * b, ADA_S + 4 * b + 1)
                eng.wait_ge(S["vbc_done"], b + 1)
                v = psum[:, (4 + 2 * (b % 2)) * 512:(6 + 2 * (b % 2)) * 512].rearrange("p (g v) -> p g v", g=GH)
                for g in range(GH):
                    last = eng.scalar_tensor_tensor(s[:, g, :], v[:, g, :], big[:, GH + g, TP + b:TP + b + 1], s[:, g, :],
                                                    ALU.mult, ALU.add)
                last.then_inc(S["s_updated"], 1)
                ada(ADA_S + 4 * b + 1, ADA_S + 4 * b + 4)
            ada(ADA_S + 4 * NB, ADA_S + 4 * NB + 4)
            eng.wait_ge(S["os_done"], NB)
            eng.tensor_copy(h[:, :, TP:T], pb[3][:, 0:64].rearrange("p (k b) -> p k b", b=NB)).then_inc(S["os_kept"], 1)
            eng.wait_ge(S["oss_done"], 1)
            for g in range(GH):
                last = eng.tensor_scalar(orstd[:, g, :], pb[4 + g][:, 0:T], 1.0 / DV, EPS, ALU.mult, ALU.add)
            last.then_inc(S["oms_ready"], 1)
            ada(72, 76)
            eng.wait_ge(S["oroot_ready"], 1)
            link(eng.reciprocal(orstd, orstd))
            eng.wait_ge(S["out_gates"], 1)
            for j in range(KC):
                link(eng.scalar_tensor_tensor(h[:, j, :], h[:, j, :], vec_b[:, GLA_GAIN + j % 2:GLA_GAIN + j % 2 + 1],
                                              orstd[:, j // 2, :], ALU.mult, ALU.mult))
                eng.tensor_tensor(h[:, j, :], h[:, j, :], big[:, 16 + j, :], ALU.mult).then_inc(S["o_ready"], 1)
                if j == 3:
                    ada(76, 80, ends=True)
            low_parts(IN_GLA_OUT)
            for i in range(8):
                add_block("gla_out", i, GATE[MIX0])

            norm(FFN0)
            for i in range(S0):
                eng.wait_ge(S[f"s0_stored{i}"], 16 * len(range(i, NB, S0)))
            eng.wait_ge(S["state_stored"], 16)
            for i in range(FFC + 1):
                if i < FFC:
                    n, u = BLOCK_AT["ffn_up", 2 * i + 1], UNIT_AT["ffn_up", i // 2] + i % 2 * 2
                    split(u + AHEAD)
                    split(u + 1 + AHEAD)
                    eng.wait_ge(S["unit_used"], u + 2)
                    eng.wait_ge(S["silu_done"], i + 1)
                    if i >= 2:
                        eng.wait_ge(S["act_ready"], i - 1)
                    eng.tensor_tensor(act32[:, i % 2, :], silu_a[:, i % 2, :], pb[n % 4][:, 0:T], ALU.mult).then_inc(S["kept_dve"], 1)
                if i >= 1:
                    eng.wait_ge(S["act_hi_ready"], i)
                    eng.tensor_tensor(act_lo[:, i - 1, :], act32[:, (i - 1) % 2, :], act_hi[:, i - 1, :],
                                      ALU.subtract).then_inc(S["act_ready"], 1)
                if i % 2 == 1 and 3 <= i <= 17:
                    ada(ADA_F + 2 * i - 6, ADA_F + 2 * i - 2, ends=i == 17)
            for i in range(48):
                add_block("ffn_down", i, GATE[FFN0])
            norm(KV)
            split_during("kv", 4)
            norm(MIX1)
            split_during("sb_q", 2)

            for b in range(NB + 1):
                by_head = lambda v: v.rearrange("p (h d) -> p h d", h=SH)
                if b < NB:
                    if b % 2 == 0:
                        landed(eng, "k_cache", b // 2)
                    eng.wait_ge(S["q_kept"], b + 1)
                    lo = (b % 2) * 2 * D
                    eng.tensor_tensor(prod, slot("k_cache", b // 2)[:, lo:lo + D], q_rows[b % 2],
                                      ALU.mult).then_inc(S["prod0_ready"], 1)
                if b >= 1:
                    eng.wait_ge(S["prod1_ready"], b)
                    eng.tensor_reduce(zs[:, 1, (b - 1) * SH:b * SH], by_head(prod1[(b - 1) % 2]), AX.X,
                                      ALU.add).then_inc(S["z_s_ready"], 1)
                if b < NB:
                    eng.wait_ge(S["prod0_ready"], b + 1)
                    link(eng.tensor_reduce(zs[:, 0, b * SH:(b + 1) * SH], by_head(prod), AX.X, ALU.add))
            eng.wait_ge(S["z_s_ready"], NB)

            G = SH // 2
            scale = float(SD) ** -0.5
            mask4 = lambda v: v[:].unsqueeze(1).to_broadcast([P, 4, P])
            as4 = lambda v: v.rearrange("p (a t) -> p a t", t=P)
            def scores(g):
                eng.wait_ge(S["z_done"], g + 1)
                if g >= 3:
                    eng.wait_ge(S["pv_done"], g - 2)
                zg = z_buf[:, g % 3, :]
                for a in range(2):
                    bias = sb_bias[:, 2 * g + a:2 * g + a + 1]
                    of_head = lambda v: v.rearrange("p (s a t) -> p s a t", s=2, a=2)[:, :, a, :]
                    got = pb[2 * (g % 2) + a]
                    eng.tensor_scalar(of_head(zg[:, 0:512]), got[:, 0:2 * P].rearrange("p (s t) -> p s t", s=2), scale, bias,
                                      ALU.mult, ALU.add)
                    last = eng.tensor_scalar(zg[:, 512 + a * P:512 + (a + 1) * P],
                                             got[:, 2 * P:3 * P], scale, bias, ALU.mult, ALU.add)
                last.then_inc(S["z_ready"], 1)

            scores(0)
            for g in range(G + 1):
                if g < G:
                    zg, lg = z_buf[:, g % 3, :], l_buf[:, g % 3, :]
                    eng.wait_ge(S["soft_ready"], g + 1)
                    eng.wait_ge(S["z_ready"], g + 1)
                    link(eng.scalar_tensor_tensor(lg, zg, 0.0, lg, ALU.max, ALU.add))
                    eng.tensor_tensor(as4(lg[:, 0:512]), as4(lg[:, 0:512]), mask4(not_before), ALU.mult)
                    eng.tensor_scalar(lg[:, 512:768], lg[:, 512:768], -1.0, None, ALU.mult).then_inc(S["l_ready"], 1)
                    link(eng.tensor_tensor(as4(zg[:, 0:512]), as4(zg[:, 0:512]), mask4(before), ALU.mult))
                if g + 1 < G:
                    scores(g + 1)
                if g >= 1:
                    before_g = z_buf[:, (g - 1) % 3, 0:512]
                    eng.wait_ge(S["p_exp"], g)
                    eng.tensor_tensor(as4(before_g), as4(before_g), mask4(before), ALU.mult).then_inc(S["p_ready"], 1)
                if g < G:
                    eng.wait_ge(S["rc_done"], g + 1)
                    eng.tensor_tensor(zg[:, 0:512], zg[:, 0:512], pb[4], ALU.add)
                    eng.tensor_tensor(zg[:, 512:768], zg[:, 512:768], pb[5][:, 0:256], ALU.add).then_inc(S["arg_ready"], 1)
            rows16 = lambda v: v.rearrange("p a b -> p (a b)").rearrange("p (a b) -> p a b", b=SH)
            eng.scalar_tensor_tensor(rows16(zs), rows16(zs), scale,
                                     sb_bias[:].unsqueeze(1).to_broadcast([P, PAGES * NB, SH]),
                                     ALU.mult, ALU.add).then_inc(S["z_ready"], 1)
            eng.wait_ge(S["soft_ready"], G + 1)
            link(eng.scalar_tensor_tensor(ls, zs, 0.0, ls, ALU.max, ALU.add))
            eng.tensor_scalar(ls, ls, -1.0, None, ALU.mult).then_inc(S["l_ready"], 1)
            eng.wait_ge(S["rcs_done"], 1)
            eng.tensor_tensor(zs, zs, pb[4][:, 0:256].rearrange("p (a b) -> p a b", a=PAGES), ALU.add).then_inc(S["args_s"], 1)
            own = ident[0:SH, 0:SH].unsqueeze(2).to_broadcast([SH, SH, SD])
            for b in range(NB):
                eng.wait_ge(S["opv_done"], b + 1)
                if b >= 1:
                    eng.wait_ge(S["ot_done"], b)
                eng.tensor_tensor(os_row.rearrange("p (h d) -> p h d", h=SH),
                                  psum[0:SH, 6 * (b % 2) * 512:(6 * (b % 2) + 2) * 512].rearrange("p (h d) -> p h d", h=SH), own, ALU.mult).then_inc(S["own_ready"], 1)
            eng.wait_ge(S["ot_done"], NB)
            eng.tensor_copy(os_tok, psum[0:NB, D:2 * D]).then_inc(S["ot_kept"], 1)
            for m in range(AHEAD):
                split(UNIT_AT["sb_out", 0] + m, late=True)
            low_parts(IN_SB_OUT)
            for i in range(8):
                add_block("sb_out", i, GATE[MIX1])

            ada(112, 116)
            norm(FFN1)
            ada(116, 124)
            eng.wait_ge(S["kv_stored"], 16 * 6)
            link(eng.memset(logit[:], 0.0))
            eng.wait_ge(S["logits_done"], 1)
            for t in range(TT):
                n = TOK[t]
                last = eng.tensor_tensor(logit[0:n, t, :], pb[4][0:n, t * NE:(t + 1) * NE], router_bias[0:n, :], ALU.add)
            link(last)
            for t in range(TT):
                last = eng.max(top[:, t, :], logit[:, t, :])
            link(last)
            eng.tensor_tensor(e2[:, 0:TT], top[:, :, 1], top[:, :, 0], ALU.subtract).then_inc(S["gates_exp"], 1)
            for t in range(TT):
                last = eng.max_index(top_i[:, t, :], top[:, t, :], logit[:, t, :])
            link(last)
            link(eng.tensor_copy(top_f[:], top_i[:]))
            ada(124, 128, ends=True)
            per_expert = lambda v: v.unsqueeze(2).to_broadcast([P, TT, NE])
            experts = iota[:, 0:NE].unsqueeze(1).to_broadcast([P, TT, NE])
            eng.tensor_tensor(hit[:], experts, per_expert(top_f[:, :, 0]), ALU.is_equal)
            link(eng.tensor_tensor(gate_tok[:], experts, per_expert(top_f[:, :, 1]), ALU.is_equal))
            eng.tensor_tensor(chosen[:], gate_tok[:], hit[:], ALU.add).then_inc(S["gates_ready"], 1)
            eng.wait_ge(S["gates_exp_done"], 1)
            link(eng.tensor_scalar(w1[:, 0:TT], e2[:, 0:TT], 1.0, None, ALU.add))
            link(eng.reciprocal(w1[:, 0:TT], w1[:, 0:TT]))
            link(eng.tensor_tensor(w2[:, 0:TT], e2[:, 0:TT], w1[:, 0:TT], ALU.mult))
            eng.tensor_tensor(hit[:], hit[:], per_expert(w1[:, 0:TT]), ALU.mult)
            link(eng.tensor_tensor(gate_tok[:], gate_tok[:], per_expert(w2[:, 0:TT]), ALU.mult))
            link(eng.tensor_tensor(gate_tok[:], gate_tok[:], hit[:], ALU.add))
            eng.wait_ge(S["gates_ready"], 1)
            eng.wait_ge(S["count_done"], 1)
            for t in range(TT):
                eng.tensor_copy(pos[0:TOK[t], t, :], pb[5][0:TOK[t], t * NE:(t + 1) * NE])
            link(eng.tensor_reduce(w1[:, 7:8], pb[5][:, TT * NE:(TT + 1) * NE], AX.X, ALU.max))
            eng.tensor_copy(most[:], w1[:, 7:8]).then_inc(S["most_ready"], 1)
            eng.wait_ge(S["most_ready"], 1)
            busiest = eng.value_load(most[0:1, 0:1], min_val=0, max_val=T)
            with eng.If(busiest > cap):
                eng.nop().then_inc(S["down_kept"], 1)
                eng.wait_ge(S["gbc_kept"], NE)
                with eng.Fori(0, NE) as it:
                    for n in range(FEC):
                        eng.wait_ge(S["pair_done"], it * FEC + (n + 1))
                        eng.tensor_tensor(gated[:, n % 2, :], pb[2 * (n % 2) + 1][:, 0:T], gate_bc[:, it, :],
                                          ALU.mult).then_inc(S["gated_ready"], 1)
                        eng.wait_ge(S["gated_ready"], it * FEC + (n + 1))
                        eng.wait_ge(S["pair_silu"], it * FEC + (n + 1))
                        eng.tensor_tensor(act_m[:, n, :], silu_m[:, n % 2, :], gated[:, n % 2, :],
                                          ALU.mult).then_inc(S["pair_kept"], 1)
                        if n % 4 == 3:
                            eng.nop().then_inc(S["lo_ready"], 4)
                            eng.nop().then_inc(S["lo_ready"], 4)
                    for n in range(56):
                        eng.wait_ge(S["down_done"], it * 56 + (n + 1))
                        eng.wait_ge(S["down_kept"], it * 56 + (n + 1))
                        add_to_x(pb[n % 4], n % 8, GATE[FFN1], S["down_part"], it * 56 + (n + 1)).then_inc(S["down_kept"], 1)
                        if n % 8 == 7:
                            eng.nop().then_inc(S["lo_ready"], 4)
                eng.wait_ge(S["down_kept"], NE * 56 + 1)
            with eng.Else():
                eng.memset(pb[5], 0.0)
                eng.memset(pb[6], 0.0)
                eng.memset(put[:], 0.0).then_inc(S["added"], 1)
                for i in range(2 * TT):
                    t, a = i // 2, i % 2
                    eng.wait_ge(S["htok_hi"], i + 1)
                    eng.tensor_tensor(tok_lo[0:TOK[t], t, a * 512:(a + 1) * 512], pb[7 - 3 * a][0:TOK[t], :],
                                      tok_hi[0:TOK[t], t, a * 512:(a + 1) * 512], ALU.subtract).then_inc(S["htok_lo"], 1)

                def keep_gathered(done):
                    for a in range(2):
                        eng.wait_ge(S["xe_hi_ready"], done + (a + 1))
                        eng.tensor_tensor(xe_lo[:, 4 * a:4 * a + 4, :], pb[7 - 3 * a].rearrange("p (k c) -> p k c", k=4),
                                          xe_hi[:, 4 * a:4 * a + 4, :], ALU.subtract).then_inc(S["xe_lo_ready"], 1)

                def add_chunk(k, done):
                    eng.wait_ge(S["scattered"], done * 8 + (k + 1))
                    add_to_x(pb[5 + k % 2], k, GATE[FFN1], S["down_part"], done * 8 + (k + 1)).then_inc(S["added"], 1)

                keep_gathered(0)
                with eng.Fori(0, NE) as it:
                    for j in range(4 * PER_E):
                        n = NU + j
                        kind = "up" if j < 56 else "down"
                        eng.wait_ge(S["hi_ready"], it * (4 * PER_E) + (n + 1))
                        eng.tensor_tensor(unit(w_lo, kind, n), quarter(ring[(BASE + j // 4) % RING], kind, j % 4),
                                          unit(w_hi, kind, n), ALU.subtract).then_inc(S["lo_ready"], 1)
                        if j % 8 == 3 and 11 <= j <= 59:
                            p = (j - 11) // 8
                            eng.wait_ge(S["unit_used"], it * (4 * PER_E) + (NU + 8 * p + 8))
                            eng.wait_ge(S["e_silu"], it * 7 + (p + 1))
                            if p >= 1:
                                eng.wait_ge(S["turned"], it * 7 + p)
                            eng.tensor_tensor(act_e[:], silu_e[:], pb[2 * (p % 2) + 1], ALU.mult).then_inc(S["gate_up_kept"], 1)
                        if j % 8 == 7 and 15 <= j <= 63:
                            p = (j - 15) // 8
                            eng.wait_ge(S["at_hi_ready"], it * 7 + (p + 1))
                            eng.tensor_tensor(at_lo[:, 4 * p:4 * p + 4, :],
                                              pb[4 if p % 2 == 0 else 7].rearrange("p (k c) -> p k c", k=4),
                                              at_hi[:, 4 * p:4 * p + 4, :], ALU.subtract).then_inc(S["at_lo_ready"], 1)
                        if j == 82:
                            keep_gathered(it * 2 + 2)
                        if ADD_AT <= j < ADD_AT + KC:
                            add_chunk(j - ADD_AT, it)
                for k in range(KC):
                    add_chunk(k, NE)
                eng.wait_ge(S["added"], (NE + 1) * 8 + 1)
            eng.nop().then_inc(S["experts_done"], 1)
            norm(FINAL)


_OUTS = [(1, TP, D), (NB, 1, D), (1, TP, SH, SD), (1, TP, SH, SD), (1, 1, GH, DK, DV), (NB, 1, SH, SD), (NB, 1, SH, SD),
         (1, NB, GH, DK, DV)]


def kernel(**inputs):
    import numpy as _np
    import concourse.bacc as _bacc
    from concourse import mybir as _mybir
    from concourse.bass_utils import run_bass_kernel_spmd as _run

    nc = _bacc.Bacc("TRN2", target_bir_lowering=False, num_devices=1)
    arrays, ins = {}, {}
    for name in inputs:
        a = _np.ascontiguousarray(inputs[name])
        arrays[f"in_{name}"] = a
        ins[name] = nc.dram_tensor(f"in_{name}", a.shape, _mybir.dt.from_np(a.dtype), kind="ExternalInput").ap()
    outs = [nc.dram_tensor(f"out_{i}", s, F32, kind="ExternalOutput").ap() for i, s in enumerate(_OUTS)]
    build(nc, ins, outs)
    r = _run(nc, [arrays], core_ids=[0])
    return tuple(r.results[0][f"out_{i}"] for i in range(len(_OUTS)))
```
